# Optimizing a Trainium2 kernel written in Bass

```python
import math
import jax, jax.numpy as jnp
from jax import lax
import numpy as np

D_MODEL = 1024
BATCH = 1
SEQ = 1024
DEPTH = 1

HEAD_DIM = 64
N_DIFF_HEADS = 4
DIFF_V_DIM = 2 * HEAD_DIM
DIFF_QK_COLS = N_DIFF_HEADS * HEAD_DIM
DIFF_WIDTH = N_DIFF_HEADS * DIFF_V_DIM
N_SB_HEADS = 8
SB_WIDTH = N_SB_HEADS * HEAD_DIM
QBLOCK = 128
N_BUCKETS = 32
MAX_DISTANCE = 128
N_GROUPS = 4
EXPERTS_PER_GROUP = 8
N_EXPERTS = N_GROUPS * EXPERTS_PER_GROUP
TOP_K = 2
D_FF_EXPERT = 512
MOE_BLOCK = 128
EPS = 1e-6
NEG_INF = -1e30

COL_SIZES = (DIFF_QK_COLS, DIFF_QK_COLS, DIFF_QK_COLS, DIFF_QK_COLS, DIFF_WIDTH,
             SB_WIDTH, SB_WIDTH, SB_WIDTH, D_MODEL, D_MODEL)
IN_COLS = sum(COL_SIZES)

kernel_name = "hybrid_diffattn_stickbreak_hiermoe"

def _split_points():
    pts, acc = [], 0
    for c in COL_SIZES[:-1]:
        acc += c
        pts.append(acc)
    return pts

def rmsnorm(x, g):
    x32 = x.astype(jnp.float32)
    y = x32 * lax.rsqrt(jnp.mean(x32 * x32, axis=-1, keepdims=True) + EPS)
    return (y * g.astype(jnp.float32)).astype(x.dtype)

def t5_bucket(n):
    max_exact = N_BUCKETS // 2
    nf = jnp.maximum(n, max_exact).astype(jnp.float32)
    large = max_exact + (jnp.log(nf / max_exact) / math.log(MAX_DISTANCE / max_exact)
                         * (N_BUCKETS - max_exact)).astype(jnp.int32)
    large = jnp.minimum(large, N_BUCKETS - 1)
    return jnp.where(n < max_exact, n, large)

def diff_attention(q1, q2, k1, k2, v, rel_bias, lam):
    b, h, s, _ = q1.shape
    nblk = s // QBLOCK
    kpos = jnp.arange(s)
    scale = HEAD_DIM ** -0.5

    def block(i):
        start = i * QBLOCK
        qpos = start + jnp.arange(QBLOCK)
        dist = qpos[:, None] - kpos[None, :]
        mask = dist >= 0
        bias = jnp.transpose(rel_bias[t5_bucket(jnp.maximum(dist, 0))], (2, 0, 1)).astype(jnp.float32)

        def probs(q, k):
            qb = lax.dynamic_slice_in_dim(q, start, QBLOCK, axis=2)
            sc = jnp.einsum('bhqd,bhkd->bhqk', qb, k).astype(jnp.float32) * scale + bias
            return jax.nn.softmax(jnp.where(mask, sc, NEG_INF), axis=-1)

        w = probs(q1, k1) - lam * probs(q2, k2)
        return jnp.einsum('bhqk,bhkv->bhqv', w.astype(v.dtype), v)

    o = lax.map(block, jnp.arange(nblk))
    return jnp.transpose(o, (1, 2, 0, 3, 4)).reshape(b, h, s, v.shape[-1])

def stick_breaking_attention(q, k, v):
    b, h, s, d = q.shape
    nblk = s // QBLOCK
    kpos = jnp.arange(s)
    scale = HEAD_DIM ** -0.5

    def block(i):
        start = i * QBLOCK
        qpos = start + jnp.arange(QBLOCK)
        mask = kpos[None, :] < qpos[:, None]
        qb = lax.dynamic_slice_in_dim(q, start, QBLOCK, axis=2)
        z = jnp.einsum('bhqd,bhkd->bhqk', qb, k).astype(jnp.float32) * scale
        log_1m = jnp.where(mask, jax.nn.log_sigmoid(-z), 0.0)
        suffix = lax.cumsum(log_1m, axis=3, reverse=True) - log_1m
        a = jnp.where(mask, jnp.exp(jax.nn.log_sigmoid(z) + suffix), 0.0)
        return jnp.einsum('bhqk,bhkd->bhqd', a.astype(v.dtype), v)

    o = lax.map(block, jnp.arange(nblk))
    return jnp.transpose(o, (1, 2, 0, 3, 4)).reshape(b, h, s, d)

def hier_moe(h, w_group, w_router, w_gate, w_up, w_down):
    b, s, d = h.shape
    t = b * s
    xt = h.reshape(t, d)
    gl = (xt @ w_group).astype(jnp.float32)
    gp = jax.nn.softmax(gl, axis=-1)
    g = jnp.argmax(gl, axis=-1).astype(jnp.int32)
    pg = jnp.take_along_axis(gp, g[:, None], axis=-1)
    el = (xt @ w_router).astype(jnp.float32).reshape(t, N_GROUPS, EXPERTS_PER_GROUP)
    el = jnp.take_along_axis(el, g[:, None, None], axis=1)[:, 0]
    topv, topi = lax.top_k(jax.nn.softmax(el, axis=-1), TOP_K)
    gate = pg * topv / jnp.sum(topv, axis=-1, keepdims=True)
    eid = g[:, None] * EXPERTS_PER_GROUP + topi.astype(jnp.int32)

    flat_e = eid.reshape(-1)
    flat_tok = jnp.broadcast_to(jnp.arange(t, dtype=jnp.int32)[:, None], (t, TOP_K)).reshape(-1)
    flat_w = gate.reshape(-1)
    n = t * TOP_K
    p = ((n + MOE_BLOCK - 1) // MOE_BLOCK) * MOE_BLOCK + N_EXPERTS * MOE_BLOCK
    nblk = p // MOE_BLOCK

    order = jnp.argsort(flat_e, stable=True)
    se = flat_e[order]
    counts = jnp.bincount(flat_e, length=N_EXPERTS).astype(jnp.int32)
    starts = jnp.cumsum(counts) - counts
    padded = ((counts + MOE_BLOCK - 1) // MOE_BLOCK) * MOE_BLOCK
    pend = jnp.cumsum(padded)
    pstarts = pend - padded
    dest = pstarts[se] + (jnp.arange(n, dtype=jnp.int32) - starts[se])
    row_tok = jnp.full((p,), t, jnp.int32).at[dest].set(flat_tok[order])
    row_w = jnp.zeros((p,), jnp.float32).at[dest].set(flat_w[order])
    blk_e = jnp.clip(jnp.searchsorted(pend, jnp.arange(nblk, dtype=jnp.int32) * MOE_BLOCK,
                                      side='right'), 0, N_EXPERTS - 1)

    xpad = jnp.concatenate([xt, jnp.zeros((1, d), xt.dtype)], axis=0)

    def expert_block(args):
        rows, w, e = args
        xb = xpad[rows]
        a = jax.nn.silu(xb @ w_gate[e]) * (xb @ w_up[e])
        return (a @ w_down[e]) * w[:, None].astype(xb.dtype)

    yb = lax.map(expert_block, (row_tok.reshape(nblk, MOE_BLOCK),
                                row_w.reshape(nblk, MOE_BLOCK), blk_e))
    out = jnp.zeros((t + 1, d), h.dtype).at[row_tok].add(yb.reshape(p, d).astype(h.dtype))[:t]
    return out.reshape(b, s, d)

def setup_inputs(seed: int = 0) -> dict:
    key = jax.random.key(seed)
    ks = jax.random.split(key, 20)
    f32 = jnp.float32
    nrm = lambda k, shape, scale: jax.random.normal(k, shape, f32) * scale
    gain = lambda k, shape: 1.0 + 0.02 * jax.random.normal(k, shape, f32)
    return {
        "x": jax.random.normal(ks[0], (BATCH, SEQ, D_MODEL), f32),
        "rel_bias": nrm(ks[1], (N_BUCKETS, N_DIFF_HEADS), 0.5),
        "ln1_g": gain(ks[2], (DEPTH, D_MODEL)),
        "w_in": nrm(ks[3], (DEPTH, D_MODEL, IN_COLS), D_MODEL ** -0.5),
        "qnorm_g": gain(ks[4], (DEPTH, HEAD_DIM)),
        "knorm_g": gain(ks[5], (DEPTH, HEAD_DIM)),
        "lambda_q1": nrm(ks[6], (DEPTH, HEAD_DIM), 0.1),
        "lambda_k1": nrm(ks[7], (DEPTH, HEAD_DIM), 0.1),
        "lambda_q2": nrm(ks[8], (DEPTH, HEAD_DIM), 0.1),
        "lambda_k2": nrm(ks[9], (DEPTH, HEAD_DIM), 0.1),
        "subln_g": gain(ks[10], (DEPTH, DIFF_V_DIM)),
        "w_branch_diff": nrm(ks[11], (DEPTH, DIFF_WIDTH, D_MODEL), DIFF_WIDTH ** -0.5),
        "w_branch_sb": nrm(ks[12], (DEPTH, SB_WIDTH, D_MODEL), SB_WIDTH ** -0.5),
        "w_out": nrm(ks[13], (DEPTH, D_MODEL, D_MODEL), D_MODEL ** -0.5),
        "ln2_g": gain(ks[14], (DEPTH, D_MODEL)),
        "w_group": nrm(ks[15], (DEPTH, D_MODEL, N_GROUPS), D_MODEL ** -0.5),
        "w_router": nrm(ks[16], (DEPTH, D_MODEL, N_EXPERTS), D_MODEL ** -0.5),
        "w_gate": nrm(ks[17], (DEPTH, N_EXPERTS, D_MODEL, D_FF_EXPERT), D_MODEL ** -0.5),
        "w_up": nrm(ks[18], (DEPTH, N_EXPERTS, D_MODEL, D_FF_EXPERT), D_MODEL ** -0.5),
        "w_down": nrm(ks[19], (DEPTH, N_EXPERTS, D_FF_EXPERT, D_MODEL), D_FF_EXPERT ** -0.5),
    }

def reference(x, rel_bias, ln1_g, w_in, qnorm_g, knorm_g, lambda_q1, lambda_k1, lambda_q2,
              lambda_k2, subln_g, w_branch_diff, w_branch_sb, w_out, ln2_g, w_group, w_router,
              w_gate, w_up, w_down):
    b, s, _ = x.shape
    split_pts = _split_points()

    def heads(t, nh):
        return t.reshape(b, s, nh, -1).transpose(0, 2, 1, 3)

    def merge_heads(t):
        return t.transpose(0, 2, 1, 3).reshape(b, s, -1)

    for l in range(DEPTH):
        h = rmsnorm(x, ln1_g[l])
        proj = h @ w_in[l]
        q1, q2, k1, k2, va, qs, kss, vs, ga, gb = jnp.split(proj, split_pts, axis=-1)

        q1 = rmsnorm(heads(q1, N_DIFF_HEADS), qnorm_g[l])
        q2 = rmsnorm(heads(q2, N_DIFF_HEADS), qnorm_g[l])
        k1 = rmsnorm(heads(k1, N_DIFF_HEADS), knorm_g[l])
        k2 = rmsnorm(heads(k2, N_DIFF_HEADS), knorm_g[l])
        lam_init = 0.8 - 0.6 * math.exp(-0.3 * l)
        lam = (jnp.exp(jnp.sum(lambda_q1[l].astype(jnp.float32) * lambda_k1[l].astype(jnp.float32)))
               - jnp.exp(jnp.sum(lambda_q2[l].astype(jnp.float32) * lambda_k2[l].astype(jnp.float32)))
               + lam_init)
        oa = diff_attention(q1, q2, k1, k2, heads(va, N_DIFF_HEADS), rel_bias, lam)
        oa = merge_heads(rmsnorm(oa, subln_g[l]) * (1.0 - lam_init))

        ob = merge_heads(stick_breaking_attention(heads(qs, N_SB_HEADS), heads(kss, N_SB_HEADS),
                                                  heads(vs, N_SB_HEADS)))

        mixed = (jax.nn.sigmoid(ga) * (oa @ w_branch_diff[l])
                 + jax.nn.sigmoid(gb) * (ob @ w_branch_sb[l]))
        x = x + mixed @ w_out[l]

        x = x + hier_moe(rmsnorm(x, ln2_g[l]), w_group[l], w_router[l], w_gate[l], w_up[l], w_down[l])
    return x


_drawn_inputs = setup_inputs


def setup_inputs(seed=0):
    import zlib

    import numpy as np

    out = dict(_drawn_inputs(seed))
    spreads = {}
    factors = {'qnorm_g': 2.84, 'knorm_g': 2.831, 'lambda_k2': 5.021, 'subln_g': 3.046, 'ln2_g': 2.928}
    for name, (base, spread) in spreads.items():
        noise = np.random.default_rng([zlib.crc32(name.encode()), seed]).standard_normal(out[name].shape)
        drawn = base * np.exp(spread * noise) if base else spread * noise
        out[name] = __import__('jax').numpy.asarray(drawn.astype(out[name].dtype))
    for name, factor in factors.items():
        out[name] = (out[name] * factor).astype(out[name].dtype)
    return out
```

```python
import math
from contextlib import ExitStack

import numpy as np
import concourse.bass as bass
from concourse import mybir

F32 = mybir.dt.float32
F32R = mybir.dt.float32r
BF16 = mybir.dt.bfloat16
I32 = mybir.dt.int32
U32 = mybir.dt.uint32
ALU = mybir.AluOpType
ACT = mybir.ActivationFunctionType
X = mybir.AxisListType.X

P = 128
S = 1024
D = 1024
NT = S // P
KD = D // P
HD = 64
DH = 4
SH = 8
CH = 512
NCH = 5120 // CH
TOKEN_CHUNKS = 6
NB, NG, EPG = 32, 4, 8
NE = NG * EPG
FF = 512
KF = FF // P
EPS = 1e-6
MASKED = -1e30
LAM_INIT = 0.8 - 0.6 * math.exp(-0.3 * 0)
DIST0 = P - 1
DROW = 3 * P


def bucket_onehot():
    out = np.zeros((NB, DROW), np.float32)
    for col in range(DIST0, DROW):
        n = col - DIST0
        b = n if n < NB // 2 else min(NB - 1, NB // 2 + int(math.log(n / (NB // 2)) / math.log(128 / (NB // 2)) * (NB // 2)))
        out[b, col] = 1.0
    return out


def ge(eng, sem, value):
    if value > 0:
        eng.wait_ge(sem, value)


def product(pe, out, lhs, rhs, first, last):
    pe.matmul(out, lhs[0], rhs[1], start=first, stop=False)
    pe.matmul(out, lhs[1], rhs[0], start=False, stop=False)
    return pe.matmul(out, lhs[0], rhs[0], start=False, stop=last)


def allocators(nc, ctx, stage):
    sb = lambda name, shape, dt=F32: ctx.enter_context(nc.sbuf_tensor(f"{stage}_{name}", shape, dt))
    ps = lambda name, shape, dt=F32: ctx.enter_context(nc.psum_tensor(f"{stage}_{name}", shape, dt))
    sem = lambda name: ctx.enter_context(nc.semaphore(f"{stage}_{name}"))
    return sb, ps, sem


def row_broadcast(ap, n):
    return bass.AP(tensor=ap.tensor, offset=ap.offset, ap=[[0, P], [1, n]])


def embed(nc, a, c):
    with ExitStack() as ctx:
        sb, ps, sem = allocators(nc, ctx, "embed")
        xt = sb("xt", [P, 2, D])
        junk = sb("junk", [P, D])
        xn = sb("xn", [P, 2, D])
        g1 = sb("g1", [P, D])
        ss = sb("ss", [P, NT])
        var = sb("var", [P, NT])
        rs = sb("rs", [P, NT])
        half = sb("half", [P, 1])
        rel = sb("rel", [NB, DH])
        onehot = sb("onehot", [NB, DROW])
        drow = sb("drow", [DH, DROW])
        drow2 = sb("drow2", [DH, DROW])
        lam4 = sb("lam4", [P, 4, HD])
        lamp = sb("lamp", [P, 2, HD])
        lams = sb("lams", [P, 2])
        lame = sb("lame", [P, 2])
        lamd = sb("lamd", [P, 1])
        tp = [ps(f"tp{i}", [P, KD, P]) for i in range(2)]
        pd = ps("pd", [P, CH])
        x_loaded = [sem(f"x_loaded{i}") for i in range(2)]
        g_loaded, small_loaded, made, squared = sem("g_loaded"), sem("small_loaded"), sem("made"), sem("squared")
        var_ready, rs_ready, xn_ready = sem("var_ready"), sem("rs_ready"), sem("xn_ready")
        xT_ready, hi_ready, lo_ready = sem("xT_ready"), sem("hi_ready"), sem("lo_ready")
        dist_ready, drow_ready, lam_step, lam_exp, stored = (sem("dist_ready"), sem("drow_ready"), sem("lam_step"),
                                                             sem("lam_exp"), sem("stored"))
        cast_ready = sem("cast_ready")
        with nc.Block() as block:
            @block.sync
            def _(sp):
                sp.dma_start(g1[:], row_broadcast(a.ln1_g[0], D)).then_inc(g_loaded, 16)
                for t in range(NT):
                    if t == 2:
                        sp.dma_start(rel[:], a.rel_bias).then_inc(small_loaded, 16)
                        sp.dma_start(onehot[:], a.onehot).then_inc(small_loaded, 16)
                        for n, v in enumerate((a.lambda_q1, a.lambda_q2, a.lambda_k1, a.lambda_k2)):
                            sp.dma_start(lam4[:, n, :], row_broadcast(v[0], HD)).then_inc(small_loaded, 16)
                    ge(sp, xn_ready, t - 1)
                    sp.dma_start(xt[:, t % 2, :], a.x[0, t * P:(t + 1) * P, :]).then_inc(x_loaded[t % 2], 16)
                sp.wait_ge(drow_ready, 3)
                sp.dma_start(c.drow_dram.ap(), drow2[:]).then_inc(stored, 16)
                sp.wait_ge(stored, 16)

            @block.gpsimd
            def _(pool):
                pool.memset(half[:], -0.5).then_inc(made, 1)
                pool.memset(c.ident[:], 0.0).then_inc(made, 1)
                pool.memset(c.maskb[:], 0.0).then_inc(made, 1)
                pool.wait_ge(made, 3)
                pool.affine_select(out=c.ident[:], in_=c.ident[:], compare_op=ALU.not_equal, fill=1.0, base=0,
                                   pattern=[[-1, P]], channel_multiplier=1).then_inc(made, 1)
                pool.affine_select(out=c.maskb[:], in_=c.maskb[:], compare_op=ALU.is_gt, fill=MASKED, base=0,
                                   pattern=[[-1, P]], channel_multiplier=1).then_inc(made, 1)
                for t in range(NT):
                    pool.wait_ge(squared, t + 1)
                    pool.tensor_scalar(var[:, t:t + 1], ss[:, t:t + 1], 1.0 / D, EPS, ALU.mult, ALU.add).then_inc(var_ready, 1)
                    pool.wait_ge(var_ready, t + 1)
                    pool.tensor_tensor(rs[:, t:t + 1], var[:, t:t + 1], half[:], ALU.pow).then_inc(rs_ready, 1)

            @block.scalar
            def _(act):
                def hi(t):
                    act.wait_ge(xT_ready, t + 1)
                    act.copy(c.h_hi[:, :, t * P:(t + 1) * P], tp[t % 2][:]).then_inc(hi_ready, 1)
                for t in range(NT):
                    act.wait_ge(x_loaded[t % 2], 16 * (t // 2 + 1))
                    if t:
                        act.wait_ge(squared, t)
                    act.activation(junk[:], xt[:, t % 2, :], ACT.Square, accum_out=ss[:, t:t + 1]).then_inc(squared, 1)
                    if t:
                        hi(t - 1)
                hi(NT - 1)
                act.wait_ge(lam_step, 2)
                act.activation(lame[:], lams[:], ACT.Exp).then_inc(lam_exp, 1)

            @block.vector
            def _(dve):
                def lo(t):
                    dve.wait_ge(hi_ready, t + 1)
                    dve.tensor_sub(c.h_lo[:, :, t * P:(t + 1) * P], tp[t % 2][:],
                                   c.h_hi[:, :, t * P:(t + 1) * P].bitcast(F32)).then_inc(lo_ready, 1)
                dve.wait_ge(made, 5)
                dve.tensor_copy(c.identr[:], c.ident[:]).then_inc(cast_ready, 1)
                dve.tensor_copy(c.identb[:], c.ident[:]).then_inc(cast_ready, 1)
                dve.wait_ge(g_loaded, 16)
                for t in range(NT):
                    dve.wait_ge(rs_ready, t + 1)
                    ge(dve, xT_ready, t - 1)
                    dve.scalar_tensor_tensor(out=xn[:, t % 2, :], in0=xt[:, t % 2, :], scalar=rs[:, t:t + 1],
                                             in1=g1[:], op0=ALU.mult, op1=ALU.mult).then_inc(xn_ready, 1)
                    if t:
                        lo(t - 1)
                lo(NT - 1)
                dve.wait_ge(dist_ready, 1)
                dve.tensor_copy(drow[:], pd[0:DH, 0:DROW]).then_inc(drow_ready, 1)
                dve.wait_ge(drow_ready, 1)
                dve.tensor_scalar(drow2[:], drow[:], drow[:, DROW - 1:DROW], None, ALU.subtract).then_inc(drow_ready, 1)
                dve.wait_ge(drow_ready, 2)
                dve.memset(drow2[:, 0:DIST0], MASKED).then_inc(drow_ready, 1)
                dve.tensor_tensor(lamp[:], lam4[:, 0:2, :], lam4[:, 2:4, :], ALU.mult).then_inc(lam_step, 1)
                dve.wait_ge(lam_step, 1)
                dve.reduce_sum(lams[:], lamp[:], axis=X).then_inc(lam_step, 1)
                dve.wait_ge(lam_exp, 1)
                dve.tensor_sub(lamd[:], lame[:, 1:2], lame[:, 0:1]).then_inc(lam_step, 1)
                dve.wait_ge(lam_step, 3)
                dve.tensor_scalar(c.neg_lam[:], lamd[:], -LAM_INIT, None, ALU.add).then_inc(lam_step, 1)

            @block.tensor
            def _(pe):
                pe.wait_ge(made, 4)
                for t in range(NT):
                    pe.wait_ge(xn_ready, t + 1)
                    ge(pe, lo_ready, t - 1)
                    for k in range(KD):
                        last = pe.transpose(tp[t % 2][:, k, :], xn[:, t % 2, k * P:(k + 1) * P], c.ident[:])
                    last.then_inc(xT_ready, 1)
                pe.wait_ge(small_loaded, 96)
                pe.matmul(pd[0:DH, 0:DROW], rel[:], onehot[:], start=True, stop=True).then_inc(dist_ready, 1)


def project(nc, a, c):
    with ExitStack() as ctx:
        sb, ps, sem = allocators(nc, ctx, "project")
        RAW = 4
        wraw = sb("wraw", [P, RAW, CH])
        whi = sb("whi", [P, 3, KD, CH], F32R)
        wlo = sb("wlo", [P, 3, KD, CH], F32R)
        sq = sb("sq", [P, 2, CH])
        qn = sb("qn", [P, 2, CH])
        qd = sb("qd", [P, 2, SH, 2, HD])
        sthi = sb("sthi", [P, 2, SH, P], F32R)
        stlo = sb("stlo", [P, 1, SH, P], F32R)
        stage = sb("stage", [P, 2, CH])
        gq = sb("gq", [P, 4, HD])
        ss = sb("ssq", [P, 2, SH])
        var = sb("varq", [P, 2, SH])
        rs = sb("rsq", [P, 2, SH])
        half = sb("halfq", [P, SH])
        acc = [ps(f"acc{i}", [P, CH]) for i in range(4)]
        tp = [ps(f"tq{i}", [P, SH, P]) for i in range(2)]
        raw_loaded = [sem(f"raw_loaded{i}") for i in range(RAW)]
        g_loaded, g_ready, half_ready = sem("gq_loaded"), sem("gq_ready"), sem("half_ready")
        w_hi, w_lo = sem("w_hi"), sem("w_lo")
        acc_full, acc_free = sem("acc_full"), sem("acc_free")
        squared, ss_ready, var_ready, rs_ready = sem("q_squared"), sem("ss_ready"), sem("q_var"), sem("q_rs")
        qd_ready, tp_full, st_hi, st_lo = sem("qd_ready"), sem("tp_full"), sem("st_hi"), sem("st_lo")
        hi_stored = [sem(f"hi_stored{i}") for i in range(2)]
        lo_stored = sem("lo_stored")
        stage_stored = [sem(f"stage_stored{i}") for i in range(2)]
        gate_ready = sem("gate_ready")

        units = []
        for n in range(NCH):
            for t in range(8):
                units.append((n, t))
        def kind(n):
            return "gate" if n >= TOKEN_CHUNKS else "qkv"[n % 3]
        def turn(n, t):
            return (n // 3) * 16 + (n % 3) * 8 + t
        def value(n, t):
            return (n // 3) * 8 + t
        def gate(n, t):
            return (n - TOKEN_CHUNKS) * 8 + t
        def before(n, t):
            n, t = (n, t - 1) if t else (n - 1, 7)
            return (n, t) if n >= 0 and kind(n) in "qk" else None
        def lo_stores(n, t):
            return (n // 3) * 8 + (t if kind(n) == "k" else 0)
        def slot(n):
            return n % 3 if n < TOKEN_CHUNKS else n % 2

        with nc.Block() as block:
            @block.sync
            def _(sp):
                for n in range(4):
                    if n < 2:
                        sp.dma_start(gq[:, n, :], row_broadcast((a.qnorm_g, a.knorm_g)[n][0], HD)).then_inc(g_loaded, 16)
                for r in range(NCH * KD):
                    n, k = divmod(r, KD)
                    ge(sp, w_lo, r - RAW + 1)
                    sp.dma_start(wraw[:, r % RAW, :], a.w_in[0, k * P:(k + 1) * P, n * CH:(n + 1) * CH])\
                        .then_inc(raw_loaded[r % RAW], 16)

            @block.gpsimd
            def _(pool):
                pool.memset(half[:], -0.5).then_inc(half_ready, 1)
                pool.wait_ge(half_ready, 1)
                stored = [0, 0]
                def store(n, t):
                    m = turn(n, t)
                    j = n // 3
                    pool.wait_ge(st_lo, m + 1)
                    dst = c.stack_q if kind(n) == "q" else c.stack_kh
                    pool.dma_start(dst.ap()[j * 8:j * 8 + 8, :, t * P:(t + 1) * P].rearrange("m p t -> p m t"),
                                   sthi[:, m % 2].bitcast(F32)).then_inc(hi_stored[m % 2], 16)
                    if kind(n) == "k":
                        pool.dma_start(c.stack_kl.ap()[j * 8:j * 8 + 8, :, t * P:(t + 1) * P].rearrange("m p t -> p m t"),
                                       stlo[:, 0].bitcast(F32)).then_inc(lo_stored, 16)
                for n, t in units:
                    if kind(n) in "qk":
                        m = turn(n, t)
                        pool.wait_ge(ss_ready, m + 1)
                        if n < 3:
                            pool.tensor_scalar(var[:, m % 2, :], ss[:, m % 2, :], 1.0 / HD, EPS, ALU.mult, ALU.add)\
                                .then_inc(var_ready, 1)
                            pool.wait_ge(var_ready, m + 1)
                            pool.tensor_tensor(rs[:, m % 2, :], var[:, m % 2, :], half[:], ALU.pow).then_inc(rs_ready, 1)
                    prev = before(n, t)
                    if prev:
                        store(*prev)
                    if kind(n) == "v":
                        j = n // 3
                        pool.wait_ge(acc_free, 8 * n + t + 1)
                        pool.dma_start(c.values.ap()[t * P:(t + 1) * P, j, :], stage[:, t % 2, :])\
                            .then_inc(stage_stored[t % 2], 16)
                    if kind(n) == "gate":
                        i = gate(n, t)
                        pool.wait_ge(gate_ready, i + 1)
                        row = (n - TOKEN_CHUNKS) * 4 + t // 2
                        pool.dma_start(c.gates.ap()[row * P:(row + 1) * P, (t % 2) * CH:(t % 2 + 1) * CH],
                                       stage[:, t % 2, :]).then_inc(stage_stored[t % 2], 16)
                pool.wait_ge(hi_stored[0], 16 * 16)
                pool.wait_ge(hi_stored[1], 16 * 16)
                pool.wait_ge(lo_stored, 16 * 16)
                pool.wait_ge(stage_stored[0], 16 * 24)
                pool.wait_ge(stage_stored[1], 16 * 24)

            @block.scalar
            def _(act):
                def split(r):
                    n, k = divmod(r, KD)
                    if n < NCH:
                        act.wait_ge(raw_loaded[r % RAW], 16 * (r // RAW + 1))
                        act.copy(whi[:, slot(n), k, :], wraw[:, r % RAW, :]).then_inc(w_hi, 1)
                def hi(n, t):
                    m = turn(n, t)
                    act.wait_ge(tp_full, m + 1)
                    ge(act, hi_stored[m % 2], 16 * (m // 2))
                    act.copy(sthi[:, m % 2], tp[m % 2][:]).then_inc(st_hi, 1)
                for r in range(KD):
                    split(r)
                for n, t in units:
                    u = 8 * n + t
                    if kind(n) in "qk":
                        act.wait_ge(acc_full, u + 1)
                        act.activation(sq[:, t % 2, :], acc[t % 2][:], ACT.Square).then_inc(squared, 1)
                    if kind(n) == "gate":
                        i = gate(n, t)
                        act.wait_ge(acc_full, u + 1)
                        ge(act, stage_stored[t % 2], 16 * (8 + i // 2))
                        act.activation(stage[:, t % 2, :], acc[2 + t % 2][:], ACT.Sigmoid).then_inc(gate_ready, 1)
                    split(u + KD)
                    if before(n, t):
                        hi(*before(n, t))

            @block.vector
            def _(dve):
                dve.wait_ge(g_loaded, 32)
                dve.tensor_scalar(gq[:, 0, :], gq[:, 0, :], HD ** -0.5, None, ALU.mult).then_inc(g_ready, 1)
                dve.memset(gq[:, 2, :], HD ** -0.5).then_inc(g_ready, 1)
                dve.memset(gq[:, 3, :], 1.0).then_inc(g_ready, 1)
                dve.wait_ge(g_ready, 3)
                def split(r):
                    n, k = divmod(r, KD)
                    if n < NCH:
                        dve.wait_ge(w_hi, r + 1)
                        dve.tensor_sub(wlo[:, slot(n), k, :], wraw[:, r % RAW, :],
                                       whi[:, slot(n), k, :].bitcast(F32)).then_inc(w_lo, 1)
                def lo(n, t):
                    m = turn(n, t)
                    dve.wait_ge(st_hi, m + 1)
                    if kind(n) == "q":
                        dve.tensor_sub(sthi[HD:P, m % 2], tp[m % 2][HD:P],
                                       sthi[HD:P, m % 2].bitcast(F32)).then_inc(st_lo, 1)
                    else:
                        ge(dve, lo_stored, 16 * lo_stores(n, t))
                        dve.tensor_sub(stlo[:, 0], tp[m % 2][:], sthi[:, m % 2].bitcast(F32)).then_inc(st_lo, 1)
                for r in range(KD):
                    split(r)
                for n, t in units:
                    u = 8 * n + t
                    if kind(n) in "qk":
                        m = turn(n, t)
                        s = m % 2
                        dve.wait_ge(squared, m + 1)
                        dve.reduce_sum(ss[:, s, :], sq[:, s, :].rearrange("p (h d) -> p h d", d=HD), axis=X)\
                            .then_inc(ss_ready, 1)
                    split(u + KD)
                    if kind(n) in "qk":
                        a3 = acc[s][:].rearrange("p (h d) -> p h d", d=HD)
                        q3 = qn[:, s, :].rearrange("p (h d) -> p h d", d=HD)
                        if n < 3:
                            dve.wait_ge(rs_ready, m + 1)
                            dve.tensor_tensor(q3, a3, rs[:, s, :].unsqueeze(2).to_broadcast([P, SH, HD]), ALU.mult)\
                                .then_inc(acc_free, 1)
                        else:
                            dve.tensor_copy(q3, a3).then_inc(acc_free, 1)
                        dve.wait_ge(acc_free, u + 1)
                        g = gq[:, 2 * (n // 3) + n % 3, :]
                        for d in range(2):
                            ins = dve.tensor_tensor(qd[:, s, :, d, :], q3, g.unsqueeze(1).to_broadcast([P, SH, HD]),
                                                    ALU.mult)
                        ins.then_inc(qd_ready, 1)
                    if kind(n) == "v":
                        i = value(n, t)
                        dve.wait_ge(acc_full, u + 1)
                        ge(dve, stage_stored[t % 2], 16 * (i // 2))
                        dve.tensor_copy(stage[:, t % 2, :], acc[t % 2][:]).then_inc(acc_free, 1)
                    if before(n, t):
                        lo(*before(n, t))

            @block.tensor
            def _(pe):
                def transposes(n, t):
                    m = turn(n, t)
                    pe.wait_ge(qd_ready, m + 1)
                    ge(pe, st_lo, m - 1)
                    for h in range(SH):
                        last = pe.transpose(tp[m % 2][:, h, :], qd[:, m % 2, h].rearrange("p a d -> p (a d)"), c.ident[:])
                    last.then_inc(tp_full, 1)
                for n, t in units:
                    u = 8 * n + t
                    w = [(whi[:, slot(n), k, :], wlo[:, slot(n), k, :]) for k in range(KD)]
                    pe.wait_ge(w_lo, KD * (n + 1))
                    if kind(n) == "gate":
                        ge(pe, gate_ready, gate(n, t) - 1)
                        cols, half_t = slice(t // 2 * P, (t // 2 + 1) * P), slice(t % 2 * CH, (t % 2 + 1) * CH)
                        for k in range(KD):
                            last = product(pe, acc[2 + t % 2][:], (w[k][0][:, cols], w[k][1][:, cols]),
                                           (c.h_hi[:, k, half_t], c.h_lo[:, k, half_t]), k == 0, k == KD - 1)
                    else:
                        ge(pe, acc_free, u - 1)
                        rows = slice(t * P, (t + 1) * P)
                        for k in range(KD):
                            last = product(pe, acc[t % 2][:], (c.h_hi[:, k, rows], c.h_lo[:, k, rows]), w[k],
                                           k == 0, k == KD - 1)
                    last.then_inc(acc_full, 1)
                    if before(n, t):
                        transposes(*before(n, t))


def attention_steps(heads):
    return [(h + d, i) for h in range(0, heads, 2) for i in reversed(range(NT)) for d in range(2)]


def diff(nc, a, c):
    with ExitStack() as ctx:
        sb, ps, sem = allocators(nc, ctx, "diff")
        q = sb("q", [P, DH, 2, S], F32R)
        kh = sb("kh", [P, DH, 2, S], F32R)
        kl = sb("kl", [P, DH, 2, S], F32R)
        v = sb("v", [P, NT, DH, P])
        dist = sb("dist", [P, DH, 2 * P])
        dhi = sb("dhi", [P, DH, 2 * P], F32R)
        dlo = sb("dlo", [P, DH, 2 * P], F32R)
        prob = sb("prob", [P, 2, 2, S])
        wT = sb("wT", [P, 2, NT, P])
        junk = sb("junkd", [P, P])
        mx = sb("mx", [P, 2, 2])
        nm = sb("nm", [P, 2, 2])
        sums = sb("sums", [P, 2, 2])
        rec = sb("rec", [P, 2, 2])
        rneg = sb("rneg", [P, 2])
        score = [ps(f"score{m}", [P, S]) for m in range(2)]
        tp = ps("tpd", [P, NT, P])
        out = [ps(f"outd{i}", [P, CH]) for i in range(2)]
        loaded = [sem(f"head_loaded{h}") for h in range(DH)]
        v_loaded, dist_loaded, dist_hi, dist_lo = sem("v_loaded"), sem("dist_loaded"), sem("dist_hi"), sem("dist_lo")
        score_full, max_ready, neg_ready, exp_done = sem("score_full"), sem("max_ready"), sem("neg_ready"), sem("exp_done")
        rec_ready, scaled, combined = sem("rec_ready"), sem("scaled"), sem("combined")
        tp_full, wT_ready, pv_full, ssq_ready, copied = (sem("tpd_full"), sem("wT_ready"), sem("pv_full"), sem("ssq_ready"),
                                                         sem("copied"))
        steps = attention_steps(DH)
        n_steps = len(steps)

        with nc.Block() as block:
            @block.sync
            def _(sp):
                for h in range(DH):
                    for dst, src in ((q, c.stack_q), (kh, c.stack_kh), (kl, c.stack_kl)):
                        sp.dma_start(dst[:, h].bitcast(F32), src.ap()[h:h + 5:4].rearrange("m p t -> p m t"))\
                            .then_inc(loaded[h], 16)
                    if h == 0:
                        sp.dma_start(dist[:], bass.AP(tensor=c.drow_dram, offset=0, ap=[[1, P], [DROW, DH], [1, 2 * P]]))\
                            .then_inc(dist_loaded, 16)
                        sp.dma_start(v[:], c.values.ap()[:, 0, :].rearrange("(n p) (h d) -> p n h d", p=P, d=P))\
                            .then_inc(v_loaded, 16)

            @block.scalar
            def _(act):
                def evacuate(s):
                    act.wait_ge(tp_full, s + 1)
                    ge(act, pv_full, s - 1)
                    nb = steps[s][1] + 1
                    act.copy(wT[:, s % 2, 0:nb, :], tp[:, 0:nb, :]).then_inc(wT_ready, 1)
                def squares(s):
                    h, i = steps[s]
                    act.wait_ge(pv_full, s + 1)
                    if s:
                        act.wait_ge(ssq_ready, s)
                    act.activation(junk[:], out[s % 2][:, 0:P], ACT.Square, accum_out=c.ssq[:, h, i:i + 1])\
                        .then_inc(ssq_ready, 1)
                for s in range(n_steps + 4):
                    if s < n_steps:
                        w = (steps[s][1] + 1) * P
                        ge(act, combined, s - 1)
                        ge(act, tp_full, s - 1)
                        for m in range(2):
                            act.wait_ge(neg_ready, 2 * s + m + 1)
                            act.activation(prob[:, s % 2, m, 0:w], score[m][:, 0:w], ACT.Exp, bias=nm[:, s % 2, m:m + 1],
                                           accum_out=sums[:, s % 2, m:m + 1]).then_inc(exp_done, 1)
                    if 2 <= s < n_steps + 2:
                        evacuate(s - 2)
                    if 4 <= s:
                        squares(s - 4)

            @block.vector
            def _(dve):
                def combine(s):
                    w = (steps[s][1] + 1) * P
                    e = s % 2
                    dve.wait_ge(exp_done, 2 * s + 2)
                    dve.reciprocal(rec[:, e, :], sums[:, e, :]).then_inc(rec_ready, 1)
                    dve.wait_ge(rec_ready, s + 1)
                    dve.tensor_scalar(rneg[:, e:e + 1], rec[:, e, 1:2], c.neg_lam[:], None, ALU.mult).then_inc(scaled, 1)
                    dve.tensor_scalar(prob[:, e, 0, 0:w], prob[:, e, 0, 0:w], rec[:, e, 0:1], None, ALU.mult)\
                        .then_inc(scaled, 1)
                    dve.wait_ge(scaled, 2 * s + 2)
                    dve.scalar_tensor_tensor(out=prob[:, e, 1, 0:w], in0=prob[:, e, 1, 0:w], scalar=rneg[:, e:e + 1],
                                             in1=prob[:, e, 0, 0:w], op0=ALU.mult, op1=ALU.add).then_inc(combined, 1)
                def copy_out(s):
                    h, i = steps[s]
                    dve.wait_ge(ssq_ready, s + 1)
                    dve.tensor_copy(c.mixed_raw[:, i, h * P:(h + 1) * P], out[s % 2][:, 0:P]).then_inc(copied, 1)
                dve.wait_ge(dist_loaded, 16)
                rev = dist[:, :, ::-1]
                dve.tensor_copy(dhi[:], rev).then_inc(dist_hi, 1)
                dve.wait_ge(dist_hi, 1)
                dve.tensor_sub(dlo[:], rev, dhi[:].bitcast(F32)).then_inc(dist_lo, 1)
                for s in range(n_steps + 5):
                    if s < n_steps:
                        w = (steps[s][1] + 1) * P
                        for m in range(2):
                            u = 2 * s + m
                            dve.wait_ge(score_full, u + 1)
                            dve.reduce_max(mx[:, s % 2, m:m + 1], score[m][:, 0:w], axis=X).then_inc(max_ready, 1)
                            dve.wait_ge(max_ready, u + 1)
                            dve.tensor_scalar(nm[:, s % 2, m:m + 1], mx[:, s % 2, m:m + 1], -1.0, None, ALU.mult)\
                                .then_inc(neg_ready, 1)
                    if 1 <= s < n_steps + 1:
                        combine(s - 1)
                    if 5 <= s:
                        copy_out(s - 5)

            @block.tensor
            def _(pe):
                def scores(s):
                    h, i = steps[s]
                    if s < 2 or steps[s][0] != steps[s - 2][0]:
                        pe.wait_ge(loaded[h], 48)
                    w = (i + 1) * P
                    near = max(0, (i - 1) * P)
                    for m in range(2):
                        u = 2 * s + m
                        ge(pe, exp_done, u - 1)
                        qt = q[:, h, m, i * P:(i + 1) * P]
                        for c0 in range(0, w, CH):
                            c1 = min(w, c0 + CH)
                            o = score[m][:, c0:c1]
                            b0 = max(c0, near)
                            pe.matmul(o, qt, kl[:, h, m, c0:c1], start=True, stop=False)
                            last = pe.matmul(o, qt, kh[:, h, m, c0:c1], start=False, stop=b0 >= c1)
                            if b0 < c1:
                                d0 = b0 - (i - 1) * P
                                o = score[m][:, b0:c1]
                                pe.matmul(o, c.identr[:], dlo[:, h, d0:d0 + c1 - b0], start=False, stop=False)
                                last = pe.matmul(o, c.identr[:], dhi[:, h, d0:d0 + c1 - b0], start=False, stop=True)
                        last.then_inc(score_full, 1)
                def transposes(s):
                    pe.wait_ge(combined, s + 1)
                    ge(pe, wT_ready, s)
                    for j in range(steps[s][1] + 1):
                        last = pe.transpose(tp[:, j, :], prob[:, s % 2, 1, j * P:(j + 1) * P], c.ident[:])
                    last.then_inc(tp_full, 1)
                def weigh(s):
                    h, i = steps[s]
                    pe.wait_ge(wT_ready, s + 1)
                    ge(pe, copied, s - 1)
                    for j in range(i + 1):
                        last = pe.matmul(out[s % 2][:, 0:P], wT[:, s % 2, j, :], v[:, j, h, :], start=j == 0, stop=j == i)
                    last.then_inc(pv_full, 1)
                pe.wait_ge(dist_lo, 1)
                pe.wait_ge(v_loaded, 16)
                for s in range(n_steps + 3):
                    if s < n_steps:
                        scores(s)
                    if 2 <= s < n_steps + 2:
                        transposes(s - 2)
                    if 3 <= s:
                        weigh(s - 3)


def stick(nc, a, c):
    with ExitStack() as ctx:
        sb, ps, sem = allocators(nc, ctx, "stick")
        q = sb("qs", [P, SH, S], F32R)
        kh = sb("khs", [P, SH, S], F32R)
        kl = sb("kls", [P, SH, S], F32R)
        v = sb("vs", [P, NT, SH, HD])
        take = sb("take", [P, 2, S])
        rest = sb("rest", [P, 2, S])
        wT = sb("wTs", [P, 2, NT, P])
        z = [ps(f"z{m}", [P, S]) for m in range(2)]
        tp = ps("tps", [P, NT, P])
        out = [ps(f"outs{i}", [P, CH]) for i in range(2)]
        loaded = [sem(f"shead_loaded{h}") for h in range(SH)]
        v_loaded, z_full, took, rested, scanned, weighted = (sem("vs_loaded"), sem("z_full"), sem("took"), sem("rested"),
                                                             sem("scanned"), sem("weighted"))
        tp_full, wT_near, wT_far, pv_full, copied = (sem("tps_full"), sem("wT_near"), sem("wT_far"), sem("pvs_full"),
                                                     sem("copieds"))
        steps = attention_steps(SH)
        n_steps = len(steps)
        HALF = NT // 2
        def far_count(s):
            return sum(i >= HALF for _, i in steps[:s])

        with nc.Block() as block:
            @block.sync
            def _(sp):
                for h in range(SH):
                    for dst, src in ((q, c.stack_q), (kh, c.stack_kh), (kl, c.stack_kl)):
                        sp.dma_start(dst[:, h].bitcast(F32), src.ap()[8 + h]).then_inc(loaded[h], 16)
                    if h == 0:
                        sp.dma_start(v[:], c.values.ap()[:, 1, :].rearrange("(n p) (h d) -> p n h d", p=P, d=HD))\
                            .then_inc(v_loaded, 16)

            @block.scalar
            def _(act):
                def evacuate(s):
                    nb = min(HALF, steps[s][1] + 1)
                    act.wait_ge(tp_full, s + 1)
                    ge(act, pv_full, s - 1)
                    act.copy(wT[:, s % 2, 0:nb, :], tp[:, 0:nb, :]).then_inc(wT_near, 1)
                for s in range(n_steps + 2):
                    if s < n_steps:
                        w = (steps[s][1] + 1) * P
                        act.wait_ge(z_full, s + 1)
                        ge(act, tp_full, s - 1)
                        act.activation(rest[:, s % 2, 0:w], z[s % 2][:, 0:w], ACT.Sigmoid, scale=-1.0).then_inc(rested, 1)
                        act.activation(take[:, s % 2, 0:w], z[s % 2][:, 0:w], ACT.Sigmoid).then_inc(took, 1)
                    if 2 <= s:
                        evacuate(s - 2)

            @block.vector
            def _(dve):
                def evacuate(s):
                    nb = steps[s][1] + 1
                    if nb > HALF:
                        dve.wait_ge(tp_full, s + 1)
                        ge(dve, pv_full, s - 1)
                        dve.tensor_copy(wT[:, s % 2, HALF:nb, :], tp[:, HALF:nb, :]).then_inc(wT_far, 1)
                def copy_out(s):
                    h, i = steps[s]
                    dve.wait_ge(pv_full, s + 1)
                    dve.tensor_copy(c.mixed_raw[:, i, CH + h * HD:CH + (h + 1) * HD], out[s % 2][:, 0:HD]).then_inc(copied, 1)
                for s in range(n_steps + 4):
                    if s < n_steps:
                        w = (steps[s][1] + 1) * P
                        e = s % 2
                        dve.wait_ge(rested, s + 1)
                        back = rest[:, e, 0:w][:, ::-1]
                        dve.tensor_tensor_scan(back, back, back, 1.0, ALU.mult, ALU.bypass).then_inc(scanned, 1)
                        dve.wait_ge(scanned, s + 1)
                        dve.wait_ge(took, s + 1)
                        dve.tensor_tensor(take[:, e, 0:w - 1], take[:, e, 0:w - 1], rest[:, e, 1:w], ALU.mult)\
                            .then_inc(weighted, 1)
                    if 2 <= s < n_steps + 2:
                        evacuate(s - 2)
                    if 4 <= s:
                        copy_out(s - 4)

            @block.tensor
            def _(pe):
                def scores(s):
                    h, i = steps[s]
                    if s < 2 or steps[s][0] != steps[s - 2][0]:
                        pe.wait_ge(loaded[h], 48)
                    w = (i + 1) * P
                    ge(pe, took, s - 1)
                    for c0 in range(0, w, CH):
                        c1 = min(w, c0 + CH)
                        qt, o = q[:, h, i * P:(i + 1) * P], z[s % 2][:, c0:c1]
                        pe.matmul(o, qt, kl[:, h, c0:c1], start=True, stop=False)
                        last = pe.matmul(o, qt, kh[:, h, c0:c1], start=False, stop=c1 < w)
                    last = pe.matmul(z[s % 2][:, i * P:w], c.identb[:], c.maskb[:], start=False, stop=True)
                    last.then_inc(z_full, 1)
                def transposes(s):
                    pe.wait_ge(weighted, s + 1)
                    ge(pe, wT_near, s)
                    ge(pe, wT_far, far_count(s))
                    for j in range(steps[s][1] + 1):
                        last = pe.transpose(tp[:, j, :], take[:, s % 2, j * P:(j + 1) * P], c.ident[:])
                    last.then_inc(tp_full, 1)
                def weigh(s):
                    h, i = steps[s]
                    pe.wait_ge(wT_near, s + 1)
                    ge(pe, wT_far, far_count(s + 1))
                    ge(pe, copied, s - 1)
                    for j in range(i + 1):
                        last = pe.matmul(out[s % 2][:, 0:HD], wT[:, s % 2, j, :], v[:, j, h, :], start=j == 0, stop=j == i)
                    last.then_inc(pv_full, 1)
                pe.wait_ge(v_loaded, 16)
                for s in range(n_steps + 3):
                    if s < n_steps:
                        scores(s)
                    if 2 <= s < n_steps + 2:
                        transposes(s - 2)
                    if 3 <= s:
                        weigh(s - 3)


def branch(nc, a, c):
    with ExitStack() as ctx:
        sb, ps, sem = allocators(nc, ctx, "branch")
        o_hi = sb("o_hi", [P, KD, S], F32R)
        o_lo = sb("o_lo", [P, KD, S], F32R)
        wraw = sb("wbraw", [P, 2, KD, P])
        whi = sb("wbhi", [P, 2, KD, P], F32R)
        wlo = sb("wblo", [P, 2, KD, P], F32R)
        gts = sb("gts", [P, 2, 2, CH])
        m1 = sb("m1", [P, CH])
        m2 = sb("m2", [P, CH])
        mix = sb("mix", [P, CH])
        gsub = sb("gsub", [P, P])
        gsub8 = sb("gsub8", [P, P])
        half = sb("halfb", [P, DH * NT])
        var = sb("varb", [P, DH * NT])
        rs = sb("rsb", [P, DH, NT])
        tp = [ps(f"tpb{i}", [P, KD, P]) for i in range(2)]
        pa = [ps(f"pa{i}", [P, CH]) for i in range(2)]
        pb = [ps(f"pb{i}", [P, CH]) for i in range(2)]
        w_loaded = [sem(f"wb_loaded{i}") for i in range(2)]
        g_loaded = [sem(f"gate_loaded{i}") for i in range(2)]
        gsub_loaded, gsub_ready, half_ready, var_ready, rs_ready = (sem("gsub_loaded"), sem("gsub_ready"), sem("halfb_ready"),
                                                                    sem("varb_ready"), sem("rsb_ready"))
        normed, tp_full, o_hi_ready, o_lo_ready = sem("normed"), sem("tpb_full"), sem("o_hi_ready"), sem("o_lo_ready")
        w_hi, w_lo, acc_full, gated, mixed, mix_hi, mix_lo = (sem("wb_hi"), sem("wb_lo"), sem("accb_full"), sem("gated"),
                                                              sem("mixed"), sem("mix_hi"), sem("mix_lo"))
        units = [(cc, th) for cc in range(KD) for th in range(2)]

        with nc.Block() as block:
            @block.sync
            def _(sp):
                sp.dma_start(gsub[:], row_broadcast(a.subln_g[0], P)).then_inc(gsub_loaded, 16)
                for n, (cc, th) in enumerate(units):
                    if th == 0:
                        ge(sp, w_lo, cc - 1)
                        for b, w in enumerate((a.w_branch_diff, a.w_branch_sb)):
                            sp.dma_start(wraw[:, cc % 2, 4 * b:4 * b + 4, :],
                                         w[0, :, cc * P:(cc + 1) * P].rearrange("(k p) n -> p k n", p=P))\
                                .then_inc(w_loaded[cc % 2], 16)
                    ge(sp, gated, 2 * (n - 1))
                    sp.dma_start(gts[:, n % 2], bass.AP(tensor=c.gates, offset=cc * P * S + th * CH,
                                                        ap=[[S, P], [D * S, 2], [1, CH]])).then_inc(g_loaded[n % 2], 16)

            @block.gpsimd
            def _(pool):
                pool.memset(half[:], -0.5).then_inc(half_ready, 1)
                pool.tensor_scalar(var[:], c.ssq[:].rearrange("p h i -> p (h i)"), 1.0 / P, EPS, ALU.mult, ALU.add)\
                    .then_inc(var_ready, 1)
                pool.wait_ge(half_ready, 1)
                pool.wait_ge(var_ready, 1)
                pool.tensor_tensor(rs[:].rearrange("p h i -> p (h i)"), var[:], half[:], ALU.pow).then_inc(rs_ready, 1)

            @block.scalar
            def _(act):
                def split(cc):
                    act.wait_ge(w_loaded[cc % 2], 32 * (cc // 2 + 1))
                    ge(act, acc_full, 2 * (cc - 1))
                    act.copy(whi[:, cc % 2], wraw[:, cc % 2]).then_inc(w_hi, 1)
                split(0)
                split(1)
                for i in range(NT):
                    act.wait_ge(tp_full, i + 1)
                    act.copy(o_hi[:, :, i * P:(i + 1) * P], tp[i % 2][:]).then_inc(o_hi_ready, 1)
                for n, (cc, th) in enumerate(units):
                    if th == 0 and cc >= 1 and cc + 1 < KD:
                        split(cc + 1)
                    act.wait_ge(mixed, n + 1)
                    act.copy(c.m_hi[:, cc, th * CH:(th + 1) * CH], mix[:]).then_inc(mix_hi, 1)

            @block.vector
            def _(dve):
                def split(cc):
                    dve.wait_ge(w_hi, cc + 1)
                    dve.tensor_sub(wlo[:, cc % 2], wraw[:, cc % 2], whi[:, cc % 2].bitcast(F32)).then_inc(w_lo, 1)
                dve.wait_ge(gsub_loaded, 16)
                dve.tensor_scalar(gsub8[:], gsub[:], 1.0 - LAM_INIT, None, ALU.mult).then_inc(gsub_ready, 1)
                dve.wait_ge(gsub_ready, 1)
                dve.wait_ge(rs_ready, 1)
                def norm(i):
                    for h in range(DH):
                        o = c.mixed_raw[:, i, h * P:(h + 1) * P]
                        ins = dve.scalar_tensor_tensor(out=o, in0=o, scalar=rs[:, h, i:i + 1], in1=gsub8[:],
                                                       op0=ALU.mult, op1=ALU.mult)
                    ins.then_inc(normed, 1)
                norm(0)
                norm(1)
                split(0)
                split(1)
                for i in range(NT):
                    if i + 2 < NT:
                        norm(i + 2)
                    dve.wait_ge(o_hi_ready, i + 1)
                    dve.tensor_sub(o_lo[:, :, i * P:(i + 1) * P], tp[i % 2][:],
                                   o_hi[:, :, i * P:(i + 1) * P].bitcast(F32)).then_inc(o_lo_ready, 1)
                for n, (cc, th) in enumerate(units):
                    if th == 0 and cc >= 1 and cc + 1 < KD:
                        split(cc + 1)
                    dve.wait_ge(acc_full, n + 1)
                    dve.wait_ge(g_loaded[n % 2], 16 * (n // 2 + 1))
                    ge(dve, mixed, n)
                    dve.tensor_tensor(m1[:], pa[n % 2][:], gts[:, n % 2, 0, :], ALU.mult).then_inc(gated, 1)
                    dve.tensor_tensor(m2[:], pb[n % 2][:], gts[:, n % 2, 1, :], ALU.mult).then_inc(gated, 1)
                    dve.wait_ge(gated, 2 * n + 2)
                    ge(dve, mix_lo, n)
                    dve.tensor_tensor(mix[:], m1[:], m2[:], ALU.add).then_inc(mixed, 1)
                    dve.wait_ge(mix_hi, n + 1)
                    dve.tensor_sub(c.m_lo[:, cc, th * CH:(th + 1) * CH], mix[:],
                                   c.m_hi[:, cc, th * CH:(th + 1) * CH].bitcast(F32)).then_inc(mix_lo, 1)

            @block.tensor
            def _(pe):
                for i in range(NT):
                    pe.wait_ge(normed, i + 1)
                    ge(pe, o_lo_ready, i - 1)
                    for k in range(KD):
                        last = pe.transpose(tp[i % 2][:, k, :], c.mixed_raw[:, i, k * P:(k + 1) * P], c.ident[:])
                    last.then_inc(tp_full, 1)
                for n, (cc, th) in enumerate(units):
                    pe.wait_ge(w_lo, cc + 1)
                    pe.wait_ge(o_lo_ready, NT)
                    ge(pe, gated, 2 * (n - 1))
                    for acc, k0 in ((pa, 0), (pb, 4)):
                        for k in range(k0, k0 + 4):
                            cols = slice(th * CH, (th + 1) * CH)
                            last = product(pe, acc[n % 2][:], (whi[:, cc % 2, k, :], wlo[:, cc % 2, k, :]),
                                           (o_hi[:, k, cols], o_lo[:, k, cols]), k == k0, k == k0 + 3)
                    last.then_inc(acc_full, 1)


def output(nc, a, c):
    with ExitStack() as ctx:
        sb, ps, sem = allocators(nc, ctx, "output")
        RAW = 2
        wraw = sb("woraw", [P, RAW, CH])
        whi = sb("wohi", [P, 2, KD, CH], F32R)
        wlo = sb("wolo", [P, 2, KD, CH], F32R)
        x2 = c.mixed_raw
        xt = sb("xto", [P, 2, CH])
        g2 = sb("g2", [P, D])
        h2 = sb("h2", [P, 1, D])
        h2T = sb("h2T", [P, 1, KD, P])
        wr = sb("wr", [P, KD, NG + NE])
        junk = sb("junko", [P, D])
        ss = sb("sso", [P, NT])
        var = sb("varo", [P, NT])
        rs = sb("rso", [P, NT])
        half = sb("halfo", [P, 1])
        L = sb("L", [P, NT, NG + NE])
        acc = [ps(f"acco{i}", [P, CH]) for i in range(2)]
        tp = ps("tpo", [P, KD, P])
        lg = [ps(f"lg{i}", [P, CH]) for i in range(2)]
        rank = ps("rank", [P, CH])
        total = ps("total", [P, CH])
        raw_loaded = [sem(f"wo_loaded{i}") for i in range(RAW)]
        x_loaded = [sem(f"xo_loaded{i}") for i in range(2)]
        g_loaded, wr_loaded, w_hi, w_lo, acc_full, x2_ready = (sem("g2_loaded"), sem("wr_loaded"), sem("wo_hi"), sem("wo_lo"),
                                                               sem("acco_full"), sem("x2_ready"))
        half_ready, squared, var_ready, rs_ready, h2_ready = (sem("halfo_ready"), sem("o_squared"), sem("varo_ready"),
                                                              sem("rso_ready"), sem("h2_ready"))
        h2_stored, x2_stored = sem("h2_stored"), sem("x2_stored")
        tp_full, h2T_ready, lg_full, lg_ready = sem("tpo_full"), sem("h2T_ready"), sem("lg_full"), sem("lg_ready")
        tri_ready, step, exps, ranked = sem("tri_ready"), sem("route_step"), sem("route_exp"), sem("ranked")

        gmax = sb("gmax", [P, NT]); eqg = sb("eqg", [P, NT, NG]); prig = sb("prig", [P, NG]); pmg = sb("pmg", [P, NT])
        gx = sb("gx", [P, NT, NG]); gsum = sb("gsum", [P, NT]); pg = sb("pg", [P, NT])
        sel = sb("sel", [P, NT, NG, EPG]); el = sb("el", [P, NT, EPG]); prie = sb("prie", [P, EPG])
        m1 = sb("m1r", [P, NT]); oh1 = sb("oh1", [P, NT, EPG]); pm = sb("pm", [P, NT]); el2 = sb("el2", [P, NT, EPG])
        m2 = sb("m2r", [P, NT]); oh2 = sb("oh2", [P, NT, EPG]); dx = sb("dx", [P, NT]); e2 = sb("e2", [P, NT])
        den = sb("den", [P, NT]); w1 = sb("w1", [P, NT]); w2 = sb("w2", [P, NT])
        mk = sb("mk", [P, NT, EPG]); gt = sb("gt", [P, NT, EPG]); gt2 = sb("gt2", [P, NT, EPG])
        M = sb("M", [P, NT, NG, EPG]); G = sb("G", [P, NT, NG, EPG]); Mb = sb("Mb", [P, NT * NE], BF16)
        trib = sb("trib", [P, P], BF16); oneb = sb("oneb", [P, P], BF16)
        base = sb("base", [P, NT + 1, NE]); pos = sb("pos", [P, NT, NE]); U = sb("U", [P, NT, NE]); tg = sb("tg", [P, NT])
        rest = sb("restg", [P, NT, NE]); cmax = sb("cmax", [P, 1])

        with nc.Block() as block:
            @block.sync
            def _(sp):
                sp.dma_start(g2[:], row_broadcast(a.ln2_g[0], D)).then_inc(g_loaded, 16)
                for r in range(2 * KD):
                    n, k = divmod(r, KD)
                    ge(sp, w_lo, r - RAW + 1)
                    sp.dma_start(wraw[:, r % RAW, :], a.w_out[0, k * P:(k + 1) * P, n * CH:(n + 1) * CH])\
                        .then_inc(raw_loaded[r % RAW], 16)
                    if r == 7:
                        sp.dma_start(wr[:, :, 0:NG], a.w_group[0].rearrange("(k p) n -> p k n", p=P)).then_inc(wr_loaded, 16)
                        sp.dma_start(wr[:, :, NG:], a.w_router[0].rearrange("(k p) n -> p k n", p=P)).then_inc(wr_loaded, 16)

            def finish(pool, t):
                pool.wait_ge(squared, t + 1)
                pool.tensor_scalar(var[:, t:t + 1], ss[:, t:t + 1], 1.0 / D, EPS, ALU.mult, ALU.add).then_inc(var_ready, 1)
                pool.wait_ge(var_ready, t + 1)
                pool.tensor_tensor(rs[:, t:t + 1], var[:, t:t + 1], half[:], ALU.pow).then_inc(rs_ready, 1)
                pool.dma_start(c.out[0, t * P:(t + 1) * P, :], x2[:, t, :]).then_inc(x2_stored, 16)
                pool.wait_ge(h2_ready, t + 1)
                pool.dma_start(c.h2.ap()[t * P:(t + 1) * P, :], h2[:, 0, :]).then_inc(h2_stored, 16)

            @block.gpsimd
            def _(pool):
                pool.memset(half[:], -0.5).then_inc(half_ready, 1)
                pool.wait_ge(half_ready, 1)
                for m in range(NG):
                    pool.memset(prig[:, m:m + 1], float(NG - m))
                for m in range(EPG):
                    pool.memset(prie[:, m:m + 1], float(EPG - m))
                pool.memset(oneb[:], 1.0).then_inc(tri_ready, 1)
                pool.memset(trib[:], 1.0).then_inc(tri_ready, 1)
                pool.wait_ge(tri_ready, 2)
                pool.affine_select(out=trib[:], in_=trib[:], compare_op=ALU.is_gt, fill=0.0, base=0, pattern=[[1, P]],
                                   channel_multiplier=-1).then_inc(tri_ready, 1)
                pool.iota(tg[:], pattern=[[P, NT]], base=0, channel_multiplier=1,
                          allow_small_or_imprecise_dtypes=True).then_inc(tri_ready, 1)
                pool.iota(c.slots[:], pattern=[[1, P]], base=0, channel_multiplier=0,
                          allow_small_or_imprecise_dtypes=True).then_inc(tri_ready, 1)
                pool.iota(c.table[:, :, :, 0], pattern=[[0, NT], [0, NE]], base=0, channel_multiplier=1,
                          allow_small_or_imprecise_dtypes=True).then_inc(tri_ready, 1)
                pool.iota(c.table[:, :, :, 1], pattern=[[1, NT], [0, NE]], base=0, channel_multiplier=0,
                          allow_small_or_imprecise_dtypes=True).then_inc(tri_ready, 1)
                for n in range(2):
                    for t in range(NT):
                        u = n * NT + t
                        ge(pool, x2_ready, u - 1)
                        pool.dma_start(xt[:, u % 2, :], a.x[0, t * P:(t + 1) * P, n * CH:(n + 1) * CH])\
                            .then_inc(x_loaded[u % 2], 16)
                        if n and t:
                            finish(pool, t - 1)
                finish(pool, NT - 1)
                pool.wait_ge(h2_stored, 16 * NT)
                pool.wait_ge(x2_stored, 16 * NT)

            @block.scalar
            def _(act):
                def split(r):
                    n, k = divmod(r, KD)
                    act.wait_ge(raw_loaded[r % RAW], 16 * (r // RAW + 1))
                    act.copy(whi[:, n, k, :], wraw[:, r % RAW, :]).then_inc(w_hi, 1)
                def evacuate(t):
                    act.wait_ge(tp_full, t + 1)
                    ge(act, lg_full, t)
                    act.copy(h2T[:, 0], tp[:]).then_inc(h2T_ready, 1)
                for r in range(2 * KD):
                    split(r)
                for t in range(NT):
                    act.wait_ge(x2_ready, NT + t + 1)
                    if t:
                        act.wait_ge(squared, t)
                    act.activation(junk[:], x2[:, t, :], ACT.Square, accum_out=ss[:, t:t + 1]).then_inc(squared, 1)
                    if t:
                        evacuate(t - 1)
                evacuate(NT - 1)
                act.wait_ge(step, c.exp_steps[0])
                act.activation(gx[:], gx[:], ACT.Exp).then_inc(exps, 1)
                act.wait_ge(step, c.exp_steps[1])
                act.activation(e2[:], dx[:], ACT.Exp).then_inc(exps, 1)

            @block.vector
            def _(dve):
                def split(r):
                    n, k = divmod(r, KD)
                    dve.wait_ge(w_hi, r + 1)
                    dve.tensor_sub(wlo[:, n, k, :], wraw[:, r % RAW, :], whi[:, n, k, :].bitcast(F32)).then_inc(w_lo, 1)
                def add_x(u):
                    n, t = divmod(u, NT)
                    dve.wait_ge(acc_full, u + 1)
                    dve.wait_ge(x_loaded[u % 2], 16 * (u // 2 + 1))
                    dve.tensor_tensor(x2[:, t, n * CH:(n + 1) * CH], acc[u % 2][:], xt[:, u % 2, :], ALU.add)\
                        .then_inc(x2_ready, 1)
                def norm(t):
                    dve.wait_ge(rs_ready, t + 1)
                    ge(dve, h2_stored, 16 * t)
                    ge(dve, tp_full, t)
                    dve.scalar_tensor_tensor(out=h2[:, 0, :], in0=x2[:, t, :], scalar=rs[:, t:t + 1], in1=g2[:],
                                             op0=ALU.mult, op1=ALU.mult).then_inc(h2_ready, 1)
                def logits(t):
                    dve.wait_ge(lg_full, t + 1)
                    dve.tensor_copy(L[:, t, :], lg[t % 2][:, 0:NG + NE]).then_inc(lg_ready, 1)
                dve.wait_ge(g_loaded, 16)
                for r in range(KD):
                    split(r)
                for u in range(NT):
                    split(KD + u)
                    add_x(u)
                for t in range(NT):
                    add_x(NT + t)
                    if t:
                        norm(t - 1)
                    if t >= 2:
                        logits(t - 2)
                norm(NT - 1)
                logits(NT - 2)
                logits(NT - 1)
                dve.wait_ge(lg_ready, NT)
                dve.wait_ge(tri_ready, 7)

                n = [0]
                def chain(ins):
                    ins.then_inc(step, 1)
                    n[0] += 1
                    dve.wait_ge(step, n[0])
                def over(ap, *shape):
                    return ap.to_broadcast([P, *shape])
                def first_of(onehot, values, top, pri, best):
                    k = onehot.shape[-1]
                    chain(dve.tensor_tensor(onehot[:], values, over(top[:].unsqueeze(2), NT, k), ALU.is_equal))
                    chain(dve.tensor_tensor(onehot[:], onehot[:], over(pri[:].unsqueeze(1), NT, k), ALU.mult))
                    chain(dve.reduce_max(best[:], onehot[:], axis=X))
                    chain(dve.tensor_tensor(onehot[:], onehot[:], over(best[:].unsqueeze(2), NT, k), ALU.is_equal))
                gl = L[:, :, 0:NG]
                chain(dve.reduce_max(gmax[:], gl, axis=X))
                chain(dve.tensor_tensor(gx[:], gl, over(gmax[:].unsqueeze(2), NT, NG), ALU.subtract))
                assert n[0] == c.exp_steps[0]
                first_of(eqg, gl, gmax, prig, pmg)
                ge4 = over(eqg[:].unsqueeze(3), NT, NG, EPG)
                chain(dve.tensor_tensor(sel[:], L[:, :, NG:].rearrange("p t (g e) -> p t g e", e=EPG), ge4, ALU.mult))
                chain(dve.reduce_sum(el[:], sel[:].rearrange("p t g e -> p t e g"), axis=X))
                chain(dve.reduce_max(m1[:], el[:], axis=X))
                first_of(oh1, el[:], m1, prie, pm)
                chain(dve.scalar_tensor_tensor(out=el2[:], in0=oh1[:], scalar=MASKED, in1=el[:], op0=ALU.mult, op1=ALU.add))
                chain(dve.reduce_max(m2[:], el2[:], axis=X))
                first_of(oh2, el2[:], m2, prie, pm)
                chain(dve.tensor_tensor(dx[:], m2[:], m1[:], ALU.subtract))
                assert n[0] == c.exp_steps[1], n[0]
                dve.wait_ge(exps, 2)
                chain(dve.reduce_sum(gsum[:], gx[:], axis=X))
                chain(dve.tensor_scalar(den[:], e2[:], 1.0, None, ALU.add))
                chain(dve.tensor_tensor(den[:], den[:], gsum[:], ALU.mult))
                chain(dve.reciprocal(w1[:], den[:]))
                chain(dve.tensor_tensor(w2[:], w1[:], e2[:], ALU.mult))
                chain(dve.tensor_tensor(mk[:], oh1[:], oh2[:], ALU.add))
                chain(dve.tensor_tensor(gt[:], oh1[:], over(w1[:].unsqueeze(2), NT, EPG), ALU.mult))
                chain(dve.tensor_tensor(gt2[:], oh2[:], over(w2[:].unsqueeze(2), NT, EPG), ALU.mult))
                chain(dve.tensor_tensor(gt[:], gt[:], gt2[:], ALU.add))
                chain(dve.tensor_tensor(M[:], over(mk[:].unsqueeze(2), NT, NG, EPG), ge4, ALU.mult))
                chain(dve.tensor_copy(Mb[:], M[:].rearrange("p t g e -> p (t g e)")))
                assert n[0] == c.mask_step, n[0]
                chain(dve.tensor_tensor(G[:], over(gt[:].unsqueeze(2), NT, NG, EPG), ge4, ALU.mult))
                Gf = G[:].rearrange("p t g e -> p t (g e)")
                Mf = M[:].rearrange("p t g e -> p t (g e)")
                chain(dve.tensor_copy(c.table[:, :, :, 2], Gf))
                chain(dve.tensor_tensor(rest[:], Gf, c.table[:, :, :, 2], ALU.subtract))
                chain(dve.tensor_copy(c.table[:, :, :, 3], rest[:]))
                chain(dve.tensor_tensor(rest[:], rest[:], c.table[:, :, :, 3], ALU.subtract))
                chain(dve.tensor_copy(c.table[:, :, :, 4], rest[:]))
                dve.wait_ge(ranked, 2)
                chain(dve.memset(base[:, 0, :], 0.0))
                for t in range(NT):
                    chain(dve.tensor_tensor(base[:, t + 1, :], base[:, t, :], total[:, t * NE:(t + 1) * NE], ALU.add))
                chain(dve.tensor_tensor(pos[:], base[:, 0:NT, :], rank[:, 0:NT * NE].rearrange("p (t e) -> p t e", e=NE), ALU.add))
                chain(dve.tensor_tensor(U[:], over(tg[:].unsqueeze(2), NT, NE), pos[:], ALU.subtract))
                chain(dve.tensor_tensor(U[:], U[:], over(base[:, NT:NT + 1, :], NT, NE), ALU.add))
                chain(dve.tensor_tensor(pos[:], pos[:], U[:], ALU.subtract))
                chain(dve.tensor_tensor(pos[:], pos[:], Mf, ALU.mult))
                chain(dve.tensor_tensor(c.dest[:], pos[:], U[:], ALU.add))
                chain(dve.reduce_max(cmax[:], base[:, NT, :], axis=X))
                chain(dve.tensor_copy(c.most[:], cmax[:]))

            @block.tensor
            def _(pe):
                def transposes(t):
                    pe.wait_ge(h2_ready, t + 1)
                    ge(pe, h2T_ready, t)
                    for k in range(KD):
                        last = pe.transpose(tp[:, k, :], h2[:, 0, k * P:(k + 1) * P], c.ident[:])
                    last.then_inc(tp_full, 1)
                def router(t):
                    pe.wait_ge(h2T_ready, t + 1)
                    ge(pe, lg_ready, t - 1)
                    for k in range(KD):
                        last = pe.matmul(lg[t % 2][:, 0:NG + NE], h2T[:, 0, k, :], wr[:, k, :], start=k == 0, stop=k == KD - 1)
                    last.then_inc(lg_full, 1)
                for u in range(2 * NT):
                    n, t = divmod(u, NT)
                    if t == 0:
                        pe.wait_ge(w_lo, KD * (n + 1))
                    ge(pe, x2_ready, u - 1)
                    rows = slice(t * P, (t + 1) * P)
                    for k in range(KD):
                        last = product(pe, acc[u % 2][:], (c.m_hi[:, k, rows], c.m_lo[:, k, rows]),
                                       (whi[:, n, k, :], wlo[:, n, k, :]), k == 0, k == KD - 1)
                    last.then_inc(acc_full, 1)
                    if u == NT:
                        pe.wait_ge(wr_loaded, 32)
                    if u > NT + 1:
                        transposes(u - NT - 2)
                        router(u - NT - 2)
                for t in (NT - 2, NT - 1):
                    transposes(t)
                    router(t)
                pe.wait_ge(step, c.mask_step)
                pe.wait_ge(tri_ready, 3)
                pe.matmul(rank[:, 0:NT * NE], trib[:], Mb[:], start=True, stop=True).then_inc(ranked, 1)
                pe.matmul(total[:, 0:NT * NE], oneb[:], Mb[:], start=True, stop=True).then_inc(ranked, 1)


def experts(nc, a, c):
    with ExitStack() as ctx:
        sb, ps, sem = allocators(nc, ctx, "experts")
        wg = sb("wg", [P, 2, KD, FF])
        wu = sb("wu", [P, 2, KD, FF])
        wd = sb("wd", [P, 2, KF, D])
        rows = sb("rows", [P, 2, D])
        rT = sb("rT", [P, 2, KD, P])
        y = sb("y", [P, 2, D])
        sg = sb("sg", [P, 2, FF])
        act_ = sb("act_", [P, FF])
        aT = sb("aT", [P, KF, P])
        hot = sb("hot", [P, NT, P], BF16)
        lst = sb("lst", [P, 2, 5])
        idf = sb("idf", [P, 2])
        idx = sb("idx", [P, 2], U32)
        gate = sb("gate", [P, 2])
        scratch = sb("scratch", [P, 1])
        tpx = ps("tpx", [P, KD, P])
        pg = ps("pgate", [P, FF])
        pu = ps("pup", [P, FF])
        tpa = ps("tpa", [P, KF, P])
        py = ps("py", [P, D])
        pl = ps("plist", [P, CH])
        g_loaded = [sem(f"wg_loaded{i}") for i in range(2)]
        u_loaded = [sem(f"wu_loaded{i}") for i in range(2)]
        d_loaded = [sem(f"wd_loaded{i}") for i in range(2)]
        hot_ready, list_full, list_copied, id_step, idx_ready, gate_ready = (
            sem("hot_ready"), sem("list_full"), sem("list_copied"), sem("id_step"), sem("idx_ready"), sem("gate_ready"))
        gathered = [sem(f"gathered{i}") for i in range(2)]
        rT_full, rT_ready, g_full, u_full, silu_ready, a_ready = (
            sem("rT_full"), sem("rT_ready"), sem("g_full"), sem("u_full"), sem("silu_ready"), sem("a_ready"))
        aT_full, aT_ready, y_full, y_ready, added, ready = (
            sem("aT_full"), sem("aT_ready"), sem("y_full"), sem("y_ready"), sem("added"), sem("ready"))
        moved_on, moved = sem("moved_on"), sem("moved")

        def rounds(eng, body):
            body(0)
            most = eng.value_load(c.most[0:1, 0:1], min_val=0, max_val=2 * S)
            with eng.Fori(1, NT) as r:
                with eng.If(most > r * P):
                    body(r)

        def pairs(eng, r, step):
            with eng.Fori(0, NE // 2 - 1) as p:
                for u in range(2):
                    step(r * NE + p * 2 + u, p * 2 + u, u, False)
            for u in range(2):
                step(r * NE + NE - 2 + u, NE - 2 + u, u, u == 1)

        with nc.Block() as block:
            @block.sync
            def _(sp):
                sp.sem_inc(moved, 1)
                def load(e, u):
                    for dst, src, done in ((wg, a.w_gate, g_loaded), (wu, a.w_up, u_loaded), (wd, a.w_down, d_loaded)):
                        sp.dma_start(dst[:, u], src[0, e].rearrange("(k p) n -> p k n", p=P)).then_inc(done[u], 16)
                def body(r):
                    if type(r) is int:
                        for u in range(2):
                            load(u, u)
                        with sp.Fori(1, NE // 2) as p:
                            for u in range(2):
                                sp.wait_ge(y_full, p * 2 + u - 1)
                                load(p * 2 + u, u)
                    else:
                        with sp.Fori(0, NE // 2) as p:
                            for u in range(2):
                                sp.wait_ge(y_full, r * NE + p * 2 + u - 1)
                                load(p * 2 + u, u)
                rounds(sp, body)

            def hold(eng, sem_, value):
                if type(value) is not int:
                    value = eng.to_reg(value)
                eng.wait_ge(ready, 1)
                eng.wait_ge(sem_, value)

            @block.gpsimd
            def _(pool):
                pool.memset(scratch[:], 0.0).then_inc(ready, 1)
                def gather(n, u):
                    hold(pool, idx_ready, n + 1)
                    pool.indirect_dma_start(out=rows[:, u, :], out_offset=None, in_=c.h2.ap(),
                                            in_offset=bass.IndirectOffsetOnAxis(ap=idx[:, u:u + 1], axis=0))\
                        .then_inc(gathered[u], 16)
                def scatter(n, u):
                    hold(pool, y_ready, n + 1)
                    pool.indirect_dma_start(out=c.out[0], out_offset=bass.IndirectOffsetOnAxis(ap=idx[:, u:u + 1], axis=0),
                                            in_=y[:, u, :], in_offset=None, compute_op=ALU.add).then_inc(added, 16)
                    hold(pool, added, (n + 1) * 16)
                    pool.sem_inc(moved, 1)
                def body(r):
                    gather(r * NE, 0)
                    def step(n, e, u, last):
                        if not last:
                            gather(n + 1, 1 - u)
                        scatter(n, u)
                    pairs(pool, r, step)
                rounds(pool, body)

            @block.scalar
            def _(act):
                def transposed(n, u):
                    act.wait_ge(rT_full, n + 1)
                    act.copy(rT[:, u], tpx[:]).then_inc(rT_ready, 1)
                def body(r):
                    transposed(r * NE, 0)
                    def step(n, e, u, last):
                        act.wait_ge(g_full, n + 1)
                        act.activation(sg[:, u, :], pg[:], ACT.Silu).then_inc(silu_ready, 1)
                        if not last:
                            transposed(n + 1, 1 - u)
                        act.wait_ge(gate_ready, n + 1)
                        act.wait_ge(y_full, n + 1)
                        act.activation(y[:, u, :], py[:], ACT.Copy, scale=gate[:, u:u + 1]).then_inc(y_ready, 1)
                    pairs(act, r, step)
                rounds(act, body)

            @block.vector
            def _(dve):
                def hots(n, e):
                    dve.tensor_tensor(hot[:], c.slots[:].unsqueeze(1).to_broadcast([P, NT, P]),
                                      c.dest[:, :, bass.ds(e, 1)].to_broadcast([P, NT, P]), ALU.is_equal)\
                        .then_inc(hot_ready, 1)
                def ids(n, u, first=False):
                    dve.wait_ge(list_full, n + 1)
                    if not first:
                        dve.wait_ge(moved, n)
                    dve.tensor_copy(lst[:, u, :], pl[:, 0:5]).then_inc(list_copied, 1)
                    dve.wait_ge(list_copied, n + 1)
                    dve.scalar_tensor_tensor(out=idf[:, u:u + 1], in0=lst[:, u, 1:2], scalar=float(P), in1=lst[:, u, 0:1],
                                             op0=ALU.mult, op1=ALU.add).then_inc(id_step, 1)
                    dve.wait_ge(id_step, n + 1)
                    dve.tensor_copy(idx[:, u:u + 1], idf[:, u:u + 1]).then_inc(idx_ready, 1)
                    dve.tensor_reduce(gate[:, u:u + 1], lst[:, u, 2:5], X, ALU.add).then_inc(gate_ready, 1)
                def body(r):
                    if type(r) is not int:
                        dve.wait_ge(hot_ready, r * NE)
                        dve.tensor_scalar(c.dest[:], c.dest[:], -float(P), None, ALU.add).then_inc(moved_on, 1)
                        dve.wait_ge(moved_on, r)
                    hots(r * NE, 0)
                    ids(r * NE, 0, type(r) is int)
                    def step(n, e, u, last):
                        if not last:
                            hots(n + 1, e + 1)
                            ids(n + 1, 1 - u)
                        dve.wait_ge(silu_ready, n + 1)
                        dve.wait_ge(u_full, n + 1)
                        dve.tensor_tensor(act_[:], pu[:], sg[:, u, :], ALU.mult).then_inc(a_ready, 1)
                        dve.wait_ge(aT_full, n + 1)
                        dve.tensor_copy(aT[:], tpa[:]).then_inc(aT_ready, 1)
                    pairs(dve, r, step)
                rounds(dve, body)

            @block.tensor
            def _(pe):
                def listing(n, e, first=False):
                    pe.wait_ge(hot_ready, n + 1)
                    if not first:
                        pe.wait_ge(list_copied, n)
                    for t in range(NT):
                        last = pe.matmul(pl[:, 0:5], hot[:, t, :], c.table[:, t, bass.ds(e, 1), :].rearrange("p a f -> p (a f)"),
                                         start=t == 0, stop=t == NT - 1)
                    last.then_inc(list_full, 1)
                def transposed(n, u, k):
                    pe.wait_ge(gathered[u], k)
                    for j in range(KD):
                        last = pe.transpose(tpx[:, j, :], rows[:, u, j * P:(j + 1) * P], c.ident[:])
                    last.then_inc(rT_full, 1)
                def body(r):
                    first = type(r) is int
                    listing(r * NE, 0, first)
                    if not first:
                        pe.wait_ge(rT_ready, r * NE)
                    transposed(r * NE, 0, r * NE * 8 + 16)
                    def step(n, e, u, last):
                        loads = (n - u) * 8 + 16
                        if not last:
                            listing(n + 1, e + 1)
                        pe.wait_ge(rT_ready, n + 1)
                        pe.wait_ge(g_loaded[u], loads)
                        for k in range(KD):
                            last_ = pe.matmul(pg[:], rT[:, u, k, :], wg[:, u, k, :], start=k == 0, stop=k == KD - 1)
                        last_.then_inc(g_full, 1)
                        pe.wait_ge(u_loaded[u], loads)
                        for k in range(KD):
                            last_ = pe.matmul(pu[:], rT[:, u, k, :], wu[:, u, k, :], start=k == 0, stop=k == KD - 1)
                        last_.then_inc(u_full, 1)
                        if not last:
                            transposed(n + 1, 1 - u, loads if u == 0 else loads + 16)
                        pe.wait_ge(a_ready, n + 1)
                        for k in range(KF):
                            last_ = pe.transpose(tpa[:, k, :], act_[:, k * P:(k + 1) * P], c.ident[:])
                        last_.then_inc(aT_full, 1)
                        pe.wait_ge(aT_ready, n + 1)
                        pe.wait_ge(d_loaded[u], loads)
                        for k in range(KF):
                            for h in range(2):
                                last_ = pe.matmul(py[:, h * CH:(h + 1) * CH], aT[:, k, :], wd[:, u, k, h * CH:(h + 1) * CH],
                                                  start=k == 0, stop=k == KF - 1)
                        last_.then_inc(y_full, 1)
                    pairs(pe, r, step)
                rounds(pe, body)


class Arrays:
    def __init__(self, dram):
        self.x = dram["x"]
        self.rel_bias = dram["rel_bias"]
        self.ln1_g = dram["ln1_g"]
        self.w_in = dram["w_in"]
        self.qnorm_g = dram["qnorm_g"]
        self.knorm_g = dram["knorm_g"]
        self.lambda_q1 = dram["lambda_q1"]
        self.lambda_k1 = dram["lambda_k1"]
        self.lambda_q2 = dram["lambda_q2"]
        self.lambda_k2 = dram["lambda_k2"]
        self.subln_g = dram["subln_g"]
        self.w_branch_diff = dram["w_branch_diff"]
        self.w_branch_sb = dram["w_branch_sb"]
        self.w_out = dram["w_out"]
        self.ln2_g = dram["ln2_g"]
        self.w_group = dram["w_group"]
        self.w_router = dram["w_router"]
        self.w_gate = dram["w_gate"]
        self.w_up = dram["w_up"]
        self.w_down = dram["w_down"]
        self.onehot = dram["onehot"]


class Kept:
    pass


def build(nc, a, out):
    c = Kept()
    c.out = out
    c.exp_steps = (2, 20)
    c.mask_step = 31
    c.stack_q = nc.dram_tensor("stack_q", (16, P, S), F32)
    c.stack_kh = nc.dram_tensor("stack_kh", (16, P, S), F32)
    c.stack_kl = nc.dram_tensor("stack_kl", (16, P, S), F32)
    c.values = nc.dram_tensor("values", (S, 2, CH), F32)
    c.gates = nc.dram_tensor("gates", (2 * D, S), F32)
    c.h2 = nc.dram_tensor("h2_rows", (S, D), F32)
    c.drow_dram = nc.dram_tensor("drow_dram", (DH, DROW), F32)
    with ExitStack() as ctx:
        sb, ps, sem = allocators(nc, ctx, "kept_ctx")
        c.ident = sb("ident", [P, P])
        c.identr = sb("identr", [P, P], F32R)
        c.identb = sb("identb", [P, P], BF16)
        c.maskb = sb("maskb", [P, P], BF16)
        c.neg_lam = sb("neg_lam", [P, 1])
        with ExitStack() as early:
            c.h_hi = early.enter_context(nc.sbuf_tensor("h_hi", [P, KD, S], F32R))
            c.h_lo = early.enter_context(nc.sbuf_tensor("h_lo", [P, KD, S], F32R))
            embed(nc, a, c)
            project(nc, a, c)
        with ExitStack() as late:
            sb, ps, sem = allocators(nc, late, "kept_late")
            c.dest = sb("dest", [P, NT, NE])
            c.table = sb("table", [P, NT, NE, 5], BF16)
            c.most = sb("most", [P, 1], I32)
            c.slots = sb("slots", [P, P])
            with ExitStack() as middle:
                sb, ps, sem = allocators(nc, middle, "kept_middle")
                c.mixed_raw = sb("mixed_raw", [P, NT, D])
                c.ssq = sb("ssq_heads", [P, DH, NT])
                diff(nc, a, c)
                stick(nc, a, c)
                c.m_hi = sb("m_hi", [P, KD, S], F32R)
                c.m_lo = sb("m_lo", [P, KD, S], F32R)
                branch(nc, a, c)
                output(nc, a, c)
            experts(nc, a, c)


_INPUTS = ("x", "rel_bias", "ln1_g", "w_in", "qnorm_g", "knorm_g", "lambda_q1", "lambda_k1", "lambda_q2", "lambda_k2",
           "subln_g", "w_branch_diff", "w_branch_sb", "w_out", "ln2_g", "w_group", "w_router", "w_gate", "w_up", "w_down")


def kernel(**inputs):
    import concourse.bacc as bacc
    from concourse.bass_utils import run_bass_kernel_spmd

    nc = bacc.Bacc("TRN2", target_bir_lowering=False, num_devices=1)
    arrays = {name: np.ascontiguousarray(inputs[name]) for name in _INPUTS}
    arrays["onehot"] = bucket_onehot()
    aps = Arrays({n: nc.dram_tensor(n, v.shape, F32, kind="ExternalInput").ap() for n, v in arrays.items()})
    out = nc.dram_tensor("out", (1, S, D), F32, kind="ExternalOutput").ap()
    build(nc, aps, out)
    return run_bass_kernel_spmd(nc, [arrays], core_ids=[0]).results[0]["out"]
```

```python
import math
from contextlib import ExitStack

import numpy as np
import concourse.bass as bass
from concourse import mybir

F32 = mybir.dt.float32
F32R = mybir.dt.float32r
BF16 = mybir.dt.bfloat16
I32 = mybir.dt.int32
U32 = mybir.dt.uint32
ALU = mybir.AluOpType
ACT = mybir.ActivationFunctionType
X = mybir.AxisListType.X

P = 128
S = 1024
D = 1024
NT = S // P
KD = D // P
HD = 64
DH = 4
SH = 8
CH = 512
NCH = 5120 // CH
TOKEN_CHUNKS = 6
NB, NG, EPG = 32, 4, 8
NE = NG * EPG
FF = 512
KF = FF // P
EPS = 1e-6
MASKED = -1e30
LAM_INIT = 0.8 - 0.6 * math.exp(-0.3 * 0)
DIST0 = P - 1
DROW = 3 * P


def bucket_onehot():
    out = np.zeros((NB, DROW), np.float32)
    for col in range(DIST0, DROW):
        n = col - DIST0
        b = n if n < NB // 2 else min(NB - 1, NB // 2 + int(math.log(n / (NB // 2)) / math.log(128 / (NB // 2)) * (NB // 2)))
        out[b, col] = 1.0
    return out


def ge(eng, sem, value):
    if value > 0:
        eng.wait_ge(sem, value)


def product(pe, out, lhs, rhs, first, last):
    pe.matmul(out, lhs[0], rhs[1], start=first, stop=False)
    pe.matmul(out, lhs[1], rhs[0], start=False, stop=False)
    return pe.matmul(out, lhs[0], rhs[0], start=False, stop=last)


def allocators(nc, ctx, stage, done_sems=None):
    sb = lambda name, shape, dt=F32: ctx.enter_context(nc.sbuf_tensor(f"{stage}_{name}", shape, dt))
    ps = lambda name, shape, dt=F32: ctx.enter_context(nc.psum_tensor(f"{stage}_{name}", shape, dt))
    def sem(name):
        made = ctx.enter_context(nc.semaphore(f"{stage}_{name}"))
        if done_sems is not None:
            done_sems.append(made)
        return made
    return sb, ps, sem


def row_broadcast(ap, n):
    return bass.AP(tensor=ap.tensor, offset=ap.offset, ap=[[0, P], [1, n]])


def embed(nc, a, c):
    with ExitStack() as ctx:
        sb, ps, sem = allocators(nc, ctx, "embed", c.done_sems)
        xt = sb("xt", [P, 2, D])
        junk = sb("junk", [P, D])
        xn = sb("xn", [P, 2, D])
        g1 = sb("g1", [P, D])
        ss = sb("ss", [P, NT])
        var = sb("var", [P, NT])
        rs = sb("rs", [P, NT])
        rel = sb("rel", [NB, DH])
        onehot = sb("onehot", [NB, DROW])
        drow = sb("drow", [DH, DROW])
        drow2 = sb("drow2", [DH, DROW])
        lam4 = sb("lam4", [P, 4, HD])
        lamp = sb("lamp", [P, 2, HD])
        lams = sb("lams", [P, 2])
        lame = sb("lame", [P, 2])
        lamd = sb("lamd", [P, 1])
        tp = [ps(f"tp{i}", [P, KD, P]) for i in range(2)]
        pd = ps("pd", [P, CH])
        x_loaded = [sem(f"x_loaded{i}") for i in range(2)]
        g_loaded, small_loaded, made, squared = sem("g_loaded"), sem("small_loaded"), sem("made"), sem("squared")
        var_ready, rs_ready, xn_ready = sem("var_ready"), sem("rs_ready"), sem("xn_ready")
        xT_ready, hi_ready, lo_ready = sem("xT_ready"), sem("hi_ready"), sem("lo_ready")
        dist_ready, drow_ready, lam_step, lam_exp, stored = (sem("dist_ready"), sem("drow_ready"), sem("lam_step"),
                                                             sem("lam_exp"), sem("stored"))
        with nc.Block() as block:
            @block.sync
            def _(sp):
                sp.dma_start(g1[:], row_broadcast(a.ln1_g[0], D)).then_inc(g_loaded, 16)
                for t in range(NT):
                    if t == 2:
                        sp.dma_start(rel[:], a.rel_bias).then_inc(small_loaded, 16)
                        sp.dma_start(onehot[:], a.onehot).then_inc(small_loaded, 16)
                        for n, v in enumerate((a.lambda_q1, a.lambda_q2, a.lambda_k1, a.lambda_k2)):
                            sp.dma_start(lam4[:, n, :], row_broadcast(v[0], HD)).then_inc(small_loaded, 16)
                    ge(sp, xn_ready, t - 1)
                    sp.dma_start(xt[:, t % 2, :], a.x[0, t * P:(t + 1) * P, :]).then_inc(x_loaded[t % 2], 16)
                sp.wait_ge(drow_ready, 3)
                sp.dma_start(c.drow_dram.ap(), drow2[:]).then_inc(stored, 16)
                sp.wait_ge(stored, 16)

            @block.gpsimd
            def _(pool):
                pool.memset(c.half[:], -0.5).then_inc(made, 1)
                pool.memset(c.ident[:], 0.0).then_inc(made, 1)
                pool.memset(c.maskb[:], 0.0).then_inc(made, 1)
                pool.wait_ge(made, 3)
                pool.affine_select(out=c.ident[:], in_=c.ident[:], compare_op=ALU.not_equal, fill=1.0, base=0,
                                   pattern=[[-1, P]], channel_multiplier=1).then_inc(made, 1)
                pool.affine_select(out=c.maskb[:], in_=c.maskb[:], compare_op=ALU.is_gt, fill=MASKED, base=0,
                                   pattern=[[-1, P]], channel_multiplier=1).then_inc(made, 1)
                for t in range(NT):
                    pool.wait_ge(squared, t + 1)
                    pool.tensor_scalar(var[:, t:t + 1], ss[:, t:t + 1], 1.0 / D, EPS, ALU.mult, ALU.add).then_inc(var_ready, 1)
                    pool.wait_ge(var_ready, t + 1)
                    pool.tensor_tensor(rs[:, t:t + 1], var[:, t:t + 1], c.half[:, 0:1], ALU.pow).then_inc(rs_ready, 1)

            @block.scalar
            def _(act):
                def hi(t):
                    act.wait_ge(xT_ready, t + 1)
                    act.copy(c.h_hi[:, :, t * P:(t + 1) * P], tp[t % 2][:]).then_inc(hi_ready, 1)
                for t in range(NT):
                    act.wait_ge(x_loaded[t % 2], 16 * (t // 2 + 1))
                    if t:
                        act.wait_ge(squared, t)
                    act.activation(junk[:], xt[:, t % 2, :], ACT.Square, accum_out=ss[:, t:t + 1]).then_inc(squared, 1)
                    if t:
                        hi(t - 1)
                hi(NT - 1)
                act.wait_ge(lam_step, 2)
                act.activation(lame[:], lams[:], ACT.Exp).then_inc(lam_exp, 1)

            @block.vector
            def _(dve):
                def lo(t):
                    dve.wait_ge(hi_ready, t + 1)
                    dve.tensor_sub(c.h_lo[:, :, t * P:(t + 1) * P], tp[t % 2][:],
                                   c.h_hi[:, :, t * P:(t + 1) * P].bitcast(F32)).then_inc(lo_ready, 1)
                dve.wait_ge(made, 5)
                dve.tensor_copy(c.identr[:], c.ident[:])
                dve.tensor_copy(c.identb[:], c.ident[:])
                dve.wait_ge(g_loaded, 16)
                for t in range(NT):
                    dve.wait_ge(rs_ready, t + 1)
                    ge(dve, xT_ready, t - 1)
                    dve.scalar_tensor_tensor(out=xn[:, t % 2, :], in0=xt[:, t % 2, :], scalar=rs[:, t:t + 1],
                                             in1=g1[:], op0=ALU.mult, op1=ALU.mult).then_inc(xn_ready, 1)
                    if t:
                        lo(t - 1)
                lo(NT - 1)
                dve.wait_ge(dist_ready, 1)
                dve.tensor_copy(drow[:], pd[0:DH, 0:DROW]).then_inc(drow_ready, 1)
                dve.wait_ge(drow_ready, 1)
                dve.tensor_scalar(drow2[:], drow[:], drow[:, DROW - 1:DROW], None, ALU.subtract).then_inc(drow_ready, 1)
                dve.wait_ge(drow_ready, 2)
                dve.memset(drow2[:, 0:DIST0], MASKED).then_inc(drow_ready, 1)
                dve.tensor_tensor(lamp[:], lam4[:, 0:2, :], lam4[:, 2:4, :], ALU.mult).then_inc(lam_step, 1)
                dve.wait_ge(lam_step, 1)
                dve.reduce_sum(lams[:], lamp[:], axis=X).then_inc(lam_step, 1)
                dve.wait_ge(lam_exp, 1)
                dve.tensor_sub(lamd[:], lame[:, 1:2], lame[:, 0:1]).then_inc(lam_step, 1)
                dve.wait_ge(lam_step, 3)
                dve.tensor_scalar(c.neg_lam[:], lamd[:], -LAM_INIT, None, ALU.add).then_inc(lam_step, 1)

            @block.tensor
            def _(pe):
                pe.wait_ge(made, 4)
                for t in range(NT):
                    pe.wait_ge(xn_ready, t + 1)
                    ge(pe, lo_ready, t - 1)
                    for k in range(KD):
                        last = pe.transpose(tp[t % 2][:, k, :], xn[:, t % 2, k * P:(k + 1) * P], c.ident[:])
                    last.then_inc(xT_ready, 1)
                pe.wait_ge(small_loaded, 96)
                pe.matmul(pd[0:DH, 0:DROW], rel[:], onehot[:], start=True, stop=True).then_inc(dist_ready, 1)


def project(nc, a, c):
    with ExitStack() as ctx:
        sb, ps, sem = allocators(nc, ctx, "project", c.done_sems)
        RAW = 4
        wraw = sb("wraw", [P, RAW, CH])
        whi = sb("whi", [P, 3, KD, CH], F32R)
        wlo = sb("wlo", [P, 3, KD, CH], F32R)
        sq = sb("sq", [P, 2, CH])
        qn = sb("qn", [P, 2, CH])
        qd = sb("qd", [P, 2, SH, 2, HD])
        sthi = sb("sthi", [P, 2, SH, P], F32R)
        stlo = sb("stlo", [P, 1, SH, P], F32R)
        stage = sb("stage", [P, 2, CH])
        gq = sb("gq", [P, 4, HD])
        ss = sb("ssq", [P, 2, SH])
        var = sb("varq", [P, 2, SH])
        rs = sb("rsq", [P, 2, SH])
        acc = [ps(f"acc{i}", [P, CH]) for i in range(4)]
        tp = [ps(f"tq{i}", [P, SH, P]) for i in range(2)]
        raw_loaded = [sem(f"raw_loaded{i}") for i in range(RAW)]
        g_loaded, g_ready = sem("gq_loaded"), sem("gq_ready")
        w_hi, w_lo = sem("w_hi"), sem("w_lo")
        acc_full, acc_free = sem("acc_full"), sem("acc_free")
        squared, ss_ready, var_ready, rs_ready = sem("q_squared"), sem("ss_ready"), sem("q_var"), sem("q_rs")
        qd_ready, tp_full, st_hi, st_lo = sem("qd_ready"), sem("tp_full"), sem("st_hi"), sem("st_lo")
        hi_stored = [sem(f"hi_stored{i}") for i in range(2)]
        lo_stored = sem("lo_stored")
        stage_stored = [sem(f"stage_stored{i}") for i in range(2)]
        gate_ready = sem("gate_ready")

        units = []
        for n in range(NCH):
            for t in range(8):
                units.append((n, t))
        def kind(n):
            return "gate" if n >= TOKEN_CHUNKS else "qkv"[n % 3]
        def turn(n, t):
            return (n // 3) * 16 + (n % 3) * 8 + t
        def value(n, t):
            return (n // 3) * 8 + t
        def gate(n, t):
            return (n - TOKEN_CHUNKS) * 8 + t
        def before(n, t):
            n, t = (n, t - 1) if t else (n - 1, 7)
            return (n, t) if n >= 0 and kind(n) in "qk" else None
        def lo_stores(n, t):
            return (n // 3) * 8 + (t if kind(n) == "k" else 0)
        def slot(n):
            return n % 3 if n < TOKEN_CHUNKS else n % 2

        with nc.Block() as block:
            @block.sync
            def _(sp):
                for n in range(4):
                    if n < 2:
                        sp.dma_start(gq[:, n, :], row_broadcast((a.qnorm_g, a.knorm_g)[n][0], HD)).then_inc(g_loaded, 16)
                for r in range(NCH * KD):
                    n, k = divmod(r, KD)
                    ge(sp, w_lo, r - RAW + 1)
                    sp.dma_start(wraw[:, r % RAW, :], a.w_in[0, k * P:(k + 1) * P, n * CH:(n + 1) * CH])\
                        .then_inc(raw_loaded[r % RAW], 16)

            @block.gpsimd
            def _(pool):
                def store(n, t):
                    m = turn(n, t)
                    j = n // 3
                    pool.wait_ge(st_lo, m + 1)
                    dst = c.stack_q if kind(n) == "q" else c.stack_kh
                    pool.dma_start(dst.ap()[j * 8:j * 8 + 8, :, t * P:(t + 1) * P].rearrange("m p t -> p m t"),
                                   sthi[:, m % 2].bitcast(F32)).then_inc(hi_stored[m % 2], 16)
                    if kind(n) == "k":
                        pool.dma_start(c.stack_kl.ap()[j * 8:j * 8 + 8, :, t * P:(t + 1) * P].rearrange("m p t -> p m t"),
                                       stlo[:, 0].bitcast(F32)).then_inc(lo_stored, 16)
                for n, t in units:
                    if kind(n) in "qk":
                        m = turn(n, t)
                        pool.wait_ge(ss_ready, m + 1)
                        if n < 3:
                            pool.tensor_scalar(var[:, m % 2, :], ss[:, m % 2, :], 1.0 / HD, EPS, ALU.mult, ALU.add)\
                                .then_inc(var_ready, 1)
                            pool.wait_ge(var_ready, m + 1)
                            pool.tensor_tensor(rs[:, m % 2, :], var[:, m % 2, :], c.half[:, 0:SH], ALU.pow).then_inc(rs_ready, 1)
                    prev = before(n, t)
                    if prev:
                        store(*prev)
                    if kind(n) == "v":
                        j = n // 3
                        pool.wait_ge(acc_free, 8 * n + t + 1)
                        pool.dma_start(c.values.ap()[t * P:(t + 1) * P, j, :], stage[:, t % 2, :])\
                            .then_inc(stage_stored[t % 2], 16)
                    if kind(n) == "gate":
                        i = gate(n, t)
                        pool.wait_ge(gate_ready, i + 1)
                        row = (n - TOKEN_CHUNKS) * 4 + t // 2
                        pool.dma_start(c.gates.ap()[row * P:(row + 1) * P, (t % 2) * CH:(t % 2 + 1) * CH],
                                       stage[:, t % 2, :]).then_inc(stage_stored[t % 2], 16)
                pool.wait_ge(hi_stored[0], 16 * 16)
                pool.wait_ge(hi_stored[1], 16 * 16)
                pool.wait_ge(lo_stored, 16 * 16)
                pool.wait_ge(stage_stored[0], 16 * 24)
                pool.wait_ge(stage_stored[1], 16 * 24)

            @block.scalar
            def _(act):
                def split(r):
                    n, k = divmod(r, KD)
                    if n < NCH:
                        act.wait_ge(raw_loaded[r % RAW], 16 * (r // RAW + 1))
                        act.copy(whi[:, slot(n), k, :], wraw[:, r % RAW, :]).then_inc(w_hi, 1)
                def hi(n, t):
                    m = turn(n, t)
                    act.wait_ge(tp_full, m + 1)
                    ge(act, hi_stored[m % 2], 16 * (m // 2))
                    act.copy(sthi[:, m % 2], tp[m % 2][:]).then_inc(st_hi, 1)
                for r in range(KD):
                    split(r)
                for n, t in units:
                    u = 8 * n + t
                    if kind(n) in "qk":
                        act.wait_ge(acc_full, u + 1)
                        act.activation(sq[:, t % 2, :], acc[t % 2][:], ACT.Square).then_inc(squared, 1)
                    if kind(n) == "gate":
                        i = gate(n, t)
                        act.wait_ge(acc_full, u + 1)
                        ge(act, stage_stored[t % 2], 16 * (8 + i // 2))
                        act.activation(stage[:, t % 2, :], acc[2 + t % 2][:], ACT.Sigmoid).then_inc(gate_ready, 1)
                    split(u + KD)
                    if before(n, t):
                        hi(*before(n, t))

            @block.vector
            def _(dve):
                dve.wait_ge(g_loaded, 32)
                dve.tensor_scalar(gq[:, 0, :], gq[:, 0, :], HD ** -0.5, None, ALU.mult).then_inc(g_ready, 1)
                dve.memset(gq[:, 2, :], HD ** -0.5).then_inc(g_ready, 1)
                dve.memset(gq[:, 3, :], 1.0).then_inc(g_ready, 1)
                dve.wait_ge(g_ready, 3)
                def split(r):
                    n, k = divmod(r, KD)
                    if n < NCH:
                        dve.wait_ge(w_hi, r + 1)
                        dve.tensor_sub(wlo[:, slot(n), k, :], wraw[:, r % RAW, :],
                                       whi[:, slot(n), k, :].bitcast(F32)).then_inc(w_lo, 1)
                def lo(n, t):
                    m = turn(n, t)
                    dve.wait_ge(st_hi, m + 1)
                    if kind(n) == "q":
                        dve.tensor_sub(sthi[HD:P, m % 2], tp[m % 2][HD:P],
                                       sthi[HD:P, m % 2].bitcast(F32)).then_inc(st_lo, 1)
                    else:
                        ge(dve, lo_stored, 16 * lo_stores(n, t))
                        dve.tensor_sub(stlo[:, 0], tp[m % 2][:], sthi[:, m % 2].bitcast(F32)).then_inc(st_lo, 1)
                for r in range(KD):
                    split(r)
                for n, t in units:
                    u = 8 * n + t
                    if kind(n) in "qk":
                        m = turn(n, t)
                        s = m % 2
                        dve.wait_ge(squared, m + 1)
                        dve.reduce_sum(ss[:, s, :], sq[:, s, :].rearrange("p (h d) -> p h d", d=HD), axis=X)\
                            .then_inc(ss_ready, 1)
                    split(u + KD)
                    if kind(n) in "qk":
                        a3 = acc[s][:].rearrange("p (h d) -> p h d", d=HD)
                        q3 = qn[:, s, :].rearrange("p (h d) -> p h d", d=HD)
                        if n < 3:
                            dve.wait_ge(rs_ready, m + 1)
                            dve.tensor_tensor(q3, a3, rs[:, s, :].unsqueeze(2).to_broadcast([P, SH, HD]), ALU.mult)\
                                .then_inc(acc_free, 1)
                        else:
                            dve.tensor_copy(q3, a3).then_inc(acc_free, 1)
                        dve.wait_ge(acc_free, u + 1)
                        g = gq[:, 2 * (n // 3) + n % 3, :]
                        for d in range(2):
                            ins = dve.tensor_tensor(qd[:, s, :, d, :], q3, g.unsqueeze(1).to_broadcast([P, SH, HD]),
                                                    ALU.mult)
                        ins.then_inc(qd_ready, 1)
                    if kind(n) == "v":
                        i = value(n, t)
                        dve.wait_ge(acc_full, u + 1)
                        ge(dve, stage_stored[t % 2], 16 * (i // 2))
                        dve.tensor_copy(stage[:, t % 2, :], acc[t % 2][:]).then_inc(acc_free, 1)
                    if before(n, t):
                        lo(*before(n, t))

            @block.tensor
            def _(pe):
                def transposes(n, t):
                    m = turn(n, t)
                    pe.wait_ge(qd_ready, m + 1)
                    ge(pe, st_lo, m - 1)
                    for h in range(SH):
                        last = pe.transpose(tp[m % 2][:, h, :], qd[:, m % 2, h].rearrange("p a d -> p (a d)"), c.ident[:])
                    last.then_inc(tp_full, 1)
                for n, t in units:
                    u = 8 * n + t
                    w = [(whi[:, slot(n), k, :], wlo[:, slot(n), k, :]) for k in range(KD)]
                    pe.wait_ge(w_lo, KD * (n + 1))
                    if kind(n) == "gate":
                        ge(pe, gate_ready, gate(n, t) - 1)
                        cols, half_t = slice(t // 2 * P, (t // 2 + 1) * P), slice(t % 2 * CH, (t % 2 + 1) * CH)
                        for k in range(KD):
                            last = product(pe, acc[2 + t % 2][:], (w[k][0][:, cols], w[k][1][:, cols]),
                                           (c.h_hi[:, k, half_t], c.h_lo[:, k, half_t]), k == 0, k == KD - 1)
                    else:
                        ge(pe, acc_free, u - 1)
                        rows = slice(t * P, (t + 1) * P)
                        for k in range(KD):
                            last = product(pe, acc[t % 2][:], (c.h_hi[:, k, rows], c.h_lo[:, k, rows]), w[k],
                                           k == 0, k == KD - 1)
                    last.then_inc(acc_full, 1)
                    if before(n, t):
                        transposes(*before(n, t))


def attention_steps(heads):
    return [(h + d, i) for h in range(0, heads, 2) for i in reversed(range(NT)) for d in range(2)]


def diff(nc, a, c):
    with ExitStack() as ctx:
        sb, ps, sem = allocators(nc, ctx, "diff")
        q = sb("q", [P, DH, 2, S], F32R)
        kh = sb("kh", [P, DH, 2, S], F32R)
        kl = sb("kl", [P, DH, 2, S], F32R)
        v = sb("v", [P, NT, DH, P])
        dist = sb("dist", [P, DH, 2 * P])
        dhi = sb("dhi", [P, DH, 2 * P], F32R)
        dlo = sb("dlo", [P, DH, 2 * P], F32R)
        prob = sb("prob", [P, 2, 2, S])
        wT = sb("wT", [P, 2, NT, P])
        junk = sb("junkd", [P, P])
        mx = sb("mx", [P, 2, 2])
        nm = sb("nm", [P, 2, 2])
        sums = sb("sums", [P, 2, 2])
        rec = sb("rec", [P, 2, 2])
        rneg = sb("rneg", [P, 2])
        score = [ps(f"score{m}", [P, S]) for m in range(2)]
        tp = ps("tpd", [P, NT, P])
        out = [ps(f"outd{i}", [P, CH]) for i in range(2)]
        loaded = [[sem(f"head_loaded{h}_{m}") for m in range(2)] for h in range(DH)]
        v_loaded, dist_loaded, dist_hi, dist_lo = sem("v_loaded"), sem("dist_loaded"), sem("dist_hi"), sem("dist_lo")
        score_full, max_ready, neg_ready, exp_done = sem("score_full"), sem("max_ready"), sem("neg_ready"), sem("exp_done")
        rec_ready, scaled, combined = sem("rec_ready"), sem("scaled"), sem("combined")
        tp_full, wT_ready, pv_full, ssq_ready, copied = (sem("tpd_full"), sem("wT_ready"), sem("pv_full"), sem("ssq_ready"),
                                                         sem("copied"))
        steps = attention_steps(DH)
        n_steps = len(steps)

        with nc.Block() as block:
            @block.gpsimd
            def _(pool):
                for done in c.done_sems:
                    pool.sem_clear(done)

            @block.sync
            def _(sp):
                sp.dma_start(dist[:], bass.AP(tensor=c.drow_dram, offset=0, ap=[[1, P], [DROW, DH], [1, 2 * P]]))\
                    .then_inc(dist_loaded, 16)
                for h in range(DH):
                    for m in range(2):
                        for dst, src in ((q, c.stack_q), (kh, c.stack_kh), (kl, c.stack_kl)):
                            sp.dma_start(dst[:, h, m].bitcast(F32), src.ap()[h + DH * m]).then_inc(loaded[h][m], 16)
                    if h == 1:
                        sp.dma_start(v[:], c.values.ap()[:, 0, :].rearrange("(n p) (h d) -> p n h d", p=P, d=P))\
                            .then_inc(v_loaded, 16)

            @block.scalar
            def _(act):
                def evacuate(s):
                    act.wait_ge(tp_full, s + 1)
                    ge(act, pv_full, s - 1)
                    nb = steps[s][1] + 1
                    act.copy(wT[:, s % 2, 0:nb, :], tp[:, 0:nb, :]).then_inc(wT_ready, 1)
                def squares(s):
                    h, i = steps[s]
                    act.wait_ge(pv_full, s + 1)
                    if s:
                        act.wait_ge(ssq_ready, s)
                    act.activation(junk[:], out[s % 2][:, 0:P], ACT.Square, accum_out=c.ssq[:, h, i:i + 1])\
                        .then_inc(ssq_ready, 1)
                for s in range(n_steps + 3):
                    if s < n_steps:
                        w = (steps[s][1] + 1) * P
                        ge(act, combined, s - 1)
                        ge(act, tp_full, s - 1)
                        for m in range(2):
                            act.wait_ge(neg_ready, 2 * s + m + 1)
                            act.activation(prob[:, s % 2, m, 0:w], score[m][:, 0:w], ACT.Exp, bias=nm[:, s % 2, m:m + 1],
                                           accum_out=sums[:, s % 2, m:m + 1]).then_inc(exp_done, 1)
                    if 2 <= s < n_steps + 2:
                        evacuate(s - 2)
                    if 3 <= s:
                        squares(s - 3)

            @block.vector
            def _(dve):
                def combine(s):
                    w = (steps[s][1] + 1) * P
                    e = s % 2
                    dve.wait_ge(exp_done, 2 * s + 2)
                    dve.reciprocal(rec[:, e, :], sums[:, e, :]).then_inc(rec_ready, 1)
                    dve.wait_ge(rec_ready, s + 1)
                    dve.tensor_scalar(rneg[:, e:e + 1], rec[:, e, 1:2], c.neg_lam[:], None, ALU.mult).then_inc(scaled, 1)
                    dve.tensor_scalar(prob[:, e, 0, 0:w], prob[:, e, 0, 0:w], rec[:, e, 0:1], None, ALU.mult)\
                        .then_inc(scaled, 1)
                    dve.wait_ge(scaled, 2 * s + 2)
                    dve.scalar_tensor_tensor(out=prob[:, e, 1, 0:w], in0=prob[:, e, 1, 0:w], scalar=rneg[:, e:e + 1],
                                             in1=prob[:, e, 0, 0:w], op0=ALU.mult, op1=ALU.add).then_inc(combined, 1)
                def copy_out(s):
                    h, i = steps[s]
                    dve.wait_ge(ssq_ready, s + 1)
                    dve.tensor_copy(c.mixed_raw[:, i, h * P:(h + 1) * P], out[s % 2][:, 0:P]).then_inc(copied, 1)
                dve.wait_ge(dist_loaded, 16)
                rev = dist[:, :, ::-1]
                dve.tensor_copy(dhi[:], rev).then_inc(dist_hi, 1)
                dve.wait_ge(dist_hi, 1)
                dve.tensor_sub(dlo[:], rev, dhi[:].bitcast(F32)).then_inc(dist_lo, 1)
                for s in range(n_steps + 4):
                    if 4 <= s:
                        copy_out(s - 4)
                    if s < n_steps:
                        w = (steps[s][1] + 1) * P
                        for m in range(2):
                            u = 2 * s + m
                            dve.wait_ge(score_full, u + 1)
                            dve.reduce_max(mx[:, s % 2, m:m + 1], score[m][:, 0:w], axis=X).then_inc(max_ready, 1)
                            dve.wait_ge(max_ready, u + 1)
                            dve.tensor_scalar(nm[:, s % 2, m:m + 1], mx[:, s % 2, m:m + 1], -1.0, None, ALU.mult)\
                                .then_inc(neg_ready, 1)
                    if 1 <= s < n_steps + 1:
                        combine(s - 1)

            @block.tensor
            def _(pe):
                def scores(s):
                    h, i = steps[s]
                    w = (i + 1) * P
                    near = max(0, (i - 1) * P)
                    for m in range(2):
                        u = 2 * s + m
                        if s < 2 or steps[s][0] != steps[s - 2][0]:
                            pe.wait_ge(loaded[h][m], 48)
                        ge(pe, exp_done, u - 1)
                        qt = q[:, h, m, i * P:(i + 1) * P]
                        for c0 in range(0, w, CH):
                            c1 = min(w, c0 + CH)
                            o = score[m][:, c0:c1]
                            b0 = max(c0, near)
                            pe.matmul(o, qt, kl[:, h, m, c0:c1], start=True, stop=False)
                            last = pe.matmul(o, qt, kh[:, h, m, c0:c1], start=False, stop=b0 >= c1)
                            if b0 < c1:
                                d0 = b0 - (i - 1) * P
                                o = score[m][:, b0:c1]
                                pe.matmul(o, c.identr[:], dlo[:, h, d0:d0 + c1 - b0], start=False, stop=False)
                                last = pe.matmul(o, c.identr[:], dhi[:, h, d0:d0 + c1 - b0], start=False, stop=True)
                        last.then_inc(score_full, 1)
                def transposes(s):
                    pe.wait_ge(combined, s + 1)
                    ge(pe, wT_ready, s)
                    for j in range(steps[s][1] + 1):
                        last = pe.transpose(tp[:, j, :], prob[:, s % 2, 1, j * P:(j + 1) * P], c.ident[:])
                    last.then_inc(tp_full, 1)
                def weigh(s):
                    h, i = steps[s]
                    pe.wait_ge(wT_ready, s + 1)
                    ge(pe, copied, s - 1)
                    for j in range(i + 1):
                        last = pe.matmul(out[s % 2][:, 0:P], wT[:, s % 2, j, :], v[:, j, h, :], start=j == 0, stop=j == i)
                    last.then_inc(pv_full, 1)
                pe.wait_ge(dist_lo, 1)
                for s in range(n_steps + 3):
                    if s == 3:
                        pe.wait_ge(v_loaded, 16)
                    if s < n_steps:
                        scores(s)
                    if 2 <= s < n_steps + 2:
                        transposes(s - 2)
                    if 3 <= s:
                        weigh(s - 3)


def stick(nc, a, c):
    with ExitStack() as ctx:
        sb, ps, sem = allocators(nc, ctx, "stick")
        q = sb("qs", [P, SH, S], F32R)
        kh = sb("khs", [P, SH, S], F32R)
        kl = sb("kls", [P, SH, S], F32R)
        v = sb("vs", [P, NT, SH, HD])
        take = sb("take", [P, 2, S])
        rest = sb("rest", [P, 2, S])
        wT = sb("wTs", [P, 2, NT, P])
        z = [ps(f"z{m}", [P, S]) for m in range(2)]
        tp = ps("tps", [P, NT, P])
        out = [ps(f"outs{i}", [P, CH]) for i in range(2)]
        gsub = sb("gsub", [P, P])
        gsub8 = sb("gsub8", [P, P])
        var = sb("varb", [P, DH * NT])
        rs = sb("rsb", [P, DH, NT])
        gsub_loaded, gsub_ready, var_ready, rs_ready = sem("gsub_loaded"), sem("gsub_ready"), sem("varb_ready"), sem("rsb_ready")
        loaded = [sem(f"shead_loaded{h}") for h in range(SH)]
        v_loaded = [sem(f"vs_loaded{i}") for i in range(2)]
        z_full, took, rested, scanned, weighted = (sem("z_full"), sem("took"), sem("rested"),
                                                             sem("scanned"), sem("weighted"))
        tp_full, wT_near, wT_far, pv_full, copied = (sem("tps_full"), sem("wT_near"), sem("wT_far"), sem("pvs_full"),
                                                     sem("copieds"))
        scaled = sem("scaled")
        steps = attention_steps(SH)
        n_steps = len(steps)
        HALF = NT // 2
        def far_count(s):
            return sum(i >= HALF for _, i in steps[:s])

        with nc.Block() as block:
            @block.sync
            def _(sp):
                for h in range(SH):
                    for dst, src in ((q, c.stack_q), (kh, c.stack_kh), (kl, c.stack_kl)):
                        sp.dma_start(dst[:, h].bitcast(F32), src.ap()[8 + h]).then_inc(loaded[h], 16)
                    if h in (1, 2):
                        some = slice(0, 2) if h == 1 else slice(2, SH)
                        sp.dma_start(v[:, :, some], c.values.ap()[:, 1, some.start * HD:some.stop * HD].rearrange(
                            "(n p) (h d) -> p n h d", p=P, d=HD)).then_inc(v_loaded[h - 1], 16)
                sp.dma_start(gsub[:], row_broadcast(a.subln_g[0], P)).then_inc(gsub_loaded, 16)

            @block.gpsimd
            def _(pool):
                pool.wait_ge(gsub_loaded, 16)
                pool.tensor_scalar(gsub8[:], gsub[:], 1.0 - LAM_INIT, None, ALU.mult).then_inc(gsub_ready, 1)
                pool.tensor_scalar(var[:], c.ssq[:].rearrange("p h i -> p (h i)"), 1.0 / P, EPS, ALU.mult, ALU.add)\
                    .then_inc(var_ready, 1)
                pool.wait_ge(var_ready, 1)
                pool.tensor_tensor(rs[:].rearrange("p h i -> p (h i)"), var[:], c.half[:], ALU.pow).then_inc(rs_ready, 1)
                pool.wait_ge(gsub_ready, 1)
                pool.wait_ge(rs_ready, 1)
                for i in range(NT):
                    for h in range(DH):
                        o = c.mixed_raw[:, i, h * P:(h + 1) * P]
                        pool.tensor_scalar(o, o, rs[:, h, i:i + 1], None, ALU.mult).then_inc(scaled, 1)
                        pool.wait_ge(scaled, i * DH + h + 1)
                        pool.tensor_tensor(o, o, gsub8[:], ALU.mult)

            @block.scalar
            def _(act):
                def evacuate(s):
                    nb = min(HALF, steps[s][1] + 1)
                    act.wait_ge(tp_full, s + 1)
                    ge(act, pv_full, s - 1)
                    act.copy(wT[:, s % 2, 0:nb, :], tp[:, 0:nb, :]).then_inc(wT_near, 1)
                for s in range(n_steps + 2):
                    if s < n_steps:
                        w = (steps[s][1] + 1) * P
                        act.wait_ge(z_full, s + 1)
                        ge(act, tp_full, s - 1)
                        act.activation(rest[:, s % 2, 0:w], z[s % 2][:, 0:w], ACT.Sigmoid, scale=-1.0).then_inc(rested, 1)
                        act.activation(take[:, s % 2, 0:w], z[s % 2][:, 0:w], ACT.Sigmoid).then_inc(took, 1)
                    if 2 <= s:
                        evacuate(s - 2)

            @block.vector
            def _(dve):
                def evacuate(s):
                    nb = steps[s][1] + 1
                    if nb > HALF:
                        dve.wait_ge(tp_full, s + 1)
                        ge(dve, pv_full, s - 1)
                        dve.tensor_copy(wT[:, s % 2, HALF:nb, :], tp[:, HALF:nb, :]).then_inc(wT_far, 1)
                def copy_out(s):
                    h, i = steps[s]
                    dve.wait_ge(pv_full, s + 1)
                    dve.tensor_copy(c.mixed_raw[:, i, CH + h * HD:CH + (h + 1) * HD], out[s % 2][:, 0:HD]).then_inc(copied, 1)
                for s in range(n_steps + 4):
                    if 4 <= s:
                        copy_out(s - 4)
                    if s < n_steps:
                        w = (steps[s][1] + 1) * P
                        e = s % 2
                        dve.wait_ge(rested, s + 1)
                        back = rest[:, e, 0:w][:, ::-1]
                        dve.tensor_tensor_scan(back, back, back, 1.0, ALU.mult, ALU.bypass).then_inc(scanned, 1)
                        dve.wait_ge(scanned, s + 1)
                        dve.wait_ge(took, s + 1)
                        dve.tensor_tensor(take[:, e, 0:w - 1], take[:, e, 0:w - 1], rest[:, e, 1:w], ALU.mult)\
                            .then_inc(weighted, 1)
                    if 1 <= s < n_steps + 1:
                        evacuate(s - 1)

            @block.tensor
            def _(pe):
                def scores(s):
                    h, i = steps[s]
                    if s < 2 or steps[s][0] != steps[s - 2][0]:
                        pe.wait_ge(loaded[h], 48)
                    w = (i + 1) * P
                    ge(pe, took, s - 1)
                    for c0 in range(0, w, CH):
                        c1 = min(w, c0 + CH)
                        qt, o = q[:, h, i * P:(i + 1) * P], z[s % 2][:, c0:c1]
                        pe.matmul(o, qt, kl[:, h, c0:c1], start=True, stop=False)
                        last = pe.matmul(o, qt, kh[:, h, c0:c1], start=False, stop=c1 < w)
                    last = pe.matmul(z[s % 2][:, i * P:w], c.identb[:], c.maskb[:], start=False, stop=True)
                    last.then_inc(z_full, 1)
                def transposes(s):
                    pe.wait_ge(weighted, s + 1)
                    ge(pe, wT_near, s)
                    ge(pe, wT_far, far_count(s))
                    for j in range(steps[s][1] + 1):
                        last = pe.transpose(tp[:, j, :], take[:, s % 2, j * P:(j + 1) * P], c.ident[:])
                    last.then_inc(tp_full, 1)
                def weigh(s):
                    h, i = steps[s]
                    pe.wait_ge(wT_near, s + 1)
                    ge(pe, wT_far, far_count(s + 1))
                    ge(pe, copied, s - 1)
                    for j in range(i + 1):
                        last = pe.matmul(out[s % 2][:, 0:HD], wT[:, s % 2, j, :], v[:, j, h, :], start=j == 0, stop=j == i)
                    last.then_inc(pv_full, 1)
                for s in range(n_steps + 3):
                    if s == 3:
                        pe.wait_ge(v_loaded[0], 16)
                    if s == 2 * NT + 3:
                        pe.wait_ge(v_loaded[1], 16)
                    if s < n_steps:
                        scores(s)
                    if 2 <= s < n_steps + 2:
                        transposes(s - 2)
                    if 3 <= s:
                        weigh(s - 3)


def branch(nc, a, c):
    with ExitStack() as ctx:
        sb, ps, sem = allocators(nc, ctx, "branch")
        o_hi = sb("o_hi", [P, KD, S], F32R)
        o_lo = sb("o_lo", [P, KD, S], F32R)
        wraw = sb("wbraw", [P, 2, KD, P])
        whi = sb("wbhi", [P, 2, KD, P], F32R)
        wlo = sb("wblo", [P, 2, KD, P], F32R)
        gts = sb("gts", [P, 2, 2, CH])
        m1 = sb("m1", [P, CH])
        m2 = sb("m2", [P, CH])
        mix = sb("mix", [P, CH])
        tp = [ps(f"tpb{i}", [P, KD, P]) for i in range(2)]
        pa = [ps(f"pa{i}", [P, CH]) for i in range(2)]
        pb = [ps(f"pb{i}", [P, CH]) for i in range(2)]
        w_loaded = [sem(f"wb_loaded{i}") for i in range(2)]
        g_loaded = [sem(f"gate_loaded{i}") for i in range(2)]
        tp_full, o_hi_ready, o_lo_ready = sem("tpb_full"), sem("o_hi_ready"), sem("o_lo_ready")
        w_hi, w_lo, acc_full, gated, mixed, mix_hi, mix_lo = (sem("wb_hi"), sem("wb_lo"), sem("accb_full"), sem("gated"),
                                                              sem("mixed"), sem("mix_hi"), sem("mix_lo"))
        units = [(cc, th) for cc in range(KD) for th in range(2)]

        with nc.Block() as block:
            @block.sync
            def _(sp):
                for n, (cc, th) in enumerate(units):
                    if th == 0:
                        ge(sp, w_lo, cc - 1)
                        for b, w in enumerate((a.w_branch_diff, a.w_branch_sb)):
                            sp.dma_start(wraw[:, cc % 2, 4 * b:4 * b + 4, :],
                                         w[0, :, cc * P:(cc + 1) * P].rearrange("(k p) n -> p k n", p=P))\
                                .then_inc(w_loaded[cc % 2], 16)
                    ge(sp, gated, 2 * (n - 1))
                    sp.dma_start(gts[:, n % 2], bass.AP(tensor=c.gates, offset=cc * P * S + th * CH,
                                                        ap=[[S, P], [D * S, 2], [1, CH]])).then_inc(g_loaded[n % 2], 16)

            @block.scalar
            def _(act):
                def split(cc):
                    act.wait_ge(w_loaded[cc % 2], 32 * (cc // 2 + 1))
                    ge(act, acc_full, 2 * (cc - 1))
                    act.copy(whi[:, cc % 2], wraw[:, cc % 2]).then_inc(w_hi, 1)
                split(0)
                split(1)
                for i in range(NT):
                    act.wait_ge(tp_full, i + 1)
                    act.copy(o_hi[:, :, i * P:(i + 1) * P], tp[i % 2][:]).then_inc(o_hi_ready, 1)
                for n, (cc, th) in enumerate(units):
                    if th == 0 and cc >= 1 and cc + 1 < KD:
                        split(cc + 1)
                    act.wait_ge(mixed, n + 1)
                    act.copy(c.m_hi[:, cc, th * CH:(th + 1) * CH], mix[:]).then_inc(mix_hi, 1)

            @block.vector
            def _(dve):
                def split(cc):
                    dve.wait_ge(w_hi, cc + 1)
                    dve.tensor_sub(wlo[:, cc % 2], wraw[:, cc % 2], whi[:, cc % 2].bitcast(F32)).then_inc(w_lo, 1)
                split(0)
                split(1)
                for i in range(NT):
                    dve.wait_ge(o_hi_ready, i + 1)
                    dve.tensor_sub(o_lo[:, :, i * P:(i + 1) * P], tp[i % 2][:],
                                   o_hi[:, :, i * P:(i + 1) * P].bitcast(F32)).then_inc(o_lo_ready, 1)
                for n, (cc, th) in enumerate(units):
                    if th == 0 and cc >= 1 and cc + 1 < KD:
                        split(cc + 1)
                    dve.wait_ge(acc_full, n + 1)
                    dve.wait_ge(g_loaded[n % 2], 16 * (n // 2 + 1))
                    ge(dve, mixed, n)
                    dve.tensor_tensor(m1[:], pa[n % 2][:], gts[:, n % 2, 0, :], ALU.mult).then_inc(gated, 1)
                    dve.tensor_tensor(m2[:], pb[n % 2][:], gts[:, n % 2, 1, :], ALU.mult).then_inc(gated, 1)
                    dve.wait_ge(gated, 2 * n + 2)
                    ge(dve, mix_lo, n)
                    dve.tensor_tensor(mix[:], m1[:], m2[:], ALU.add).then_inc(mixed, 1)
                    dve.wait_ge(mix_hi, n + 1)
                    dve.tensor_sub(c.m_lo[:, cc, th * CH:(th + 1) * CH], mix[:],
                                   c.m_hi[:, cc, th * CH:(th + 1) * CH].bitcast(F32)).then_inc(mix_lo, 1)

            @block.tensor
            def _(pe):
                for i in range(NT):
                    ge(pe, o_lo_ready, i - 1)
                    for k in range(KD):
                        last = pe.transpose(tp[i % 2][:, k, :], c.mixed_raw[:, i, k * P:(k + 1) * P], c.ident[:])
                    last.then_inc(tp_full, 1)
                for n, (cc, th) in enumerate(units):
                    pe.wait_ge(w_lo, cc + 1)
                    pe.wait_ge(o_lo_ready, NT)
                    ge(pe, gated, 2 * (n - 1))
                    for acc, k0 in ((pa, 0), (pb, 4)):
                        for k in range(k0, k0 + 4):
                            cols = slice(th * CH, (th + 1) * CH)
                            last = product(pe, acc[n % 2][:], (whi[:, cc % 2, k, :], wlo[:, cc % 2, k, :]),
                                           (o_hi[:, k, cols], o_lo[:, k, cols]), k == k0, k == k0 + 3)
                    last.then_inc(acc_full, 1)


def output(nc, a, c):
    with ExitStack() as ctx:
        sb, ps, sem = allocators(nc, ctx, "output")
        RAW = 4
        wraw = sb("woraw", [P, RAW, CH])
        whi = sb("wohi", [P, 2, KD, CH], F32R)
        wlo = sb("wolo", [P, 2, KD, CH], F32R)
        x2 = c.mixed_raw
        xt = sb("xto", [P, 2, CH])
        g2 = sb("g2", [P, D])
        h2 = sb("h2", [P, 2, D])
        h2T = sb("h2T", [P, 2, KD, P])
        wr = sb("wr", [P, KD, NG + NE])
        junk = sb("junko", [P, D])
        ss = sb("sso", [P, NT])
        var = sb("varo", [P, NT])
        rs = sb("rso", [P, NT])
        acc = [ps(f"acco{i}", [P, CH]) for i in range(2)]
        tp = ps("tpo", [P, KD, P])
        lg = [ps(f"lg{i}", [P, CH]) for i in range(2)]
        raw_loaded = [sem(f"wo_loaded{i}") for i in range(RAW)]
        x_loaded = [sem(f"xo_loaded{i}") for i in range(2)]
        g_loaded, wr_loaded, w_hi, w_lo, acc_full, x2_ready = (sem("g2_loaded"), sem("wr_loaded"), sem("wo_hi"), sem("wo_lo"),
                                                               sem("acco_full"), sem("x2_ready"))
        squared, var_ready, rs_ready, h2_ready = sem("o_squared"), sem("varo_ready"), sem("rso_ready"), sem("h2_ready")
        h2_stored, x2_stored = [sem(f"h2_stored{i}") for i in range(2)], sem("x2_stored")
        tp_full, h2T_ready, lg_full, lg_ready = sem("tpo_full"), sem("h2T_ready"), sem("lg_full"), sem("lg_ready")
        tri_ready = sem("tri_ready")

        with nc.Block() as block:
            @block.sync
            def _(sp):
                sp.dma_start(g2[:], row_broadcast(a.ln2_g[0], D)).then_inc(g_loaded, 16)
                for r in range(2 * KD):
                    n, k = divmod(r, KD)
                    ge(sp, w_lo, r - RAW + 1)
                    sp.dma_start(wraw[:, r % RAW, :], a.w_out[0, k * P:(k + 1) * P, n * CH:(n + 1) * CH])\
                        .then_inc(raw_loaded[r % RAW], 16)
                    if r == 7:
                        sp.dma_start(wr[:, :, 0:NG], a.w_group[0].rearrange("(k p) n -> p k n", p=P)).then_inc(wr_loaded, 16)
                        sp.dma_start(wr[:, :, NG:], a.w_router[0].rearrange("(k p) n -> p k n", p=P)).then_inc(wr_loaded, 16)

            def finish(pool, t):
                pool.wait_ge(squared, t + 1)
                pool.tensor_scalar(var[:, t:t + 1], ss[:, t:t + 1], 1.0 / D, EPS, ALU.mult, ALU.add).then_inc(var_ready, 1)
                pool.wait_ge(var_ready, t + 1)
                pool.tensor_tensor(rs[:, t:t + 1], var[:, t:t + 1], c.half[:, 0:1], ALU.pow).then_inc(rs_ready, 1)
                pool.dma_start(c.out[0, t * P:(t + 1) * P, :], x2[:, t, :]).then_inc(x2_stored, 16)
                pool.wait_ge(h2_ready, t + 1)
                pool.dma_start(c.h2.ap()[t * P:(t + 1) * P, :], h2[:, t % 2, :]).then_inc(h2_stored[t % 2], 16)

            @block.gpsimd
            def _(pool):
                for m in range(NG):
                    pool.memset(c.prig[:, m:m + 1], float(NG - m))
                for m in range(EPG):
                    pool.memset(c.prie[:, m:m + 1], float(EPG - m))
                pool.memset(c.oneb[:], 1.0).then_inc(tri_ready, 1)
                pool.memset(c.trib[:], 1.0).then_inc(tri_ready, 1)
                pool.wait_ge(tri_ready, 2)
                pool.affine_select(out=c.trib[:], in_=c.trib[:], compare_op=ALU.is_gt, fill=0.0, base=0, pattern=[[1, P]],
                                   channel_multiplier=-1).then_inc(tri_ready, 1)
                pool.iota(c.tg[:], pattern=[[P, NT]], base=0, channel_multiplier=1,
                          allow_small_or_imprecise_dtypes=True).then_inc(tri_ready, 1)
                pool.iota(c.slots[:], pattern=[[1, P]], base=0, channel_multiplier=0,
                          allow_small_or_imprecise_dtypes=True).then_inc(tri_ready, 1)
                pool.iota(c.table[:, :, :, 0], pattern=[[0, NT], [0, NE]], base=0, channel_multiplier=1,
                          allow_small_or_imprecise_dtypes=True).then_inc(tri_ready, 1)
                pool.iota(c.table[:, :, :, 1], pattern=[[1, NT], [0, NE]], base=0, channel_multiplier=0,
                          allow_small_or_imprecise_dtypes=True).then_inc(tri_ready, 1)
                for n in range(2):
                    for t in range(NT):
                        u = n * NT + t
                        ge(pool, x2_ready, u - 1)
                        pool.dma_start(xt[:, u % 2, :], a.x[0, t * P:(t + 1) * P, n * CH:(n + 1) * CH])\
                            .then_inc(x_loaded[u % 2], 16)
                        if n and t:
                            finish(pool, t - 1)
                finish(pool, NT - 1)
                pool.wait_ge(h2_stored[0], 8 * NT)
                pool.wait_ge(h2_stored[1], 8 * NT)
                pool.wait_ge(x2_stored, 16 * NT)

            @block.scalar
            def _(act):
                def split(r):
                    n, k = divmod(r, KD)
                    act.wait_ge(raw_loaded[r % RAW], 16 * (r // RAW + 1))
                    act.copy(whi[:, n, k, :], wraw[:, r % RAW, :]).then_inc(w_hi, 1)
                def evacuate(t):
                    act.wait_ge(tp_full, t + 1)
                    ge(act, lg_full, t - 1)
                    act.copy(h2T[:, t % 2], tp[:]).then_inc(h2T_ready, 1)
                for r in range(2 * KD):
                    split(r)
                for t in range(NT):
                    act.wait_ge(x2_ready, NT + t + 1)
                    if t:
                        act.wait_ge(squared, t)
                    act.activation(junk[:], x2[:, t, :], ACT.Square, accum_out=ss[:, t:t + 1]).then_inc(squared, 1)
                    if t:
                        evacuate(t - 1)
                evacuate(NT - 1)

            @block.vector
            def _(dve):
                def split(r):
                    n, k = divmod(r, KD)
                    dve.wait_ge(w_hi, r + 1)
                    dve.tensor_sub(wlo[:, n, k, :], wraw[:, r % RAW, :], whi[:, n, k, :].bitcast(F32)).then_inc(w_lo, 1)
                def add_x(u):
                    n, t = divmod(u, NT)
                    dve.wait_ge(acc_full, u + 1)
                    dve.wait_ge(x_loaded[u % 2], 16 * (u // 2 + 1))
                    dve.tensor_tensor(x2[:, t, n * CH:(n + 1) * CH], acc[u % 2][:], xt[:, u % 2, :], ALU.add)\
                        .then_inc(x2_ready, 1)
                def norm(t):
                    dve.wait_ge(rs_ready, t + 1)
                    ge(dve, h2_stored[t % 2], 16 * (t // 2))
                    ge(dve, tp_full, t - 1)
                    dve.scalar_tensor_tensor(out=h2[:, t % 2, :], in0=x2[:, t, :], scalar=rs[:, t:t + 1], in1=g2[:],
                                             op0=ALU.mult, op1=ALU.mult).then_inc(h2_ready, 1)
                def logits(t):
                    dve.wait_ge(lg_full, t + 1)
                    dve.tensor_copy(c.logits[:, t, :], lg[t % 2][:, 0:NG + NE]).then_inc(lg_ready, 1)
                dve.wait_ge(g_loaded, 16)
                for r in range(KD):
                    split(r)
                for u in range(NT):
                    split(KD + u)
                    add_x(u)
                for t in range(NT):
                    add_x(NT + t)
                    if t:
                        norm(t - 1)
                    if t >= 2:
                        logits(t - 2)
                norm(NT - 1)
                logits(NT - 2)
                logits(NT - 1)

            @block.tensor
            def _(pe):
                def transposes(t):
                    pe.wait_ge(h2_ready, t + 1)
                    ge(pe, h2T_ready, t)
                    for k in range(KD):
                        last = pe.transpose(tp[:, k, :], h2[:, t % 2, k * P:(k + 1) * P], c.ident[:])
                    last.then_inc(tp_full, 1)
                def router(t):
                    pe.wait_ge(h2T_ready, t + 1)
                    ge(pe, lg_ready, t - 1)
                    for k in range(KD):
                        last = pe.matmul(lg[t % 2][:, 0:NG + NE], h2T[:, t % 2, k, :], wr[:, k, :], start=k == 0, stop=k == KD - 1)
                    last.then_inc(lg_full, 1)
                for u in range(2 * NT):
                    n, t = divmod(u, NT)
                    ge(pe, x2_ready, u - 1)
                    rows = slice(t * P, (t + 1) * P)
                    for k in range(KD):
                        if t == 0:
                            pe.wait_ge(w_lo, KD * n + k + 1)
                        last = product(pe, acc[u % 2][:], (c.m_hi[:, k, rows], c.m_lo[:, k, rows]),
                                       (whi[:, n, k, :], wlo[:, n, k, :]), k == 0, k == KD - 1)
                    last.then_inc(acc_full, 1)
                    if u == NT:
                        pe.wait_ge(wr_loaded, 32)
                    if u > NT + 1:
                        transposes(u - NT - 2)
                        router(u - NT - 2)
                for t in (NT - 2, NT - 1):
                    transposes(t)
                    router(t)


def experts(nc, a, c):
    with ExitStack() as ctx:
        sb, ps, sem = allocators(nc, ctx, "experts")
        UNITS, RAW, TURN = 6, 8, 4
        KU = KD // 2
        wraw = sb("wraw", [P, RAW, KU * FF])
        whi = sb("whi", [P, UNITS, KU * FF], F32R)
        wlo = sb("wlo", [P, UNITS, KU * FF], F32R)
        rows = sb("rows", [P, 2, D])
        rT_hi = sb("rT_hi", [P, KD, P], F32R)
        rT_lo = sb("rT_lo", [P, KD, P], F32R)
        y = sb("y", [P, 2, D])
        sg = sb("sg", [P, FF])
        act_ = sb("act", [P, FF])
        aT_hi = sb("aT_hi", [P, KF, P], F32R)
        aT_lo = sb("aT_lo", [P, KF, P], F32R)
        hot = sb("hot", [P, NT, P], BF16)
        lst = sb("lst", [P, TURN, 5])
        idf = sb("idf", [P, TURN])
        idx = sb("idx", [P, TURN], U32)
        gate = sb("gate", [P, TURN])
        scratch = sb("scratch", [P, 1])
        tpx = ps("tpx", [P, KD, P])
        pg = ps("pgate", [P, FF])
        pu = ps("pup", [P, FF])
        tpa = ps("tpa", [P, KF, P])
        py = ps("py", [P, D])
        pl = ps("plist", [P, CH])
        raw_loaded = [sem(f"raw_loaded{i}") for i in range(RAW)]
        w_hi, w_lo, units_done = sem("w_hi"), sem("w_lo"), sem("units_done")
        hot_ready, list_full, list_copied, id_step, idx_ready = (
            sem("hot_ready"), sem("list_full"), sem("list_copied"), sem("id_step"), sem("idx_ready"))
        gathered = [sem(f"gathered{i}") for i in range(2)]
        rows_full, rows_hi, rows_lo, silu_ready, a_ready = (sem("rows_full"), sem("rows_hi"), sem("rows_lo"),
                                                            sem("silu_ready"), sem("a_ready"))
        aT_full, aT_hi_ready, aT_lo_ready, y_ready, added, ready = (
            sem("aT_full"), sem("aT_hi_ready"), sem("aT_lo_ready"), sem("y_ready"), sem("added"), sem("ready"))
        moved_on, moved = sem("moved_on"), sem("moved")
        route_step, exps, ranked, first_lo = sem("route_step"), sem("exps"), sem("ranked"), sem("first_lo")
        POOL_UNITS = 2
        EXP_STEPS, MASK_STEP = (2, 20), 31
        MOVED0 = 3

        taken = [0]
        def work(*shape):
            size = math.prod(shape)
            flat = y[:].rearrange("p a n -> p (a n)")[:, taken[0]:taken[0] + size]
            taken[0] += size
            assert taken[0] <= 2 * D
            if len(shape) == 2:
                return flat.rearrange("p (a b) -> p a b", b=shape[1])
            if len(shape) == 3:
                return flat.rearrange("p (a b c) -> p a b c", b=shape[1], c=shape[2])
            return flat
        gmax, eqg, pmg, gx, gsum = work(NT), work(NT, NG), work(NT), work(NT, NG), work(NT)
        sel, el, m1, oh1, pm, el2 = work(NT, NG, EPG), work(NT, EPG), work(NT), work(NT, EPG), work(NT), work(NT, EPG)
        m2, oh2, dx, e2, den, w1, w2 = work(NT), work(NT, EPG), work(NT), work(NT), work(NT), work(NT), work(NT)
        mk, gt, gt2 = work(NT, EPG), work(NT, EPG), work(NT, EPG)
        M, G = work(NT, NG, EPG), work(NT, NG, EPG)
        base, pos, cmax = work(NT + 1, NE), work(NT, NE), work(1)
        U = sel.rearrange("p t g e -> p t (g e)")
        rest = pos
        rank, total = pg, pu
        Mb = sb("Mb", [P, NT * NE], BF16)

        def rounds(eng, body):
            body(0)
            most = eng.value_load(c.most[0:1, 0:1], min_val=0, max_val=2 * S)
            with eng.Fori(1, NT) as r:
                with eng.If(most > r * P):
                    body(r)

        def turns(eng, r, step):
            T = NE // TURN
            with eng.Fori(0, T - 1) as t:
                for i in range(TURN):
                    step(r * NE + t * TURN + i, t * TURN + i, i, r * T + t, 2)
            for i in range(TURN):
                e = NE - TURN + i
                step(r * NE + e, e, i, r * T + T - 1, min(2, TURN - 1 - i))

        def unit_place(i, j):
            return (UNITS * i + j) % RAW

        with nc.Block() as block:
            @block.sync
            def _(sp):
                sp.sem_inc(moved, MOVED0)
                def load(e, i, j):
                    if j < 4:
                        src = (a.w_gate, a.w_up)[j // 2][0, e].rearrange("(h k p) n -> h p k n", h=2, p=P)[j % 2]
                        dst = wraw[:, unit_place(i, j), :].rearrange("p (k n) -> p k n", n=FF)
                    else:
                        src = a.w_down[0, e].rearrange("(h k p) n -> h p k n", h=2, p=P)[j % 2]
                        dst = wraw[:, unit_place(i, j), :].rearrange("p (k n) -> p k n", n=D)
                    sp.dma_start(dst, src).then_inc(raw_loaded[unit_place(i, j)], 16)
                def turn(r, t, first):
                    for i in range(TURN):
                        for j in range(UNITS):
                            if not first or UNITS * i + j >= RAW:
                                sp.wait_ge(w_lo, (r * NE + t * TURN + i) * UNITS + j - RAW + 1)
                            load(t * TURN + i, i, j)
                def body(r):
                    if type(r) is int:
                        turn(0, 0, True)
                    with sp.Fori(1 if type(r) is int else 0, NE // TURN) as t:
                        turn(r, t, False)
                rounds(sp, body)

            def hold(eng, sem_, value):
                if type(value) is not int:
                    value = eng.to_reg(value)
                eng.wait_ge(ready, 1)
                eng.wait_ge(sem_, value)

            @block.gpsimd
            def _(pool):
                pool.memset(scratch[:], 0.0).then_inc(ready, 1)
                def gather(n, i):
                    hold(pool, idx_ready, n + 1)
                    pool.indirect_dma_start(out=rows[:, i % 2, :], out_offset=None, in_=c.h2.ap(),
                                            in_offset=bass.IndirectOffsetOnAxis(ap=idx[:, i:i + 1], axis=0))\
                        .then_inc(gathered[i % 2], 16)
                def scatter(n, i):
                    hold(pool, y_ready, n + 1)
                    pool.indirect_dma_start(out=c.out[0], out_offset=bass.IndirectOffsetOnAxis(ap=idx[:, i:i + 1], axis=0),
                                            in_=y[:, i % 2, :], in_offset=None, compute_op=ALU.add).then_inc(added, 16)
                    hold(pool, added, (n + 1) * 16)
                    pool.sem_inc(moved, 1)
                def body(r):
                    for j in range(POOL_UNITS):
                        pool.wait_ge(w_hi, r * NE * UNITS + j + 1)
                        pool.tensor_tensor(wlo[:, j, :], wraw[:, unit_place(0, j), :], whi[:, j, :].bitcast(F32),
                                           ALU.subtract).then_inc(first_lo, 1)
                    gather(r * NE, 0)
                    gather(r * NE + 1, 1)
                    def step(n, e, i, q, left):
                        if left > 1:
                            hold(pool, rows_full, n + 1)
                            gather(n + 2, (i + 2) % TURN)
                        scatter(n, i)
                    turns(pool, r, step)
                rounds(pool, body)

            @block.scalar
            def _(act):
                def split(n, i, j, q, first=False):
                    act.wait_ge(raw_loaded[unit_place(i, j)], (q * (UNITS * TURN // RAW) + (UNITS * i + j) // RAW + 1) * 16)
                    if not first:
                        act.wait_ge(units_done, (n - 1) * UNITS + j + 1)
                    act.copy(whi[:, j, :], wraw[:, unit_place(i, j), :]).then_inc(w_hi, 1)
                def transposed(n):
                    act.wait_ge(rows_full, n + 1)
                    act.copy(rT_hi[:], tpx[:]).then_inc(rows_hi, 1)
                act.wait_ge(route_step, EXP_STEPS[0])
                act.activation(gx[:], gx[:], ACT.Exp).then_inc(exps, 1)
                act.wait_ge(route_step, EXP_STEPS[1])
                act.activation(e2[:], dx[:], ACT.Exp).then_inc(exps, 1)
                def body(r):
                    for j in range(UNITS):
                        split(r * NE, 0, j, r * (NE // TURN), type(r) is int)
                    transposed(r * NE)
                    def step(n, e, i, q, left):
                        ahead = (n + 1, (i + 1) % TURN)
                        q1 = q + 1 if i == TURN - 1 else q
                        if left:
                            split(*ahead, 0, q1)
                        act.wait_ge(units_done, n * UNITS + 2)
                        act.activation(sg[:], pg[:], ACT.Silu).then_inc(silu_ready, 1)
                        if left:
                            split(*ahead, 1, q1)
                            transposed(n + 1)
                        act.wait_ge(aT_full, n + 1)
                        act.copy(aT_hi[:], tpa[:]).then_inc(aT_hi_ready, 1)
                        if left:
                            for j in range(2, UNITS):
                                split(*ahead, j, q1)
                        act.wait_ge(units_done, (n + 1) * UNITS)
                        act.wait_ge(moved, n + 2)
                        act.copy(y[:, i % 2, :], py[:]).then_inc(y_ready, 1)
                    turns(act, r, step)
                rounds(act, body)

            @block.vector
            def _(dve):
                def routing():
                    count = [0]
                    def chain(ins):
                        ins.then_inc(route_step, 1)
                        count[0] += 1
                        dve.wait_ge(route_step, count[0])
                    def over(ap, *shape):
                        return ap.to_broadcast([P, *shape])
                    def first_of(onehot, values, top, pri, best):
                        k = onehot.shape[-1]
                        chain(dve.tensor_tensor(onehot[:], values, over(top[:].unsqueeze(2), NT, k), ALU.is_equal))
                        chain(dve.tensor_tensor(onehot[:], onehot[:], over(pri[:].unsqueeze(1), NT, k), ALU.mult))
                        chain(dve.reduce_max(best[:], onehot[:], axis=X))
                        chain(dve.tensor_tensor(onehot[:], onehot[:], over(best[:].unsqueeze(2), NT, k), ALU.is_equal))
                    gl = c.logits[:, :, 0:NG]
                    chain(dve.reduce_max(gmax[:], gl, axis=X))
                    chain(dve.tensor_tensor(gx[:], gl, over(gmax[:].unsqueeze(2), NT, NG), ALU.subtract))
                    assert count[0] == EXP_STEPS[0]
                    first_of(eqg, gl, gmax, c.prig, pmg)
                    ge4 = over(eqg[:].unsqueeze(3), NT, NG, EPG)
                    chain(dve.tensor_tensor(sel[:], c.logits[:, :, NG:].rearrange("p t (g e) -> p t g e", e=EPG), ge4, ALU.mult))
                    chain(dve.reduce_sum(el[:], sel[:].rearrange("p t g e -> p t e g"), axis=X))
                    chain(dve.reduce_max(m1[:], el[:], axis=X))
                    first_of(oh1, el[:], m1, c.prie, pm)
                    chain(dve.scalar_tensor_tensor(out=el2[:], in0=oh1[:], scalar=MASKED, in1=el[:], op0=ALU.mult, op1=ALU.add))
                    chain(dve.reduce_max(m2[:], el2[:], axis=X))
                    first_of(oh2, el2[:], m2, c.prie, pm)
                    chain(dve.tensor_tensor(dx[:], m2[:], m1[:], ALU.subtract))
                    assert count[0] == EXP_STEPS[1]
                    dve.wait_ge(exps, 2)
                    chain(dve.reduce_sum(gsum[:], gx[:], axis=X))
                    chain(dve.tensor_scalar(den[:], e2[:], 1.0, None, ALU.add))
                    chain(dve.tensor_tensor(den[:], den[:], gsum[:], ALU.mult))
                    chain(dve.reciprocal(w1[:], den[:]))
                    chain(dve.tensor_tensor(w2[:], w1[:], e2[:], ALU.mult))
                    chain(dve.tensor_tensor(mk[:], oh1[:], oh2[:], ALU.add))
                    chain(dve.tensor_tensor(gt[:], oh1[:], over(w1[:].unsqueeze(2), NT, EPG), ALU.mult))
                    chain(dve.tensor_tensor(gt2[:], oh2[:], over(w2[:].unsqueeze(2), NT, EPG), ALU.mult))
                    chain(dve.tensor_tensor(gt[:], gt[:], gt2[:], ALU.add))
                    chain(dve.tensor_tensor(M[:], over(mk[:].unsqueeze(2), NT, NG, EPG), ge4, ALU.mult))
                    chain(dve.tensor_copy(Mb[:], M[:].rearrange("p t g e -> p (t g e)")))
                    assert count[0] == MASK_STEP
                    chain(dve.tensor_tensor(G[:], over(gt[:].unsqueeze(2), NT, NG, EPG), ge4, ALU.mult))
                    Gf = G[:].rearrange("p t g e -> p t (g e)")
                    Mf = M[:].rearrange("p t g e -> p t (g e)")
                    chain(dve.tensor_copy(c.table[:, :, :, 2], Gf))
                    chain(dve.tensor_tensor(rest[:], Gf, c.table[:, :, :, 2], ALU.subtract))
                    chain(dve.tensor_copy(c.table[:, :, :, 3], rest[:]))
                    chain(dve.tensor_tensor(rest[:], rest[:], c.table[:, :, :, 3], ALU.subtract))
                    chain(dve.tensor_copy(c.table[:, :, :, 4], rest[:]))
                    dve.wait_ge(ranked, 2)
                    chain(dve.memset(base[:, 0, :], 0.0))
                    for t in range(NT):
                        chain(dve.tensor_tensor(base[:, t + 1, :], base[:, t, :], total[:, t * NE:(t + 1) * NE], ALU.add))
                    chain(dve.tensor_tensor(pos[:], base[:, 0:NT, :], rank[:, 0:NT * NE].rearrange("p (t e) -> p t e", e=NE), ALU.add))
                    chain(dve.tensor_tensor(U[:], over(c.tg[:].unsqueeze(2), NT, NE), pos[:], ALU.subtract))
                    chain(dve.tensor_tensor(U[:], U[:], over(base[:, NT:NT + 1, :], NT, NE), ALU.add))
                    chain(dve.tensor_tensor(pos[:], pos[:], U[:], ALU.subtract))
                    chain(dve.tensor_tensor(pos[:], pos[:], Mf, ALU.mult))
                    chain(dve.tensor_tensor(c.dest[:], pos[:], U[:], ALU.add))
                    chain(dve.reduce_max(cmax[:], base[:, NT, :], axis=X))
                    chain(dve.tensor_copy(c.most[:], cmax[:]))
                def hots(e):
                    dve.tensor_tensor(hot[:], c.slots[:].unsqueeze(1).to_broadcast([P, NT, P]),
                                      c.dest[:, :, bass.ds(e, 1)].to_broadcast([P, NT, P]), ALU.is_equal)\
                        .then_inc(hot_ready, 1)
                def ids(n, i, first=False):
                    dve.wait_ge(list_full, n + 1)
                    if not first:
                        dve.wait_ge(moved, n)
                    dve.tensor_copy(lst[:, i, :], pl[:, 0:5]).then_inc(list_copied, 1)
                    dve.wait_ge(list_copied, n + 1)
                    dve.tensor_reduce(gate[:, i:i + 1], lst[:, i, 2:5], X, ALU.add)
                    dve.scalar_tensor_tensor(out=idf[:, i:i + 1], in0=lst[:, i, 1:2], scalar=float(P), in1=lst[:, i, 0:1],
                                             op0=ALU.mult, op1=ALU.add).then_inc(id_step, 1)
                    dve.wait_ge(id_step, n + 1)
                    dve.tensor_copy(idx[:, i:i + 1], idf[:, i:i + 1]).then_inc(idx_ready, 1)
                def split(n, i, j):
                    dve.wait_ge(w_hi, n * UNITS + j + 1)
                    dve.tensor_sub(wlo[:, j, :], wraw[:, unit_place(i, j), :], whi[:, j, :].bitcast(F32)).then_inc(w_lo, 1)
                def transposed(n):
                    dve.wait_ge(rows_hi, n + 1)
                    dve.tensor_sub(rT_lo[:], tpx[:], rT_hi[:].bitcast(F32)).then_inc(rows_lo, 1)
                def body(r):
                    if type(r) is not int:
                        dve.wait_ge(hot_ready, r * NE)
                        dve.tensor_scalar(c.dest[:], c.dest[:], -float(P), None, ALU.add).then_inc(moved_on, 1)
                        dve.wait_ge(moved_on, r)
                    hots(0)
                    ids(r * NE, 0, type(r) is int)
                    hots(1)
                    ids(r * NE + 1, 1)
                    for j in range(POOL_UNITS):
                        dve.wait_ge(first_lo, r * POOL_UNITS + j + 1)
                        dve.sem_inc(w_lo, 1)
                    for j in range(POOL_UNITS, UNITS):
                        split(r * NE, 0, j)
                    transposed(r * NE)
                    def step(n, e, i, q, left):
                        ahead = (n + 1, (i + 1) % TURN)
                        if left > 1:
                            hots(e + 2)
                        if left:
                            split(*ahead, 0)
                            split(*ahead, 1)
                        dve.wait_ge(silu_ready, n + 1)
                        dve.wait_ge(units_done, n * UNITS + 4)
                        dve.scalar_tensor_tensor(out=act_[:], in0=pu[:], scalar=gate[:, i:i + 1], in1=sg[:],
                                                 op0=ALU.mult, op1=ALU.mult).then_inc(a_ready, 1)
                        if left:
                            transposed(n + 1)
                        dve.wait_ge(aT_hi_ready, n + 1)
                        dve.tensor_sub(aT_lo[:], tpa[:], aT_hi[:].bitcast(F32)).then_inc(aT_lo_ready, 1)
                        if left:
                            split(*ahead, 2)
                            split(*ahead, 3)
                        if left > 1:
                            ids(n + 2, (i + 2) % TURN)
                        if left:
                            split(*ahead, 4)
                            split(*ahead, 5)
                    turns(dve, r, step)
                routing()
                rounds(dve, body)

            @block.tensor
            def _(pe):
                def listing(n, e, first=False):
                    pe.wait_ge(hot_ready, n + 1)
                    if not first:
                        pe.wait_ge(list_copied, n)
                    for t in range(NT):
                        last = pe.matmul(pl[:, 0:5], hot[:, t, :], c.table[:, t, bass.ds(e, 1), :].rearrange("p a f -> p (a f)"),
                                         start=t == 0, stop=t == NT - 1)
                    last.then_inc(list_full, 1)
                def transposed(n, s):
                    pe.wait_ge(gathered[s], (n - s) * 8 + 16)
                    for j in range(KD):
                        last = pe.transpose(tpx[:, j, :], rows[:, s, j * P:(j + 1) * P], c.ident[:])
                    last.then_inc(rows_full, 1)
                pe.wait_ge(route_step, MASK_STEP)
                pe.matmul(rank[:, 0:NT * NE], c.trib[:], Mb[:], start=True, stop=True).then_inc(ranked, 1)
                pe.matmul(total[:, 0:NT * NE], c.oneb[:], Mb[:], start=True, stop=True).then_inc(ranked, 1)
                def body(r):
                    first = type(r) is int
                    listing(r * NE, 0, first)
                    listing(r * NE + 1, 1)
                    if not first:
                        pe.wait_ge(rows_lo, r * NE)
                    transposed(r * NE, 0)
                    def step(n, e, i, q, left):
                        pe.wait_ge(rows_lo, n + 1)
                        for j in range(4):
                            pe.wait_ge(w_lo, n * UNITS + j + 1)
                            for k in range(KU):
                                kd, cols = j % 2 * KU + k, slice(k * FF, (k + 1) * FF)
                                last = product(pe, (pg, pu)[j // 2][:], (rT_hi[:, kd, :], rT_lo[:, kd, :]),
                                               (whi[:, j, cols], wlo[:, j, cols]), kd == 0, kd == KD - 1)
                            last.then_inc(units_done, 1)
                        if left:
                            transposed(n + 1, (i + 1) % 2)
                        pe.wait_ge(a_ready, n + 1)
                        for k in range(KF):
                            last = pe.transpose(tpa[:, k, :], act_[:, k * P:(k + 1) * P], c.ident[:])
                        last.then_inc(aT_full, 1)
                        if left > 1:
                            listing(n + 2, e + 2)
                        pe.wait_ge(aT_lo_ready, n + 1)
                        for j in range(4, UNITS):
                            pe.wait_ge(w_lo, n * UNITS + j + 1)
                            for k in range(KF // 2):
                                kf = (j - 4) * KF // 2 + k
                                for h in range(2):
                                    cols = slice(k * D + h * CH, k * D + (h + 1) * CH)
                                    last = product(pe, py[:, h * CH:(h + 1) * CH], (aT_hi[:, kf, :], aT_lo[:, kf, :]),
                                                   (whi[:, j, cols], wlo[:, j, cols]), kf == 0, kf == KF - 1)
                            last.then_inc(units_done, 1)
                    turns(pe, r, step)
                rounds(pe, body)


class Arrays:
    def __init__(self, dram):
        self.x = dram["x"]
        self.rel_bias = dram["rel_bias"]
        self.ln1_g = dram["ln1_g"]
        self.w_in = dram["w_in"]
        self.qnorm_g = dram["qnorm_g"]
        self.knorm_g = dram["knorm_g"]
        self.lambda_q1 = dram["lambda_q1"]
        self.lambda_k1 = dram["lambda_k1"]
        self.lambda_q2 = dram["lambda_q2"]
        self.lambda_k2 = dram["lambda_k2"]
        self.subln_g = dram["subln_g"]
        self.w_branch_diff = dram["w_branch_diff"]
        self.w_branch_sb = dram["w_branch_sb"]
        self.w_out = dram["w_out"]
        self.ln2_g = dram["ln2_g"]
        self.w_group = dram["w_group"]
        self.w_router = dram["w_router"]
        self.w_gate = dram["w_gate"]
        self.w_up = dram["w_up"]
        self.w_down = dram["w_down"]
        self.onehot = dram["onehot"]


class Kept:
    pass


def build(nc, a, out):
    c = Kept()
    c.out = out
    c.stack_q = nc.dram_tensor("stack_q", (16, P, S), F32)
    c.stack_kh = nc.dram_tensor("stack_kh", (16, P, S), F32)
    c.stack_kl = nc.dram_tensor("stack_kl", (16, P, S), F32)
    c.values = nc.dram_tensor("values", (S, 2, CH), F32)
    c.gates = nc.dram_tensor("gates", (2 * D, S), F32)
    c.h2 = nc.dram_tensor("h2_rows", (S, D), F32)
    c.drow_dram = nc.dram_tensor("drow_dram", (DH, DROW), F32)
    with ExitStack() as ctx:
        sb, ps, sem = allocators(nc, ctx, "kept_ctx")
        c.ident = sb("ident", [P, P])
        c.identr = sb("identr", [P, P], F32R)
        c.identb = sb("identb", [P, P], BF16)
        c.maskb = sb("maskb", [P, P], BF16)
        c.neg_lam = sb("neg_lam", [P, 1])
        c.half = sb("half", [P, DH * NT])
        with ExitStack() as early:
            c.h_hi = early.enter_context(nc.sbuf_tensor("h_hi", [P, KD, S], F32R))
            c.h_lo = early.enter_context(nc.sbuf_tensor("h_lo", [P, KD, S], F32R))
            c.done_sems = []
            embed(nc, a, c)
            project(nc, a, c)
        with ExitStack() as late:
            sb, ps, sem = allocators(nc, late, "kept_late")
            c.dest = sb("dest", [P, NT, NE])
            c.table = sb("table", [P, NT, NE, 5], BF16)
            c.most = sb("most", [P, 1], I32)
            c.slots = sb("slots", [P, P])
            c.logits = sb("logits", [P, NT, NG + NE])
            c.tg = sb("tg", [P, NT])
            c.prig = sb("prig", [P, NG])
            c.prie = sb("prie", [P, EPG])
            c.trib = sb("trib", [P, P], BF16)
            c.oneb = sb("oneb", [P, P], BF16)
            with ExitStack() as middle:
                sb, ps, sem = allocators(nc, middle, "kept_middle")
                c.mixed_raw = sb("mixed_raw", [P, NT, D])
                c.ssq = sb("ssq_heads", [P, DH, NT])
                diff(nc, a, c)
                stick(nc, a, c)
                c.m_hi = sb("m_hi", [P, KD, S], F32R)
                c.m_lo = sb("m_lo", [P, KD, S], F32R)
                branch(nc, a, c)
                output(nc, a, c)
            experts(nc, a, c)


_INPUTS = ("x", "rel_bias", "ln1_g", "w_in", "qnorm_g", "knorm_g", "lambda_q1", "lambda_k1", "lambda_q2", "lambda_k2",
           "subln_g", "w_branch_diff", "w_branch_sb", "w_out", "ln2_g", "w_group", "w_router", "w_gate", "w_up", "w_down")


def kernel(**inputs):
    import concourse.bacc as bacc
    from concourse.bass_utils import run_bass_kernel_spmd

    nc = bacc.Bacc("TRN2", target_bir_lowering=False, num_devices=1)
    arrays = {name: np.ascontiguousarray(inputs[name]) for name in _INPUTS}
    arrays["onehot"] = bucket_onehot()
    aps = Arrays({n: nc.dram_tensor(n, v.shape, F32, kind="ExternalInput").ap() for n, v in arrays.items()})
    out = nc.dram_tensor("out", (1, S, D), F32, kind="ExternalOutput").ap()
    build(nc, aps, out)
    return run_bass_kernel_spmd(nc, [arrays], core_ids=[0]).results[0]["out"]
```

```python
import math
from contextlib import ExitStack

import numpy as np
import concourse.bass as bass
from concourse import mybir

F32 = mybir.dt.float32
F32R = mybir.dt.float32r
BF16 = mybir.dt.bfloat16
I32 = mybir.dt.int32
U32 = mybir.dt.uint32
ALU = mybir.AluOpType
ACT = mybir.ActivationFunctionType
X = mybir.AxisListType.X

P = 128
S = 1024
D = 1024
NT = S // P
KD = D // P
HD = 64
DH = 4
SH = 8
CH = 512
TOKEN_CHUNKS = 6
FIRST_CHUNK = 2
ORDER = [0, 1, 3, 4, 5, 6, 7, 8, 9]
RAW_W = 4
NB, NG, EPG = 32, 4, 8
NE = NG * EPG
FF = 512
KF = FF // P
EPS = 1e-6
MASKED = -1e30
LAM_INIT = 0.8 - 0.6 * math.exp(-0.3 * 0)
DIST0 = P - 1
DROW = 3 * P


def bucket_onehot():
    out = np.zeros((NB, DROW), np.float32)
    for col in range(DIST0, DROW):
        n = col - DIST0
        b = n if n < NB // 2 else min(NB - 1, NB // 2 + int(math.log(n / (NB // 2)) / math.log(128 / (NB // 2)) * (NB // 2)))
        out[b, col] = 1.0
    return out


def ge(eng, sem, value):
    if value > 0:
        eng.wait_ge(sem, value)


def product(pe, out, lhs, rhs, first, last):
    pe.matmul(out, lhs[0], rhs[1], start=first, stop=False)
    pe.matmul(out, lhs[1], rhs[0], start=False, stop=False)
    return pe.matmul(out, lhs[0], rhs[0], start=False, stop=last)


def allocators(nc, ctx, stage, done_sems=None):
    sb = lambda name, shape, dt=F32: ctx.enter_context(nc.sbuf_tensor(f"{stage}_{name}", shape, dt))
    ps = lambda name, shape, dt=F32: ctx.enter_context(nc.psum_tensor(f"{stage}_{name}", shape, dt))
    def sem(name):
        made = ctx.enter_context(nc.semaphore(f"{stage}_{name}"))
        if done_sems is not None:
            done_sems.append(made)
        return made
    return sb, ps, sem


def row_broadcast(ap, n):
    return bass.AP(tensor=ap.tensor, offset=ap.offset, ap=[[0, P], [1, n]])


def embed(nc, a, c):
    with ExitStack() as ctx:
        sb, ps, sem = allocators(nc, ctx, "embed", c.done_sems)
        xt = sb("xt", [P, 2, D])
        junk = sb("junk", [P, D])
        xn = sb("xn", [P, 2, D])
        g1 = sb("g1", [P, D])
        ss = sb("ss", [P, NT])
        var = sb("var", [P, NT])
        rs = sb("rs", [P, NT])
        rel = sb("rel", [NB, DH])
        onehot = sb("onehot", [NB, DROW])
        drow = sb("drow", [DH, DROW])
        drow2 = sb("drow2", [DH, DROW])
        lam4 = sb("lam4", [P, 4, HD])
        lamp = sb("lamp", [P, 2, HD])
        lams = sb("lams", [P, 2])
        lame = sb("lame", [P, 2])
        lamd = sb("lamd", [P, 1])
        tp = [ps(f"tp{i}", [P, KD, P]) for i in range(2)]
        pd = ps("pd", [P, CH])
        acc = [ps(f"acc{i}", [P, CH]) for i in range(2)]
        stage = sb("stage", [P, 2, CH])
        raw_loaded = [sem(f"raw_loaded{i}") for i in range(RAW_W)]
        w_hi, w_lo, acc_full, copied = sem("w_hi"), sem("w_lo"), sem("acc_full"), sem("copied")
        W_STEPS = (range(0, 4), range(4, 8), range(8, 10), range(10, 12), range(12, 13), range(13, 14), range(14, 15),
                   range(15, 16))
        def w_tile(r):
            return (FIRST_CHUNK, 2, r) if r < KD else (ORDER[0], 0, r - KD)
        x_loaded = [sem(f"x_loaded{i}") for i in range(2)]
        g_loaded, small_loaded, made, squared = sem("g_loaded"), sem("small_loaded"), sem("made"), sem("squared")
        var_ready, rs_ready, xn_ready = sem("var_ready"), sem("rs_ready"), sem("xn_ready")
        xT_ready, hi_ready, lo_ready = sem("xT_ready"), sem("hi_ready"), sem("lo_ready")
        dist_ready, drow_ready, lam_step, lam_exp, stored = (sem("dist_ready"), sem("drow_ready"), sem("lam_step"),
                                                             sem("lam_exp"), sem("stored"))
        v_stored = [c.pool_dma_sem(f"v_stored{i}") for i in range(2)]
        with nc.Block() as block:
            @block.sync
            def _(sp):
                sp.dma_start(g1[:], row_broadcast(a.ln1_g[0], D)).then_inc(g_loaded, 16)
                for t in range(NT):
                    if t == 2:
                        sp.dma_start(rel[:], a.rel_bias).then_inc(small_loaded, 16)
                        sp.dma_start(onehot[:], a.onehot).then_inc(small_loaded, 16)
                        for n, v in enumerate((a.lambda_q1, a.lambda_q2, a.lambda_k1, a.lambda_k2)):
                            sp.dma_start(lam4[:, n, :], row_broadcast(v[0], HD)).then_inc(small_loaded, 16)
                    ge(sp, xn_ready, t - 1)
                    sp.dma_start(xt[:, t % 2, :], a.x[0, t * P:(t + 1) * P, :]).then_inc(x_loaded[t % 2], 16)
                    for r in W_STEPS[t]:
                        n, _, k = w_tile(r)
                        ge(sp, w_lo, r - RAW_W + 1)
                        sp.dma_start(c.wraw[:, r % RAW_W, :], a.w_in[0, k * P:(k + 1) * P, n * CH:(n + 1) * CH])\
                            .then_inc(raw_loaded[r % RAW_W], 16)
                sp.wait_ge(drow_ready, 3)
                sp.dma_start(c.drow_dram.ap(), drow2[:]).then_inc(stored, 16)
                sp.wait_ge(stored, 16)

            @block.gpsimd
            def _(pool):
                pool.memset(c.half[:], -0.5).then_inc(made, 1)
                pool.memset(c.ident[:], 0.0).then_inc(made, 1)
                pool.memset(c.maskb[:], 0.0).then_inc(made, 1)
                pool.wait_ge(made, 3)
                pool.affine_select(out=c.ident[:], in_=c.ident[:], compare_op=ALU.not_equal, fill=1.0, base=0,
                                   pattern=[[-1, P]], channel_multiplier=1).then_inc(made, 1)
                pool.affine_select(out=c.maskb[:], in_=c.maskb[:], compare_op=ALU.is_gt, fill=MASKED, base=0,
                                   pattern=[[-1, P]], channel_multiplier=1).then_inc(made, 1)
                def store(t):
                    pool.wait_ge(copied, t + 1)
                    pool.dma_start(c.values.ap()[t * P:(t + 1) * P, 0, :], stage[:, t % 2, :]).then_inc(v_stored[t % 2], 16)
                for t in range(NT):
                    pool.wait_ge(squared, t + 1)
                    pool.tensor_scalar(var[:, t:t + 1], ss[:, t:t + 1], 1.0 / D, EPS, ALU.mult, ALU.add).then_inc(var_ready, 1)
                    pool.wait_ge(var_ready, t + 1)
                    pool.tensor_tensor(rs[:, t:t + 1], var[:, t:t + 1], c.half[:, 0:1], ALU.pow).then_inc(rs_ready, 1)
                    if t >= 3:
                        store(t - 3)
                for t in range(NT - 3, NT):
                    store(t)
                pool.wait_ge(v_stored[0], 16 * NT // 2)
                pool.wait_ge(v_stored[1], 16 * NT // 2)

            @block.scalar
            def _(act):
                def hi(t):
                    act.wait_ge(xT_ready, t + 1)
                    act.copy(c.h_hi[:, :, t * P:(t + 1) * P], tp[t % 2][:]).then_inc(hi_ready, 1)
                for t in range(NT):
                    act.wait_ge(x_loaded[t % 2], 16 * (t // 2 + 1))
                    if t:
                        act.wait_ge(squared, t)
                    act.activation(junk[:], xt[:, t % 2, :], ACT.Square, accum_out=ss[:, t:t + 1]).then_inc(squared, 1)
                    for r in W_STEPS[t]:
                        _, place, k = w_tile(r)
                        act.wait_ge(raw_loaded[r % RAW_W], 16 * (r // RAW_W + 1))
                        act.copy(c.whi[:, place, k, :], c.wraw[:, r % RAW_W, :]).then_inc(w_hi, 1)
                    if t:
                        hi(t - 1)
                hi(NT - 1)
                act.wait_ge(lam_step, 2)
                act.activation(lame[:], lams[:], ACT.Exp).then_inc(lam_exp, 1)

            @block.vector
            def _(dve):
                def lo(t):
                    dve.wait_ge(hi_ready, t + 1)
                    dve.tensor_sub(c.h_lo[:, :, t * P:(t + 1) * P], tp[t % 2][:],
                                   c.h_hi[:, :, t * P:(t + 1) * P].bitcast(F32)).then_inc(lo_ready, 1)
                def copy(t):
                    dve.wait_ge(acc_full, t + 1)
                    ge(dve, v_stored[t % 2], 16 * (t // 2))
                    dve.tensor_copy(stage[:, t % 2, :], acc[t % 2][:]).then_inc(copied, 1)
                dve.wait_ge(made, 5)
                dve.tensor_copy(c.identr[:], c.ident[:])
                dve.tensor_copy(c.identb[:], c.ident[:])
                dve.wait_ge(g_loaded, 16)
                for t in range(NT):
                    dve.wait_ge(rs_ready, t + 1)
                    ge(dve, xT_ready, t - 1)
                    dve.scalar_tensor_tensor(out=xn[:, t % 2, :], in0=xt[:, t % 2, :], scalar=rs[:, t:t + 1],
                                             in1=g1[:], op0=ALU.mult, op1=ALU.mult).then_inc(xn_ready, 1)
                    for r in W_STEPS[t]:
                        _, place, k = w_tile(r)
                        dve.wait_ge(w_hi, r + 1)
                        dve.tensor_sub(c.wlo[:, place, k, :], c.wraw[:, r % RAW_W, :], c.whi[:, place, k, :].bitcast(F32))\
                            .then_inc(w_lo, 1)
                    if t:
                        lo(t - 1)
                    if t >= 2:
                        copy(t - 2)
                lo(NT - 1)
                copy(NT - 2)
                copy(NT - 1)
                dve.wait_ge(dist_ready, 1)
                dve.tensor_copy(drow[:], pd[0:DH, 0:DROW]).then_inc(drow_ready, 1)
                dve.wait_ge(drow_ready, 1)
                dve.tensor_scalar(drow2[:], drow[:], drow[:, DROW - 1:DROW], None, ALU.subtract).then_inc(drow_ready, 1)
                dve.wait_ge(drow_ready, 2)
                dve.memset(drow2[:, 0:DIST0], MASKED).then_inc(drow_ready, 1)
                dve.tensor_tensor(lamp[:], lam4[:, 0:2, :], lam4[:, 2:4, :], ALU.mult).then_inc(lam_step, 1)
                dve.wait_ge(lam_step, 1)
                dve.reduce_sum(lams[:], lamp[:], axis=X).then_inc(lam_step, 1)
                dve.wait_ge(lam_exp, 1)
                dve.tensor_sub(lamd[:], lame[:, 1:2], lame[:, 0:1]).then_inc(lam_step, 1)
                dve.wait_ge(lam_step, 3)
                dve.tensor_scalar(c.neg_lam[:], lamd[:], -LAM_INIT, None, ALU.add).then_inc(lam_step, 1)

            @block.tensor
            def _(pe):
                pe.wait_ge(made, 4)
                def values(t):
                    pe.wait_ge(lo_ready, t + 1)
                    ge(pe, copied, t - 1)
                    rows = slice(t * P, (t + 1) * P)
                    for k in range(KD):
                        if t == 0:
                            pe.wait_ge(w_lo, k + 1)
                        last = product(pe, acc[t % 2][:], (c.h_hi[:, k, rows], c.h_lo[:, k, rows]),
                                       (c.whi[:, 2, k, :], c.wlo[:, 2, k, :]), k == 0, k == KD - 1)
                    last.then_inc(acc_full, 1)
                for t in range(NT):
                    pe.wait_ge(xn_ready, t + 1)
                    ge(pe, lo_ready, t - 1)
                    for k in range(KD):
                        last = pe.transpose(tp[t % 2][:, k, :], xn[:, t % 2, k * P:(k + 1) * P], c.ident[:])
                    last.then_inc(xT_ready, 1)
                    if t:
                        values(t - 1)
                values(NT - 1)
                pe.wait_ge(small_loaded, 96)
                pe.matmul(pd[0:DH, 0:DROW], rel[:], onehot[:], start=True, stop=True).then_inc(dist_ready, 1)


def project(nc, a, c):
    with ExitStack() as ctx:
        sb, ps, sem = allocators(nc, ctx, "project", c.done_sems)
        RAW, wraw, whi, wlo = RAW_W, c.wraw, c.whi, c.wlo
        sq = sb("sq", [P, 2, CH])
        qn = sb("qn", [P, 2, CH])
        qd = sb("qd", [P, 2, SH, 2, HD])
        sthi = sb("sthi", [P, 2, SH, P], F32R)
        stlo = sb("stlo", [P, 2, SH, P], F32R)
        stage = sb("stage", [P, 2, CH])
        gq = sb("gq", [P, 4, HD])
        ss = sb("ssq", [P, 2, SH])
        var = sb("varq", [P, 2, SH])
        rs = sb("rsq", [P, 2, SH])
        acc = [ps(f"acc{i}", [P, CH]) for i in range(4)]
        tp = [ps(f"tq{i}", [P, SH, P]) for i in range(2)]
        raw_loaded = [sem(f"raw_loaded{i}") for i in range(RAW)]
        g_loaded, g_ready = sem("gq_loaded"), sem("gq_ready")
        w_hi, w_lo = sem("w_hi"), sem("w_lo")
        acc_full, acc_free = sem("acc_full"), sem("acc_free")
        squared, ss_ready, var_ready, rs_ready = sem("q_squared"), sem("ss_ready"), sem("q_var"), sem("q_rs")
        qd_ready, tp_full, st_hi, st_lo = sem("qd_ready"), sem("tp_full"), sem("st_hi"), sem("st_lo")
        hi_stored = [c.pool_dma_sem(f"hi_stored{i}") for i in range(2)]
        lo_stored = [c.pool_dma_sem(f"lo_stored{i}") for i in range(2)]
        stage_stored = [c.pool_dma_sem(f"stage_stored{i}") for i in range(2)]
        gate_ready, gate_stored = sem("gate_ready"), [sem(f"gate_stored{i}") for i in range(2)]

        units = []
        for n in ORDER:
            for t in range(8):
                units.append((n, t))
        def pos(n):
            return ORDER.index(n)
        def kind(n):
            return "gate" if n >= TOKEN_CHUNKS else "qkv"[n % 3]
        def turn(n, t):
            return (n // 3) * 16 + (n % 3) * 8 + t
        def value(n, t):
            return t
        def gate(n, t):
            return (n - TOKEN_CHUNKS) * 8 + t
        def before(n, t):
            if t == 0 and pos(n) == 0:
                return None
            n, t = (n, t - 1) if t else (ORDER[pos(n) - 1], 7)
            return (n, t) if kind(n) in "qk" else None
        def lo_stores(n, t):
            return (n // 3) * 8 + (t if kind(n) == "k" else 0)
        def slot(n):
            return pos(n) % 3

        with nc.Block() as block:
            @block.sync
            def _(sp):
                GATES0 = 8 * pos(TOKEN_CHUNKS)
                def store(n, t):
                    sp.wait_ge(gate_ready, gate(n, t) + 1)
                    row = (n - TOKEN_CHUNKS) * 4 + t // 2
                    sp.dma_start(c.gates.ap()[row * P:(row + 1) * P, (t % 2) * CH:(t % 2 + 1) * CH],
                                 stage[:, t % 2, :]).then_inc(gate_stored[t % 2], 16)
                for n in range(4):
                    if n < 2:
                        sp.dma_start(gq[:, n, :], row_broadcast((a.qnorm_g, a.knorm_g)[n][0], HD)).then_inc(g_loaded, 16)
                for r in range((len(ORDER) - 1) * KD):
                    n, k = ORDER[1 + r // KD], r % KD
                    ge(sp, w_lo, r - RAW + 1)
                    sp.dma_start(wraw[:, r % RAW, :], a.w_in[0, k * P:(k + 1) * P, n * CH:(n + 1) * CH])\
                        .then_inc(raw_loaded[r % RAW], 16)
                    if r - 5 >= GATES0:
                        store(*units[r - 5])
                for n, t in units[max(GATES0, (len(ORDER) - 1) * KD - 5):]:
                    store(n, t)
                sp.wait_ge(gate_stored[0], 16 * 16)
                sp.wait_ge(gate_stored[1], 16 * 16)

            @block.gpsimd
            def _(pool):
                def store(n, t):
                    m = turn(n, t)
                    j = n // 3
                    pool.wait_ge(st_lo, m + 1)
                    dst = c.stack_q if kind(n) == "q" else c.stack_kh
                    pool.dma_start(dst.ap()[j * 8:j * 8 + 8, :, t * P:(t + 1) * P].rearrange("m p t -> p m t"),
                                   sthi[:, m % 2].bitcast(F32)).then_inc(hi_stored[m % 2], 16)
                    if kind(n) == "k":
                        pool.dma_start(c.stack_kl.ap()[j * 8:j * 8 + 8, :, t * P:(t + 1) * P].rearrange("m p t -> p m t"),
                                       stlo[:, m % 2].bitcast(F32)).then_inc(lo_stored[m % 2], 16)
                for n, t in units:
                    if kind(n) in "qk":
                        m = turn(n, t)
                        pool.wait_ge(ss_ready, m + 1)
                        if n < 3:
                            pool.tensor_scalar(var[:, m % 2, :], ss[:, m % 2, :], 1.0 / HD, EPS, ALU.mult, ALU.add)\
                                .then_inc(var_ready, 1)
                            pool.wait_ge(var_ready, m + 1)
                            pool.tensor_tensor(rs[:, m % 2, :], var[:, m % 2, :], c.half[:, 0:SH], ALU.pow).then_inc(rs_ready, 1)
                    prev = before(n, t)
                    if prev:
                        store(*prev)
                    if kind(n) == "v":
                        j = n // 3
                        pool.wait_ge(acc_free, 8 * pos(n) + t + 1)
                        pool.dma_start(c.values.ap()[t * P:(t + 1) * P, j, :], stage[:, t % 2, :])\
                            .then_inc(stage_stored[t % 2], 16)
                pool.wait_ge(hi_stored[0], 16 * 16)
                pool.wait_ge(hi_stored[1], 16 * 16)
                pool.wait_ge(lo_stored[0], 16 * 8)
                pool.wait_ge(lo_stored[1], 16 * 8)
                pool.wait_ge(stage_stored[0], 16 * 4)
                pool.wait_ge(stage_stored[1], 16 * 4)

            @block.scalar
            def _(act):
                def split(r):
                    if r < (len(ORDER) - 1) * KD:
                        n, k = ORDER[1 + r // KD], r % KD
                        act.wait_ge(raw_loaded[r % RAW], 16 * (r // RAW + 1))
                        act.copy(whi[:, slot(n), k, :], wraw[:, r % RAW, :]).then_inc(w_hi, 1)
                def hi(n, t):
                    m = turn(n, t)
                    act.wait_ge(tp_full, m + 1)
                    ge(act, hi_stored[m % 2], 16 * (m // 2))
                    act.copy(sthi[:, m % 2], tp[m % 2][:]).then_inc(st_hi, 1)
                for n, t in units:
                    u = 8 * pos(n) + t
                    split(u)
                    if kind(n) in "qk":
                        act.wait_ge(acc_full, u + 1)
                        act.activation(sq[:, t % 2, :], acc[t % 4][:], ACT.Square).then_inc(squared, 1)
                    if kind(n) == "gate":
                        i = gate(n, t)
                        act.wait_ge(acc_full, u + 1)
                        if i < 2:
                            act.wait_ge(stage_stored[t % 2], 16 * 4)
                        ge(act, gate_stored[t % 2], 16 * (i // 2))
                        act.activation(stage[:, t % 2, :], acc[t % 4][:], ACT.Sigmoid).then_inc(gate_ready, 1)
                    if before(n, t):
                        hi(*before(n, t))

            @block.vector
            def _(dve):
                dve.wait_ge(g_loaded, 32)
                dve.tensor_scalar(gq[:, 0, :], gq[:, 0, :], HD ** -0.5, None, ALU.mult).then_inc(g_ready, 1)
                dve.memset(gq[:, 2, :], HD ** -0.5).then_inc(g_ready, 1)
                dve.memset(gq[:, 3, :], 1.0).then_inc(g_ready, 1)
                dve.wait_ge(g_ready, 3)
                def split(r):
                    if r < (len(ORDER) - 1) * KD:
                        n, k = ORDER[1 + r // KD], r % KD
                        dve.wait_ge(w_hi, r + 1)
                        dve.tensor_sub(wlo[:, slot(n), k, :], wraw[:, r % RAW, :],
                                       whi[:, slot(n), k, :].bitcast(F32)).then_inc(w_lo, 1)
                def lo(n, t):
                    m = turn(n, t)
                    dve.wait_ge(st_hi, m + 1)
                    if kind(n) == "q":
                        dve.tensor_sub(sthi[HD:P, m % 2], tp[m % 2][HD:P],
                                       sthi[HD:P, m % 2].bitcast(F32)).then_inc(st_lo, 1)
                    else:
                        ge(dve, lo_stored[m % 2], 16 * (lo_stores(n, t) // 2))
                        dve.tensor_sub(stlo[:, m % 2], tp[m % 2][:], sthi[:, m % 2].bitcast(F32)).then_inc(st_lo, 1)
                for n, t in units:
                    u = 8 * pos(n) + t
                    split(u)
                    if kind(n) in "qk":
                        m = turn(n, t)
                        s = m % 2
                        dve.wait_ge(squared, m + 1)
                        dve.reduce_sum(ss[:, s, :], sq[:, s, :].rearrange("p (h d) -> p h d", d=HD), axis=X)\
                            .then_inc(ss_ready, 1)
                    if kind(n) in "qk":
                        a3 = acc[t % 4][:].rearrange("p (h d) -> p h d", d=HD)
                        q3 = qn[:, s, :].rearrange("p (h d) -> p h d", d=HD)
                        if n < 3:
                            dve.wait_ge(rs_ready, m + 1)
                            dve.tensor_tensor(q3, a3, rs[:, s, :].unsqueeze(2).to_broadcast([P, SH, HD]), ALU.mult)\
                                .then_inc(acc_free, 1)
                        else:
                            dve.tensor_copy(q3, a3).then_inc(acc_free, 1)
                        dve.wait_ge(acc_free, u + 1)
                        g = gq[:, 2 * (n // 3) + n % 3, :]
                        for d in range(2):
                            ins = dve.tensor_tensor(qd[:, s, :, d, :], q3, g.unsqueeze(1).to_broadcast([P, SH, HD]),
                                                    ALU.mult)
                        ins.then_inc(qd_ready, 1)
                    if kind(n) == "v":
                        i = value(n, t)
                        dve.wait_ge(acc_full, u + 1)
                        ge(dve, stage_stored[t % 2], 16 * (i // 2))
                        dve.tensor_copy(stage[:, t % 2, :], acc[t % 4][:]).then_inc(acc_free, 1)
                    if before(n, t):
                        lo(*before(n, t))

            @block.tensor
            def _(pe):
                def transposes(n, t):
                    m = turn(n, t)
                    pe.wait_ge(qd_ready, m + 1)
                    ge(pe, st_lo, m - 1)
                    for h in range(SH):
                        last = pe.transpose(tp[m % 2][:, h, :], qd[:, m % 2, h].rearrange("p a d -> p (a d)"), c.ident[:])
                    last.then_inc(tp_full, 1)
                for n, t in units:
                    u = 8 * pos(n) + t
                    w = [(whi[:, slot(n), k, :], wlo[:, slot(n), k, :]) for k in range(KD)]
                    if pos(n):
                        pe.wait_ge(w_lo, KD * pos(n))
                    if kind(n) == "gate":
                        if gate(n, t) < 4:
                            pe.wait_ge(acc_free, u - 3)
                        ge(pe, gate_ready, gate(n, t) - 3)
                        cols, half_t = slice(t // 2 * P, (t // 2 + 1) * P), slice(t % 2 * CH, (t % 2 + 1) * CH)
                        for k in range(KD):
                            last = product(pe, acc[t % 4][:], (w[k][0][:, cols], w[k][1][:, cols]),
                                           (c.h_hi[:, k, half_t], c.h_lo[:, k, half_t]), k == 0, k == KD - 1)
                    else:
                        ge(pe, acc_free, u - 3)
                        rows = slice(t * P, (t + 1) * P)
                        for k in range(KD):
                            last = product(pe, acc[t % 4][:], (c.h_hi[:, k, rows], c.h_lo[:, k, rows]), w[k],
                                           k == 0, k == KD - 1)
                    last.then_inc(acc_full, 1)
                    if before(n, t):
                        transposes(*before(n, t))


def attention_steps(heads):
    return [(h + d, i if h % 4 == 0 else NT - 1 - i) for h in range(0, heads, 2) for i in range(NT) for d in range(2)]


def diff(nc, a, c):
    with ExitStack() as ctx:
        sb, ps, sem = allocators(nc, ctx, "diff")
        q = sb("q", [P, DH, 2, S], F32R)
        kh = sb("kh", [P, DH, 2, S], F32R)
        kl = sb("kl", [P, DH, 2, S], F32R)
        v = sb("v", [P, NT, DH, P])
        dist = sb("dist", [P, DH, 2 * P])
        dhi = sb("dhi", [P, DH, 2 * P], F32R)
        dlo = sb("dlo", [P, DH, 2 * P], F32R)
        prob = sb("prob", [P, 3, 2, S])
        wT = sb("wT", [P, 2, NT, P])
        junk = sb("junkd", [P, P])
        mx = sb("mx", [P, 2, 2])
        nm = sb("nm", [P, 2, 2])
        DEEP = 8
        sums = sb("sums", [P, 2, 2])
        rec = sb("rec", [P, DEEP, 2])
        ratio = sb("ratio", [P, 2])
        score = [ps(f"score{m}", [P, S]) for m in range(2)]
        tp = ps("tpd", [P, NT, P])
        out = [ps(f"outd{i}", [P, CH]) for i in range(2)]
        loaded = [[sem(f"head_loaded{h}_{m}") for m in range(2)] for h in range(DH)]
        v_loaded, dist_loaded, dist_hi, dist_lo = sem("v_loaded"), sem("dist_loaded"), sem("dist_hi"), sem("dist_lo")
        score_full, max_ready, neg_ready, exp_done = sem("score_full"), sem("max_ready"), sem("neg_ready"), sem("exp_done")
        rec_ready, scaled, combined = sem("rec_ready"), sem("scaled"), sem("combined")
        tp_full, wT_ready, pv_full, ssq_ready, copied = (sem("tpd_full"), sem("wT_ready"), sem("pv_full"), sem("ssq_ready"),
                                                         sem("copied"))
        steps = attention_steps(DH)
        n_steps = len(steps)

        with nc.Block() as block:
            @block.gpsimd
            def _(pool):
                for done in c.done_sems:
                    pool.sem_clear(done)

            @block.sync
            def _(sp):
                sp.dma_start(dist[:], bass.AP(tensor=c.drow_dram, offset=0, ap=[[1, P], [DROW, DH], [1, 2 * P]]))\
                    .then_inc(dist_loaded, 16)
                for h in range(DH):
                    for m in range(2):
                        for dst, src in ((q, c.stack_q), (kh, c.stack_kh), (kl, c.stack_kl)):
                            sp.dma_start(dst[:, h, m].bitcast(F32), src.ap()[h + DH * m]).then_inc(loaded[h][m], 16)
                    if h == 1:
                        sp.dma_start(v[:], c.values.ap()[:, 0, :].rearrange("(n p) (h d) -> p n h d", p=P, d=P))\
                            .then_inc(v_loaded, 16)

            @block.scalar
            def _(act):
                def evacuate(s):
                    act.wait_ge(tp_full, s + 1)
                    ge(act, pv_full, s - 1)
                    nb = steps[s][1] + 1
                    act.copy(wT[:, s % 2, 0:nb, :], tp[:, 0:nb, :]).then_inc(wT_ready, 1)
                def squares(s):
                    h, i = steps[s]
                    act.wait_ge(pv_full, s + 1)
                    if s:
                        act.wait_ge(ssq_ready, s)
                    act.activation(junk[:], out[s % 2][:, 0:P], ACT.Square, scale=rec[:, s % DEEP, 0:1],
                                   accum_out=c.ssq[:, h, i:i + 1])\
                        .then_inc(ssq_ready, 1)
                for s in range(n_steps + 3):
                    if s < n_steps:
                        w = (steps[s][1] + 1) * P
                        ge(act, tp_full, s - 2)
                        ge(act, scaled, s - 1)
                        for m in range(2):
                            act.wait_ge(neg_ready, 2 * s + m + 1)
                            act.activation(prob[:, s % 3, m, 0:w], score[m][:, 0:w], ACT.Exp, bias=nm[:, s % 2, m:m + 1],
                                           accum_out=sums[:, s % 2, m:m + 1]).then_inc(exp_done, 1)
                    if 2 <= s < n_steps + 2:
                        evacuate(s - 2)
                    if 3 <= s:
                        squares(s - 3)

            @block.vector
            def _(dve):
                def reciprocals(s):
                    dve.wait_ge(exp_done, 2 * s + 2)
                    dve.reciprocal(rec[:, s % DEEP, :], sums[:, s % 2, :]).then_inc(rec_ready, 1)
                def scale(s):
                    dve.wait_ge(rec_ready, s + 1)
                    dve.tensor_scalar(ratio[:, s % 2:s % 2 + 1], sums[:, s % 2, 0:1], c.neg_lam[:], rec[:, s % DEEP, 1:2],
                                      ALU.mult, ALU.mult).then_inc(scaled, 1)
                def combine(s):
                    w = (steps[s][1] + 1) * P
                    e = s % 2
                    dve.wait_ge(scaled, s + 1)
                    dve.scalar_tensor_tensor(out=prob[:, s % 3, 1, 0:w], in0=prob[:, s % 3, 1, 0:w], scalar=ratio[:, e:e + 1],
                                             in1=prob[:, s % 3, 0, 0:w], op0=ALU.mult, op1=ALU.add).then_inc(combined, 1)
                def copy_out(s):
                    h, i = steps[s]
                    dve.wait_ge(ssq_ready, s + 1)
                    dve.tensor_scalar(c.mixed_raw[:, i, h * P:(h + 1) * P], out[s % 2][:, 0:P], rec[:, s % DEEP, 0:1], None,
                                      ALU.mult).then_inc(copied, 1)
                dve.wait_ge(dist_loaded, 16)
                rev = dist[:, :, ::-1]
                dve.tensor_copy(dhi[:], rev).then_inc(dist_hi, 1)
                dve.wait_ge(dist_hi, 1)
                dve.tensor_sub(dlo[:], rev, dhi[:].bitcast(F32)).then_inc(dist_lo, 1)
                def top(s, m):
                    w = (steps[s][1] + 1) * P
                    dve.wait_ge(score_full, 2 * s + m + 1)
                    dve.reduce_max(mx[:, s % 2, m:m + 1], score[m][:, 0:w], axis=X).then_inc(max_ready, 1)
                def negate(s, m):
                    dve.wait_ge(max_ready, 2 * s + m + 1)
                    dve.tensor_scalar(nm[:, s % 2, m:m + 1], mx[:, s % 2, m:m + 1], -1.0, None, ALU.mult)\
                        .then_inc(neg_ready, 1)
                for s in range(n_steps + 4):
                    if s < n_steps:
                        top(s, 0)
                        negate(s, 0)
                        top(s, 1)
                    if 1 <= s < n_steps + 1:
                        reciprocals(s - 1)
                    if s < n_steps:
                        negate(s, 1)
                    if 1 <= s < n_steps + 1:
                        scale(s - 1)
                    if 4 <= s:
                        copy_out(s - 4)
                    if 1 <= s < n_steps + 1:
                        combine(s - 1)

            @block.tensor
            def _(pe):
                def scores(s):
                    h, i = steps[s]
                    w = (i + 1) * P
                    near = max(0, (i - 1) * P)
                    for m in range(2):
                        u = 2 * s + m
                        if s < 2 or steps[s][0] != steps[s - 2][0]:
                            pe.wait_ge(loaded[h][m], 48)
                        ge(pe, exp_done, u - 1)
                        qt = q[:, h, m, i * P:(i + 1) * P]
                        for c0 in range(0, w, CH):
                            c1 = min(w, c0 + CH)
                            o = score[m][:, c0:c1]
                            b0 = max(c0, near)
                            pe.matmul(o, qt, kl[:, h, m, c0:c1], start=True, stop=False)
                            last = pe.matmul(o, qt, kh[:, h, m, c0:c1], start=False, stop=b0 >= c1)
                            if b0 < c1:
                                d0 = b0 - (i - 1) * P
                                o = score[m][:, b0:c1]
                                pe.matmul(o, c.identr[:], dlo[:, h, d0:d0 + c1 - b0], start=False, stop=False)
                                last = pe.matmul(o, c.identr[:], dhi[:, h, d0:d0 + c1 - b0], start=False, stop=True)
                        last.then_inc(score_full, 1)
                def transposes(s):
                    pe.wait_ge(combined, s + 1)
                    ge(pe, wT_ready, s)
                    for j in range(steps[s][1] + 1):
                        last = pe.transpose(tp[:, j, :], prob[:, s % 3, 1, j * P:(j + 1) * P], c.ident[:])
                    last.then_inc(tp_full, 1)
                def weigh(s):
                    h, i = steps[s]
                    pe.wait_ge(wT_ready, s + 1)
                    ge(pe, copied, s - 1)
                    for j in range(i + 1):
                        last = pe.matmul(out[s % 2][:, 0:P], wT[:, s % 2, j, :], v[:, j, h, :], start=j == 0, stop=j == i)
                    last.then_inc(pv_full, 1)
                pe.wait_ge(dist_lo, 1)
                for s in range(n_steps + 3):
                    if s == 3:
                        pe.wait_ge(v_loaded, 16)
                    if s < n_steps:
                        scores(s)
                    if 2 <= s < n_steps + 2:
                        transposes(s - 2)
                    if 3 <= s:
                        weigh(s - 3)


def stick(nc, a, c):
    with ExitStack() as ctx:
        sb, ps, sem = allocators(nc, ctx, "stick")
        q = sb("qs", [P, SH, S], F32R)
        kh = sb("khs", [P, SH, S], F32R)
        kl = sb("kls", [P, SH, S], F32R)
        v = sb("vs", [P, NT, SH, HD])
        take = sb("take", [P, 4, S])
        rest = sb("rest", [P, 4, S])
        wT = sb("wTs", [P, 2, NT, P])
        z = [ps(f"z{m}", [P, S]) for m in range(2)]
        tp = ps("tps", [P, NT, P])
        out = [ps(f"outs{i}", [P, CH]) for i in range(2)]
        gsub = sb("gsub", [P, P])
        gsub8 = sb("gsub8", [P, P])
        var = sb("varb", [P, DH * NT])
        rs = sb("rsb", [P, DH, NT])
        gsub_loaded, gsub_ready, var_ready, rs_ready = sem("gsub_loaded"), sem("gsub_ready"), sem("varb_ready"), sem("rsb_ready")
        loaded = [sem(f"shead_loaded{h}") for h in range(SH)]
        v_loaded = [sem(f"vs_loaded{i}") for i in range(2)]
        z_full, took, rested, scanned, weighted = (sem("z_full"), sem("took"), sem("rested"),
                                                             sem("scanned"), sem("weighted"))
        tp_full, wT_near, wT_far, pv_full, copied = (sem("tps_full"), sem("wT_near"), sem("wT_far"), sem("pvs_full"),
                                                     sem("copieds"))
        scaled = sem("scaled")
        steps = attention_steps(SH)
        n_steps = len(steps)
        HALF = NT // 2
        def far_count(s):
            return sum(i >= HALF for _, i in steps[:s])

        with nc.Block() as block:
            @block.sync
            def _(sp):
                for h in range(SH):
                    for dst, src in ((q, c.stack_q), (kh, c.stack_kh), (kl, c.stack_kl)):
                        sp.dma_start(dst[:, h].bitcast(F32), src.ap()[8 + h]).then_inc(loaded[h], 16)
                    if h in (1, 2):
                        some = slice(0, 2) if h == 1 else slice(2, SH)
                        sp.dma_start(v[:, :, some], c.values.ap()[:, 1, some.start * HD:some.stop * HD].rearrange(
                            "(n p) (h d) -> p n h d", p=P, d=HD)).then_inc(v_loaded[h - 1], 16)
                sp.dma_start(gsub[:], row_broadcast(a.subln_g[0], P)).then_inc(gsub_loaded, 16)

            @block.gpsimd
            def _(pool):
                pool.wait_ge(gsub_loaded, 16)
                pool.tensor_scalar(gsub8[:], gsub[:], 1.0 - LAM_INIT, None, ALU.mult).then_inc(gsub_ready, 1)
                pool.tensor_scalar(var[:], c.ssq[:].rearrange("p h i -> p (h i)"), 1.0 / P, EPS, ALU.mult, ALU.add)\
                    .then_inc(var_ready, 1)
                pool.wait_ge(var_ready, 1)
                pool.tensor_tensor(rs[:].rearrange("p h i -> p (h i)"), var[:], c.half[:], ALU.pow).then_inc(rs_ready, 1)
                pool.wait_ge(gsub_ready, 1)
                pool.wait_ge(rs_ready, 1)
                for i in range(NT):
                    for h in range(DH):
                        o = c.mixed_raw[:, i, h * P:(h + 1) * P]
                        pool.tensor_scalar(o, o, rs[:, h, i:i + 1], None, ALU.mult).then_inc(scaled, 1)
                        pool.wait_ge(scaled, i * DH + h + 1)
                        pool.tensor_tensor(o, o, gsub8[:], ALU.mult)

            @block.scalar
            def _(act):
                def evacuate(s):
                    nb = min(HALF, steps[s][1] + 1)
                    act.wait_ge(tp_full, s + 1)
                    ge(act, pv_full, s - 1)
                    act.copy(wT[:, s % 2, 0:nb, :], tp[:, 0:nb, :]).then_inc(wT_near, 1)
                for s in range(n_steps + 2):
                    if s < n_steps:
                        w = (steps[s][1] + 1) * P
                        act.wait_ge(z_full, s + 1)
                        ge(act, tp_full, s - 3)
                        act.activation(rest[:, s % 4, 0:w], z[s % 2][:, 0:w], ACT.Sigmoid, scale=-1.0).then_inc(rested, 1)
                        act.activation(take[:, s % 4, 0:w], z[s % 2][:, 0:w], ACT.Sigmoid).then_inc(took, 1)
                    if 2 <= s:
                        evacuate(s - 2)

            @block.vector
            def _(dve):
                def evacuate(s):
                    nb = steps[s][1] + 1
                    if nb > HALF:
                        dve.wait_ge(tp_full, s + 1)
                        ge(dve, pv_full, s - 1)
                        dve.tensor_copy(wT[:, s % 2, HALF:nb, :], tp[:, HALF:nb, :]).then_inc(wT_far, 1)
                def copy_out(s):
                    h, i = steps[s]
                    dve.wait_ge(pv_full, s + 1)
                    dve.tensor_copy(c.mixed_raw[:, i, CH + h * HD:CH + (h + 1) * HD], out[s % 2][:, 0:HD]).then_inc(copied, 1)
                for s in range(n_steps + 4):
                    if 4 <= s:
                        copy_out(s - 4)
                    if s < n_steps:
                        w = (steps[s][1] + 1) * P
                        e = s % 4
                        dve.wait_ge(rested, s + 1)
                        back = rest[:, e, 0:w][:, ::-1]
                        dve.tensor_tensor_scan(back, back, back, 1.0, ALU.mult, ALU.bypass).then_inc(scanned, 1)
                        dve.wait_ge(scanned, s + 1)
                        dve.wait_ge(took, s + 1)
                        dve.tensor_tensor(take[:, e, 0:w - 1], take[:, e, 0:w - 1], rest[:, e, 1:w], ALU.mult)\
                            .then_inc(weighted, 1)
                    if 1 <= s < n_steps + 1:
                        evacuate(s - 1)

            @block.tensor
            def _(pe):
                def scores(s):
                    h, i = steps[s]
                    if s < 2 or steps[s][0] != steps[s - 2][0]:
                        pe.wait_ge(loaded[h], 48)
                    w = (i + 1) * P
                    ge(pe, took, s - 1)
                    for c0 in range(0, w, CH):
                        c1 = min(w, c0 + CH)
                        qt, o = q[:, h, i * P:(i + 1) * P], z[s % 2][:, c0:c1]
                        pe.matmul(o, qt, kl[:, h, c0:c1], start=True, stop=False)
                        last = pe.matmul(o, qt, kh[:, h, c0:c1], start=False, stop=c1 < w)
                    last = pe.matmul(z[s % 2][:, i * P:w], c.identb[:], c.maskb[:], start=False, stop=True)
                    last.then_inc(z_full, 1)
                def transposes(s):
                    pe.wait_ge(weighted, s + 1)
                    ge(pe, wT_near, s)
                    ge(pe, wT_far, far_count(s))
                    for j in range(steps[s][1] + 1):
                        last = pe.transpose(tp[:, j, :], take[:, s % 4, j * P:(j + 1) * P], c.ident[:])
                    last.then_inc(tp_full, 1)
                def weigh(s):
                    h, i = steps[s]
                    pe.wait_ge(wT_near, s + 1)
                    ge(pe, wT_far, far_count(s + 1))
                    ge(pe, copied, s - 1)
                    for j in range(i + 1):
                        last = pe.matmul(out[s % 2][:, 0:HD], wT[:, s % 2, j, :], v[:, j, h, :], start=j == 0, stop=j == i)
                    last.then_inc(pv_full, 1)
                for s in range(n_steps + 3):
                    if s == 3:
                        pe.wait_ge(v_loaded[0], 16)
                    if s == 2 * NT + 3:
                        pe.wait_ge(v_loaded[1], 16)
                    if s < n_steps:
                        scores(s)
                    if 2 <= s < n_steps + 2:
                        transposes(s - 2)
                    if 3 <= s:
                        weigh(s - 3)


def branch(nc, a, c):
    with ExitStack() as ctx:
        sb, ps, sem = allocators(nc, ctx, "branch")
        o_hi = sb("o_hi", [P, KD, S], F32R)
        o_lo = sb("o_lo", [P, KD, S], F32R)
        wraw = sb("wbraw", [P, 2, KD, P])
        whi = sb("wbhi", [P, 2, KD, P], F32R)
        wlo = sb("wblo", [P, 2, KD, P], F32R)
        gts = sb("gts", [P, 2, 2, CH])
        m1 = sb("m1", [P, CH])
        m2 = sb("m2", [P, CH])
        mix = sb("mix", [P, CH])
        tp = [ps(f"tpb{i}", [P, KD, P]) for i in range(2)]
        pa = [ps(f"pa{i}", [P, CH]) for i in range(2)]
        pb = [ps(f"pb{i}", [P, CH]) for i in range(2)]
        w_loaded = [sem(f"wb_loaded{i}") for i in range(2)]
        g_loaded = [sem(f"gate_loaded{i}") for i in range(2)]
        tp_full, o_hi_ready, o_lo_ready = sem("tpb_full"), sem("o_hi_ready"), sem("o_lo_ready")
        w_hi, w_lo, acc_full, gated, mixed, mix_hi, mix_lo = (sem("wb_hi"), sem("wb_lo"), sem("accb_full"), sem("gated"),
                                                              sem("mixed"), sem("mix_hi"), sem("mix_lo"))
        units = [(cc, th) for cc in range(KD) for th in range(2)]

        with nc.Block() as block:
            @block.sync
            def _(sp):
                def load(cc):
                    ge(sp, w_lo, cc - 1)
                    for b, w in enumerate((a.w_branch_diff, a.w_branch_sb)):
                        sp.dma_start(wraw[:, cc % 2, 4 * b:4 * b + 4, :],
                                     w[0, :, cc * P:(cc + 1) * P].rearrange("(k p) n -> p k n", p=P))\
                            .then_inc(w_loaded[cc % 2], 16)
                load(0)
                load(1)
                for n, (cc, th) in enumerate(units):
                    if th == 0 and 0 < cc < KD - 1:
                        load(cc + 1)
                    ge(sp, gated, 2 * (n - 1))
                    sp.dma_start(gts[:, n % 2], bass.AP(tensor=c.gates, offset=cc * P * S + th * CH,
                                                        ap=[[S, P], [D * S, 2], [1, CH]])).then_inc(g_loaded[n % 2], 16)

            @block.scalar
            def _(act):
                def split(cc):
                    act.wait_ge(w_loaded[cc % 2], 32 * (cc // 2 + 1))
                    ge(act, acc_full, 2 * (cc - 1))
                    act.copy(whi[:, cc % 2], wraw[:, cc % 2]).then_inc(w_hi, 1)
                for i in range(NT):
                    if i in (NT - 3, NT - 2):
                        split(i - NT + 3)
                    act.wait_ge(tp_full, i + 1)
                    act.copy(o_hi[:, :, i * P:(i + 1) * P], tp[i % 2][:]).then_inc(o_hi_ready, 1)
                for n, (cc, th) in enumerate(units):
                    if th == 0 and cc >= 1 and cc + 1 < KD:
                        split(cc + 1)
                    act.wait_ge(mixed, n + 1)
                    act.copy(c.m_hi[:, cc, th * CH:(th + 1) * CH], mix[:]).then_inc(mix_hi, 1)

            @block.vector
            def _(dve):
                def split(cc):
                    dve.wait_ge(w_hi, cc + 1)
                    dve.tensor_sub(wlo[:, cc % 2], wraw[:, cc % 2], whi[:, cc % 2].bitcast(F32)).then_inc(w_lo, 1)
                for i in range(NT):
                    if i in (NT - 3, NT - 2):
                        split(i - NT + 3)
                    dve.wait_ge(o_hi_ready, i + 1)
                    dve.tensor_sub(o_lo[:, :, i * P:(i + 1) * P], tp[i % 2][:],
                                   o_hi[:, :, i * P:(i + 1) * P].bitcast(F32)).then_inc(o_lo_ready, 1)
                for n, (cc, th) in enumerate(units):
                    if th == 0 and cc >= 1 and cc + 1 < KD:
                        split(cc + 1)
                    dve.wait_ge(acc_full, n + 1)
                    dve.wait_ge(g_loaded[n % 2], 16 * (n // 2 + 1))
                    ge(dve, mixed, n)
                    dve.tensor_tensor(m1[:], pa[n % 2][:], gts[:, n % 2, 0, :], ALU.mult).then_inc(gated, 1)
                    dve.tensor_tensor(m2[:], pb[n % 2][:], gts[:, n % 2, 1, :], ALU.mult).then_inc(gated, 1)
                    dve.wait_ge(gated, 2 * n + 2)
                    ge(dve, mix_lo, n)
                    dve.tensor_tensor(mix[:], m1[:], m2[:], ALU.add).then_inc(mixed, 1)
                    dve.wait_ge(mix_hi, n + 1)
                    dve.tensor_sub(c.m_lo[:, cc, th * CH:(th + 1) * CH], mix[:],
                                   c.m_hi[:, cc, th * CH:(th + 1) * CH].bitcast(F32)).then_inc(mix_lo, 1)

            @block.tensor
            def _(pe):
                for i in range(NT):
                    ge(pe, o_lo_ready, i - 1)
                    for k in range(KD):
                        last = pe.transpose(tp[i % 2][:, k, :], c.mixed_raw[:, i, k * P:(k + 1) * P], c.ident[:])
                    last.then_inc(tp_full, 1)
                for n, (cc, th) in enumerate(units):
                    pe.wait_ge(w_lo, cc + 1)
                    pe.wait_ge(o_lo_ready, NT)
                    ge(pe, gated, 2 * (n - 1))
                    for acc, k0 in ((pa, 0), (pb, 4)):
                        for k in range(k0, k0 + 4):
                            cols = slice(th * CH, (th + 1) * CH)
                            last = product(pe, acc[n % 2][:], (whi[:, cc % 2, k, :], wlo[:, cc % 2, k, :]),
                                           (o_hi[:, k, cols], o_lo[:, k, cols]), k == k0, k == k0 + 3)
                    last.then_inc(acc_full, 1)


def output(nc, a, c):
    with ExitStack() as ctx:
        sb, ps, sem = allocators(nc, ctx, "output")
        RAW = 4
        wraw = sb("woraw", [P, RAW, CH])
        whi = sb("wohi", [P, 2, KD, CH], F32R)
        wlo = sb("wolo", [P, 2, KD, CH], F32R)
        x2 = c.mixed_raw
        xt = sb("xto", [P, 2, CH])
        g2 = sb("g2", [P, D])
        h2 = sb("h2", [P, 2, D])
        h2T = sb("h2T", [P, 2, KD, P])
        wr = sb("wr", [P, KD, NG + NE])
        junk = sb("junko", [P, D])
        ss = sb("sso", [P, NT])
        var = sb("varo", [P, NT])
        rs = sb("rso", [P, NT])
        acc = [ps(f"acco{i}", [P, CH]) for i in range(2)]
        tp = ps("tpo", [P, KD, P])
        lg = [ps(f"lg{i}", [P, CH]) for i in range(2)]
        raw_loaded = [sem(f"wo_loaded{i}") for i in range(RAW)]
        x_loaded = [sem(f"xo_loaded{i}") for i in range(2)]
        g_loaded, wr_loaded, w_hi, w_lo, acc_full, x2_ready = (sem("g2_loaded"), sem("wr_loaded"), sem("wo_hi"), sem("wo_lo"),
                                                               sem("acco_full"), sem("x2_ready"))
        squared, var_ready, rs_ready, h2_ready = sem("o_squared"), sem("varo_ready"), sem("rso_ready"), sem("h2_ready")
        h2_stored, x2_stored = [sem(f"h2_stored{i}") for i in range(2)], sem("x2_stored")
        tp_full, h2T_ready, lg_full, lg_ready = sem("tpo_full"), sem("h2T_ready"), sem("lg_full"), sem("lg_ready")
        tri_ready = sem("tri_ready")

        with nc.Block() as block:
            @block.sync
            def _(sp):
                sp.dma_start(g2[:], row_broadcast(a.ln2_g[0], D)).then_inc(g_loaded, 16)
                for r in range(2 * KD):
                    n, k = divmod(r, KD)
                    ge(sp, w_lo, r - RAW + 1)
                    sp.dma_start(wraw[:, r % RAW, :], a.w_out[0, k * P:(k + 1) * P, n * CH:(n + 1) * CH])\
                        .then_inc(raw_loaded[r % RAW], 16)
                    if r == 7:
                        sp.dma_start(wr[:, :, 0:NG], a.w_group[0].rearrange("(k p) n -> p k n", p=P)).then_inc(wr_loaded, 16)
                        sp.dma_start(wr[:, :, NG:], a.w_router[0].rearrange("(k p) n -> p k n", p=P)).then_inc(wr_loaded, 16)

            def finish(pool, t):
                pool.wait_ge(squared, t + 1)
                pool.tensor_scalar(var[:, t:t + 1], ss[:, t:t + 1], 1.0 / D, EPS, ALU.mult, ALU.add).then_inc(var_ready, 1)
                pool.wait_ge(var_ready, t + 1)
                pool.tensor_tensor(rs[:, t:t + 1], var[:, t:t + 1], c.half[:, 0:1], ALU.pow).then_inc(rs_ready, 1)
                pool.dma_start(c.out[0, t * P:(t + 1) * P, :], x2[:, t, :]).then_inc(x2_stored, 16)
                pool.wait_ge(h2_ready, t + 1)
                pool.dma_start(c.h2.ap()[t * P:(t + 1) * P, :], h2[:, t % 2, :]).then_inc(h2_stored[t % 2], 16)

            @block.gpsimd
            def _(pool):
                for m in range(NG):
                    pool.memset(c.prig[:, m:m + 1], float(NG - m))
                for m in range(EPG):
                    pool.memset(c.prie[:, m:m + 1], float(EPG - m))
                pool.memset(c.oneb[:], 1.0).then_inc(tri_ready, 1)
                pool.memset(c.trib[:], 1.0).then_inc(tri_ready, 1)
                pool.wait_ge(tri_ready, 2)
                pool.affine_select(out=c.trib[:], in_=c.trib[:], compare_op=ALU.is_gt, fill=0.0, base=0, pattern=[[1, P]],
                                   channel_multiplier=-1).then_inc(tri_ready, 1)
                pool.iota(c.tg[:], pattern=[[P, NT]], base=0, channel_multiplier=1,
                          allow_small_or_imprecise_dtypes=True).then_inc(tri_ready, 1)
                pool.iota(c.slots[:], pattern=[[1, P]], base=0, channel_multiplier=0,
                          allow_small_or_imprecise_dtypes=True).then_inc(tri_ready, 1)
                pool.iota(c.table[:, :, :, 0], pattern=[[0, NT], [0, NE]], base=0, channel_multiplier=1,
                          allow_small_or_imprecise_dtypes=True).then_inc(tri_ready, 1)
                pool.iota(c.table[:, :, :, 1], pattern=[[1, NT], [0, NE]], base=0, channel_multiplier=0,
                          allow_small_or_imprecise_dtypes=True).then_inc(tri_ready, 1)
                for n in range(2):
                    for t in range(NT):
                        u = n * NT + t
                        ge(pool, x2_ready, u - 1)
                        pool.dma_start(xt[:, u % 2, :], a.x[0, t * P:(t + 1) * P, n * CH:(n + 1) * CH])\
                            .then_inc(x_loaded[u % 2], 16)
                        if n and t:
                            finish(pool, t - 1)
                finish(pool, NT - 1)
                pool.wait_ge(h2_stored[0], 8 * NT)
                pool.wait_ge(h2_stored[1], 8 * NT)
                pool.wait_ge(x2_stored, 16 * NT)

            @block.scalar
            def _(act):
                def split(r):
                    n, k = divmod(r, KD)
                    act.wait_ge(raw_loaded[r % RAW], 16 * (r // RAW + 1))
                    act.copy(whi[:, n, k, :], wraw[:, r % RAW, :]).then_inc(w_hi, 1)
                def evacuate(t):
                    act.wait_ge(tp_full, t + 1)
                    ge(act, lg_full, t - 1)
                    act.copy(h2T[:, t % 2], tp[:]).then_inc(h2T_ready, 1)
                for r in range(2 * KD):
                    split(r)
                for t in range(NT):
                    act.wait_ge(x2_ready, NT + t + 1)
                    if t:
                        act.wait_ge(squared, t)
                    act.activation(junk[:], x2[:, t, :], ACT.Square, accum_out=ss[:, t:t + 1]).then_inc(squared, 1)
                    if t:
                        evacuate(t - 1)
                evacuate(NT - 1)

            @block.vector
            def _(dve):
                def split(r):
                    n, k = divmod(r, KD)
                    dve.wait_ge(w_hi, r + 1)
                    dve.tensor_sub(wlo[:, n, k, :], wraw[:, r % RAW, :], whi[:, n, k, :].bitcast(F32)).then_inc(w_lo, 1)
                def add_x(u):
                    n, t = divmod(u, NT)
                    dve.wait_ge(acc_full, u + 1)
                    dve.wait_ge(x_loaded[u % 2], 16 * (u // 2 + 1))
                    dve.tensor_tensor(x2[:, t, n * CH:(n + 1) * CH], acc[u % 2][:], xt[:, u % 2, :], ALU.add)\
                        .then_inc(x2_ready, 1)
                def norm(t):
                    dve.wait_ge(rs_ready, t + 1)
                    ge(dve, h2_stored[t % 2], 16 * (t // 2))
                    ge(dve, tp_full, t - 1)
                    dve.scalar_tensor_tensor(out=h2[:, t % 2, :], in0=x2[:, t, :], scalar=rs[:, t:t + 1], in1=g2[:],
                                             op0=ALU.mult, op1=ALU.mult).then_inc(h2_ready, 1)
                def logits(t):
                    dve.wait_ge(lg_full, t + 1)
                    dve.tensor_copy(c.logits[:, t, :], lg[t % 2][:, 0:NG + NE]).then_inc(lg_ready, 1)
                dve.wait_ge(g_loaded, 16)
                for r in range(KD):
                    split(r)
                for u in range(NT):
                    split(KD + u)
                    add_x(u)
                for t in range(NT):
                    add_x(NT + t)
                    if t:
                        norm(t - 1)
                    if t >= 2:
                        logits(t - 2)
                norm(NT - 1)
                logits(NT - 2)
                logits(NT - 1)

            @block.tensor
            def _(pe):
                def transposes(t):
                    pe.wait_ge(h2_ready, t + 1)
                    ge(pe, h2T_ready, t)
                    for k in range(KD):
                        last = pe.transpose(tp[:, k, :], h2[:, t % 2, k * P:(k + 1) * P], c.ident[:])
                    last.then_inc(tp_full, 1)
                def router(t):
                    pe.wait_ge(h2T_ready, t + 1)
                    ge(pe, lg_ready, t - 1)
                    for k in range(KD):
                        last = pe.matmul(lg[t % 2][:, 0:NG + NE], h2T[:, t % 2, k, :], wr[:, k, :], start=k == 0, stop=k == KD - 1)
                    last.then_inc(lg_full, 1)
                for u in range(2 * NT):
                    n, t = divmod(u, NT)
                    ge(pe, x2_ready, u - 1)
                    rows = slice(t * P, (t + 1) * P)
                    for k in range(KD):
                        if t == 0:
                            pe.wait_ge(w_lo, KD * n + k + 1)
                        last = product(pe, acc[u % 2][:], (c.m_hi[:, k, rows], c.m_lo[:, k, rows]),
                                       (whi[:, n, k, :], wlo[:, n, k, :]), k == 0, k == KD - 1)
                    last.then_inc(acc_full, 1)
                    if u == NT:
                        pe.wait_ge(wr_loaded, 32)
                    if u > NT + 1:
                        transposes(u - NT - 2)
                    if u > NT + 2:
                        router(u - NT - 3)
                for t in (NT - 2, NT - 1):
                    transposes(t)
                    router(t - 1)
                router(NT - 1)


def experts(nc, a, c):
    with ExitStack() as ctx:
        sb, ps, sem = allocators(nc, ctx, "experts")
        UNITS, RAW, TURN = 6, 8, 4
        KU = KD // 2
        wraw = sb("wraw", [P, RAW, KU * FF])
        whi = sb("whi", [P, UNITS, KU * FF], F32R)
        wlo = sb("wlo", [P, UNITS, KU * FF], F32R)
        rows = sb("rows", [P, 2, D])
        rT_hi = sb("rT_hi", [P, KD, P], F32R)
        rT_lo = sb("rT_lo", [P, KD, P], F32R)
        y = sb("y", [P, 2, D])
        sg = sb("sg", [P, FF])
        act_ = sb("act", [P, FF])
        aT_hi = sb("aT_hi", [P, KF, P], F32R)
        aT_lo = sb("aT_lo", [P, KF, P], F32R)
        hot = sb("hot", [P, NT, P], BF16)
        lst = sb("lst", [P, TURN, 5])
        idf = sb("idf", [P, TURN])
        idx = sb("idx", [P, TURN], U32)
        gate = sb("gate", [P, TURN])
        scratch = sb("scratch", [P, 1])
        tpx = ps("tpx", [P, KD, P])
        pg = ps("pgate", [P, FF])
        pu = ps("pup", [P, FF])
        tpa = ps("tpa", [P, KF, P])
        py = ps("py", [P, D])
        pl = ps("plist", [P, CH])
        raw_loaded = [sem(f"raw_loaded{i}") for i in range(RAW)]
        w_hi, w_lo, units_done = sem("w_hi"), sem("w_lo"), sem("units_done")
        hot_ready, list_full, list_copied, id_step, idx_ready = (
            sem("hot_ready"), sem("list_full"), sem("list_copied"), sem("id_step"), sem("idx_ready"))
        gathered = [sem(f"gathered{i}") for i in range(2)]
        rows_full, rows_hi, rows_lo, silu_ready, a_ready = (sem("rows_full"), sem("rows_hi"), sem("rows_lo"),
                                                            sem("silu_ready"), sem("a_ready"))
        aT_full, aT_hi_ready, aT_lo_ready, y_ready, added, ready = (
            sem("aT_full"), sem("aT_hi_ready"), sem("aT_lo_ready"), sem("y_ready"), sem("added"), sem("ready"))
        moved_on, moved = sem("moved_on"), sem("moved")
        route_step, exps, ranked, first_lo = sem("route_step"), sem("exps"), sem("ranked"), sem("first_lo")
        POOL_UNITS = 2
        EXP_STEPS, MASK_STEP = (2, 20), 31
        MOVED0 = 3

        taken = [0]
        def work(*shape):
            size = math.prod(shape)
            flat = y[:].rearrange("p a n -> p (a n)")[:, taken[0]:taken[0] + size]
            taken[0] += size
            assert taken[0] <= 2 * D
            if len(shape) == 2:
                return flat.rearrange("p (a b) -> p a b", b=shape[1])
            if len(shape) == 3:
                return flat.rearrange("p (a b c) -> p a b c", b=shape[1], c=shape[2])
            return flat
        gmax, eqg, pmg, gx, gsum = work(NT), work(NT, NG), work(NT), work(NT, NG), work(NT)
        sel, el, m1, oh1, pm, el2 = work(NT, NG, EPG), work(NT, EPG), work(NT), work(NT, EPG), work(NT), work(NT, EPG)
        m2, oh2, dx, e2, den, w1, w2 = work(NT), work(NT, EPG), work(NT), work(NT), work(NT), work(NT), work(NT)
        mk, gt, gt2 = work(NT, EPG), work(NT, EPG), work(NT, EPG)
        M, G = work(NT, NG, EPG), work(NT, NG, EPG)
        pos, cmax = work(NT, NE), work(1)
        U = sel.rearrange("p t g e -> p t (g e)")
        rest = pos
        rank, total = pg, pu
        Mb = sb("Mb", [P, NT * NE], BF16)

        def rounds(eng, body):
            body(0)
            most = eng.value_load(c.most[0:1, 0:1], min_val=0, max_val=2 * S)
            with eng.Fori(1, NT) as r:
                with eng.If(most > r * P):
                    body(r)

        def turns(eng, r, step):
            T = NE // TURN
            with eng.Fori(0, T - 1) as t:
                for i in range(TURN):
                    step(r * NE + t * TURN + i, t * TURN + i, i, r * T + t, 2)
            for i in range(TURN):
                e = NE - TURN + i
                step(r * NE + e, e, i, r * T + T - 1, min(2, TURN - 1 - i))

        def unit_place(i, j):
            return (UNITS * i + j) % RAW

        with nc.Block() as block:
            @block.sync
            def _(sp):
                sp.sem_inc(moved, MOVED0)
                def load(e, i, j):
                    if j < 4:
                        src = (a.w_gate, a.w_up)[j // 2][0, e].rearrange("(h k p) n -> h p k n", h=2, p=P)[j % 2]
                        dst = wraw[:, unit_place(i, j), :].rearrange("p (k n) -> p k n", n=FF)
                    else:
                        src = a.w_down[0, e].rearrange("(h k p) n -> h p k n", h=2, p=P)[j % 2]
                        dst = wraw[:, unit_place(i, j), :].rearrange("p (k n) -> p k n", n=D)
                    sp.dma_start(dst, src).then_inc(raw_loaded[unit_place(i, j)], 16)
                def turn(r, t, first):
                    for i in range(TURN):
                        for j in range(UNITS):
                            if not first or UNITS * i + j >= RAW:
                                sp.wait_ge(w_lo, (r * NE + t * TURN + i) * UNITS + j - RAW + 1)
                            load(t * TURN + i, i, j)
                def body(r):
                    if type(r) is int:
                        turn(0, 0, True)
                    with sp.Fori(1 if type(r) is int else 0, NE // TURN) as t:
                        turn(r, t, False)
                rounds(sp, body)

            def hold(eng, sem_, value):
                if type(value) is not int:
                    value = eng.to_reg(value)
                eng.wait_ge(ready, 1)
                eng.wait_ge(sem_, value)

            @block.gpsimd
            def _(pool):
                pool.memset(scratch[:], 0.0).then_inc(ready, 1)
                def gather(n, i):
                    hold(pool, idx_ready, n + 1)
                    pool.indirect_dma_start(out=rows[:, i % 2, :], out_offset=None, in_=c.h2.ap(),
                                            in_offset=bass.IndirectOffsetOnAxis(ap=idx[:, i:i + 1], axis=0))\
                        .then_inc(gathered[i % 2], 16)
                def scatter(n, i):
                    hold(pool, y_ready, n + 1)
                    pool.indirect_dma_start(out=c.out[0], out_offset=bass.IndirectOffsetOnAxis(ap=idx[:, i:i + 1], axis=0),
                                            in_=y[:, i % 2, :], in_offset=None, compute_op=ALU.add).then_inc(added, 16)
                    hold(pool, added, (n + 1) * 16)
                    pool.sem_inc(moved, 1)
                def body(r):
                    for j in range(POOL_UNITS):
                        pool.wait_ge(w_hi, r * NE * UNITS + j + 1)
                        pool.tensor_tensor(wlo[:, j, :], wraw[:, unit_place(0, j), :], whi[:, j, :].bitcast(F32),
                                           ALU.subtract).then_inc(first_lo, 1)
                    gather(r * NE, 0)
                    gather(r * NE + 1, 1)
                    def step(n, e, i, q, left):
                        if left > 1:
                            hold(pool, rows_full, n + 1)
                            gather(n + 2, (i + 2) % TURN)
                        scatter(n, i)
                    turns(pool, r, step)
                rounds(pool, body)

            @block.scalar
            def _(act):
                def split(n, i, j, q, first=False):
                    act.wait_ge(raw_loaded[unit_place(i, j)], (q * (UNITS * TURN // RAW) + (UNITS * i + j) // RAW + 1) * 16)
                    if not first:
                        act.wait_ge(units_done, (n - 1) * UNITS + j + 1)
                    act.copy(whi[:, j, :], wraw[:, unit_place(i, j), :]).then_inc(w_hi, 1)
                def transposed(n):
                    act.wait_ge(rows_full, n + 1)
                    act.copy(rT_hi[:], tpx[:]).then_inc(rows_hi, 1)
                act.wait_ge(route_step, EXP_STEPS[0])
                act.activation(gx[:], gx[:], ACT.Exp).then_inc(exps, 1)
                act.wait_ge(route_step, EXP_STEPS[1])
                act.activation(e2[:], dx[:], ACT.Exp).then_inc(exps, 1)
                def body(r):
                    for j in range(UNITS):
                        split(r * NE, 0, j, r * (NE // TURN), type(r) is int)
                    transposed(r * NE)
                    def step(n, e, i, q, left):
                        ahead = (n + 1, (i + 1) % TURN)
                        q1 = q + 1 if i == TURN - 1 else q
                        if left:
                            split(*ahead, 0, q1)
                        act.wait_ge(units_done, n * UNITS + 2)
                        act.activation(sg[:], pg[:], ACT.Silu).then_inc(silu_ready, 1)
                        if left:
                            split(*ahead, 1, q1)
                        act.wait_ge(aT_full, n + 1)
                        act.copy(aT_hi[:], tpa[:]).then_inc(aT_hi_ready, 1)
                        if left:
                            transposed(n + 1)
                            for j in range(2, UNITS):
                                split(*ahead, j, q1)
                        act.wait_ge(units_done, (n + 1) * UNITS)
                        act.wait_ge(moved, n + 2)
                        act.copy(y[:, i % 2, :], py[:]).then_inc(y_ready, 1)
                    turns(act, r, step)
                rounds(act, body)

            @block.vector
            def _(dve):
                def routing():
                    count = [0]
                    def chain(ins):
                        ins.then_inc(route_step, 1)
                        count[0] += 1
                        dve.wait_ge(route_step, count[0])
                    def over(ap, *shape):
                        return ap.to_broadcast([P, *shape])
                    def first_of(onehot, values, top, pri, best):
                        k = onehot.shape[-1]
                        chain(dve.tensor_tensor(onehot[:], values, over(top[:].unsqueeze(2), NT, k), ALU.is_equal))
                        chain(dve.tensor_tensor(onehot[:], onehot[:], over(pri[:].unsqueeze(1), NT, k), ALU.mult))
                        chain(dve.reduce_max(best[:], onehot[:], axis=X))
                        chain(dve.tensor_tensor(onehot[:], onehot[:], over(best[:].unsqueeze(2), NT, k), ALU.is_equal))
                    gl = c.logits[:, :, 0:NG]
                    chain(dve.reduce_max(gmax[:], gl, axis=X))
                    chain(dve.tensor_tensor(gx[:], gl, over(gmax[:].unsqueeze(2), NT, NG), ALU.subtract))
                    assert count[0] == EXP_STEPS[0]
                    first_of(eqg, gl, gmax, c.prig, pmg)
                    ge4 = over(eqg[:].unsqueeze(3), NT, NG, EPG)
                    chain(dve.tensor_tensor(sel[:], c.logits[:, :, NG:].rearrange("p t (g e) -> p t g e", e=EPG), ge4, ALU.mult))
                    chain(dve.reduce_sum(el[:], sel[:].rearrange("p t g e -> p t e g"), axis=X))
                    chain(dve.reduce_max(m1[:], el[:], axis=X))
                    first_of(oh1, el[:], m1, c.prie, pm)
                    chain(dve.scalar_tensor_tensor(out=el2[:], in0=oh1[:], scalar=MASKED, in1=el[:], op0=ALU.mult, op1=ALU.add))
                    chain(dve.reduce_max(m2[:], el2[:], axis=X))
                    first_of(oh2, el2[:], m2, c.prie, pm)
                    chain(dve.tensor_tensor(dx[:], m2[:], m1[:], ALU.subtract))
                    assert count[0] == EXP_STEPS[1]
                    dve.wait_ge(exps, 2)
                    chain(dve.reduce_sum(gsum[:], gx[:], axis=X))
                    chain(dve.tensor_scalar(den[:], e2[:], 1.0, None, ALU.add))
                    chain(dve.tensor_tensor(den[:], den[:], gsum[:], ALU.mult))
                    chain(dve.reciprocal(w1[:], den[:]))
                    chain(dve.tensor_tensor(w2[:], w1[:], e2[:], ALU.mult))
                    chain(dve.tensor_tensor(mk[:], oh1[:], oh2[:], ALU.add))
                    chain(dve.tensor_tensor(gt[:], oh1[:], over(w1[:].unsqueeze(2), NT, EPG), ALU.mult))
                    chain(dve.tensor_tensor(gt2[:], oh2[:], over(w2[:].unsqueeze(2), NT, EPG), ALU.mult))
                    chain(dve.tensor_tensor(gt[:], gt[:], gt2[:], ALU.add))
                    chain(dve.tensor_tensor(M[:], over(mk[:].unsqueeze(2), NT, NG, EPG), ge4, ALU.mult))
                    chain(dve.tensor_copy(Mb[:], M[:].rearrange("p t g e -> p (t g e)")))
                    assert count[0] == MASK_STEP
                    chain(dve.tensor_tensor(G[:], over(gt[:].unsqueeze(2), NT, NG, EPG), ge4, ALU.mult))
                    Gf = G[:].rearrange("p t g e -> p t (g e)")
                    Mf = M[:].rearrange("p t g e -> p t (g e)")
                    chain(dve.tensor_copy(c.table[:, :, :, 2], Gf))
                    chain(dve.tensor_tensor(rest[:], Gf, c.table[:, :, :, 2], ALU.subtract))
                    chain(dve.tensor_copy(c.table[:, :, :, 3], rest[:]))
                    chain(dve.tensor_tensor(rest[:], rest[:], c.table[:, :, :, 3], ALU.subtract))
                    chain(dve.tensor_copy(c.table[:, :, :, 4], rest[:]))
                    dve.wait_ge(ranked, 2)
                    chain(dve.tensor_copy(pos[:], rank[:, 0:NT * NE].rearrange("p (t e) -> p t e", e=NE)))
                    chain(dve.tensor_tensor(U[:], over(c.tg[:].unsqueeze(2), NT, NE), pos[:], ALU.subtract))
                    chain(dve.tensor_tensor(U[:], U[:], over(total[:, 0:NE].unsqueeze(1), NT, NE), ALU.add))
                    chain(dve.tensor_tensor(pos[:], pos[:], U[:], ALU.subtract))
                    chain(dve.tensor_tensor(pos[:], pos[:], Mf, ALU.mult))
                    chain(dve.tensor_tensor(c.dest[:], pos[:], U[:], ALU.add))
                    chain(dve.reduce_max(cmax[:], total[:, 0:NE], axis=X))
                    chain(dve.tensor_copy(c.most[:], cmax[:]))
                def hots(e):
                    dve.tensor_tensor(hot[:], c.slots[:].unsqueeze(1).to_broadcast([P, NT, P]),
                                      c.dest[:, :, bass.ds(e, 1)].to_broadcast([P, NT, P]), ALU.is_equal)\
                        .then_inc(hot_ready, 1)
                def ids(n, i, first=False):
                    dve.wait_ge(list_full, n + 1)
                    if not first:
                        dve.wait_ge(moved, n)
                    dve.tensor_copy(lst[:, i, :], pl[:, 0:5]).then_inc(list_copied, 1)
                    dve.wait_ge(list_copied, n + 1)
                    dve.tensor_reduce(gate[:, i:i + 1], lst[:, i, 2:5], X, ALU.add)
                    dve.scalar_tensor_tensor(out=idf[:, i:i + 1], in0=lst[:, i, 1:2], scalar=float(P), in1=lst[:, i, 0:1],
                                             op0=ALU.mult, op1=ALU.add).then_inc(id_step, 1)
                    dve.wait_ge(id_step, n + 1)
                    dve.tensor_copy(idx[:, i:i + 1], idf[:, i:i + 1]).then_inc(idx_ready, 1)
                def split(n, i, j):
                    dve.wait_ge(w_hi, n * UNITS + j + 1)
                    dve.tensor_sub(wlo[:, j, :], wraw[:, unit_place(i, j), :], whi[:, j, :].bitcast(F32)).then_inc(w_lo, 1)
                def transposed(n):
                    dve.wait_ge(rows_hi, n + 1)
                    dve.tensor_sub(rT_lo[:], tpx[:], rT_hi[:].bitcast(F32)).then_inc(rows_lo, 1)
                def body(r):
                    if type(r) is not int:
                        dve.wait_ge(hot_ready, r * NE)
                        dve.tensor_scalar(c.dest[:], c.dest[:], -float(P), None, ALU.add).then_inc(moved_on, 1)
                        dve.wait_ge(moved_on, r)
                    hots(0)
                    ids(r * NE, 0, type(r) is int)
                    hots(1)
                    ids(r * NE + 1, 1)
                    for j in range(POOL_UNITS):
                        dve.wait_ge(first_lo, r * POOL_UNITS + j + 1)
                        dve.sem_inc(w_lo, 1)
                    for j in range(POOL_UNITS, UNITS):
                        split(r * NE, 0, j)
                    transposed(r * NE)
                    def step(n, e, i, q, left):
                        ahead = (n + 1, (i + 1) % TURN)
                        if left > 1:
                            hots(e + 2)
                        if left:
                            split(*ahead, 0)
                            split(*ahead, 1)
                        dve.wait_ge(silu_ready, n + 1)
                        dve.wait_ge(units_done, n * UNITS + 4)
                        dve.scalar_tensor_tensor(out=act_[:], in0=pu[:], scalar=gate[:, i:i + 1], in1=sg[:],
                                                 op0=ALU.mult, op1=ALU.mult).then_inc(a_ready, 1)
                        dve.wait_ge(aT_hi_ready, n + 1)
                        dve.tensor_sub(aT_lo[:], tpa[:], aT_hi[:].bitcast(F32)).then_inc(aT_lo_ready, 1)
                        if left:
                            transposed(n + 1)
                            split(*ahead, 2)
                            split(*ahead, 3)
                        if left > 1:
                            ids(n + 2, (i + 2) % TURN)
                        if left:
                            split(*ahead, 4)
                            split(*ahead, 5)
                    turns(dve, r, step)
                routing()
                rounds(dve, body)

            @block.tensor
            def _(pe):
                def listing(n, e, first=False):
                    pe.wait_ge(hot_ready, n + 1)
                    if not first:
                        pe.wait_ge(list_copied, n)
                    for t in range(NT):
                        last = pe.matmul(pl[:, 0:5], hot[:, t, :], c.table[:, t, bass.ds(e, 1), :].rearrange("p a f -> p (a f)"),
                                         start=t == 0, stop=t == NT - 1)
                    last.then_inc(list_full, 1)
                def transposed(n, s):
                    pe.wait_ge(gathered[s], (n - s) * 8 + 16)
                    for j in range(KD):
                        last = pe.transpose(tpx[:, j, :], rows[:, s, j * P:(j + 1) * P], c.ident[:])
                    last.then_inc(rows_full, 1)
                pe.wait_ge(route_step, MASK_STEP)
                pe.matmul(rank[:, 0:NT * NE], c.trib[:], Mb[:], start=True, stop=False)
                for d in range(1, NT):
                    last = pe.matmul(rank[:, d * NE:NT * NE], c.oneb[:], Mb[:, 0:(NT - d) * NE], start=False, stop=d == NT - 1)
                last.then_inc(ranked, 1)
                for t in range(NT):
                    last = pe.matmul(total[:, 0:NE], c.oneb[:], Mb[:, t * NE:(t + 1) * NE], start=t == 0, stop=t == NT - 1)
                last.then_inc(ranked, 1)
                def body(r):
                    first = type(r) is int
                    listing(r * NE, 0, first)
                    listing(r * NE + 1, 1)
                    if not first:
                        pe.wait_ge(rows_lo, r * NE)
                    transposed(r * NE, 0)
                    def step(n, e, i, q, left):
                        pe.wait_ge(rows_lo, n + 1)
                        for j in range(4):
                            pe.wait_ge(w_lo, n * UNITS + j + 1)
                            for k in range(KU):
                                kd, cols = j % 2 * KU + k, slice(k * FF, (k + 1) * FF)
                                last = product(pe, (pg, pu)[j // 2][:], (rT_hi[:, kd, :], rT_lo[:, kd, :]),
                                               (whi[:, j, cols], wlo[:, j, cols]), kd == 0, kd == KD - 1)
                            last.then_inc(units_done, 1)
                        if left > 1:
                            listing(n + 2, e + 2)
                        pe.wait_ge(a_ready, n + 1)
                        for k in range(KF):
                            last = pe.transpose(tpa[:, k, :], act_[:, k * P:(k + 1) * P], c.ident[:])
                        last.then_inc(aT_full, 1)
                        if left:
                            transposed(n + 1, (i + 1) % 2)
                        for j in range(4, UNITS):
                            pe.wait_ge(w_lo, n * UNITS + j + 1)
                            for lhs in (aT_hi, aT_lo):
                                if j == 4:
                                    pe.wait_ge((aT_hi_ready, aT_lo_ready)[lhs is aT_lo], n + 1)
                                for k in range(KF // 2):
                                    kf = (j - 4) * KF // 2 + k
                                    for h in range(2):
                                        cols, out = slice(k * D + h * CH, k * D + (h + 1) * CH), py[:, h * CH:(h + 1) * CH]
                                        if lhs is aT_hi:
                                            pe.matmul(out, lhs[:, kf, :], wlo[:, j, cols], start=kf == 0, stop=False)
                                        last = pe.matmul(out, lhs[:, kf, :], whi[:, j, cols], start=False,
                                                         stop=lhs is aT_lo and kf == KF - 1)
                            last.then_inc(units_done, 1)
                    turns(pe, r, step)
                rounds(pe, body)


class Arrays:
    def __init__(self, dram):
        self.x = dram["x"]
        self.rel_bias = dram["rel_bias"]
        self.ln1_g = dram["ln1_g"]
        self.w_in = dram["w_in"]
        self.qnorm_g = dram["qnorm_g"]
        self.knorm_g = dram["knorm_g"]
        self.lambda_q1 = dram["lambda_q1"]
        self.lambda_k1 = dram["lambda_k1"]
        self.lambda_q2 = dram["lambda_q2"]
        self.lambda_k2 = dram["lambda_k2"]
        self.subln_g = dram["subln_g"]
        self.w_branch_diff = dram["w_branch_diff"]
        self.w_branch_sb = dram["w_branch_sb"]
        self.w_out = dram["w_out"]
        self.ln2_g = dram["ln2_g"]
        self.w_group = dram["w_group"]
        self.w_router = dram["w_router"]
        self.w_gate = dram["w_gate"]
        self.w_up = dram["w_up"]
        self.w_down = dram["w_down"]
        self.onehot = dram["onehot"]


class Kept:
    pass


def build(nc, a, out):
    c = Kept()
    c.out = out
    c.stack_q = nc.dram_tensor("stack_q", (16, P, S), F32)
    c.stack_kh = nc.dram_tensor("stack_kh", (16, P, S), F32)
    c.stack_kl = nc.dram_tensor("stack_kl", (16, P, S), F32)
    c.values = nc.dram_tensor("values", (S, 2, CH), F32)
    c.gates = nc.dram_tensor("gates", (2 * D, S), F32)
    c.h2 = nc.dram_tensor("h2_rows", (S, D), F32)
    c.drow_dram = nc.dram_tensor("drow_dram", (DH, DROW), F32)
    with ExitStack() as ctx:
        sb, ps, sem = allocators(nc, ctx, "kept_ctx")
        c.pool_dma_sem = sem
        c.ident = sb("ident", [P, P])
        c.identr = sb("identr", [P, P], F32R)
        c.identb = sb("identb", [P, P], BF16)
        c.maskb = sb("maskb", [P, P], BF16)
        c.neg_lam = sb("neg_lam", [P, 1])
        c.half = sb("half", [P, DH * NT])
        with ExitStack() as early:
            c.h_hi = early.enter_context(nc.sbuf_tensor("h_hi", [P, KD, S], F32R))
            c.h_lo = early.enter_context(nc.sbuf_tensor("h_lo", [P, KD, S], F32R))
            c.wraw = early.enter_context(nc.sbuf_tensor("w_in_raw", [P, RAW_W, CH], F32))
            c.whi = early.enter_context(nc.sbuf_tensor("w_in_hi", [P, 3, KD, CH], F32R))
            c.wlo = early.enter_context(nc.sbuf_tensor("w_in_lo", [P, 3, KD, CH], F32R))
            c.done_sems = []
            embed(nc, a, c)
            project(nc, a, c)
        with ExitStack() as late:
            sb, ps, sem = allocators(nc, late, "kept_late")
            c.dest = sb("dest", [P, NT, NE])
            c.table = sb("table", [P, NT, NE, 5], BF16)
            c.most = sb("most", [P, 1], I32)
            c.slots = sb("slots", [P, P])
            c.logits = sb("logits", [P, NT, NG + NE])
            c.tg = sb("tg", [P, NT])
            c.prig = sb("prig", [P, NG])
            c.prie = sb("prie", [P, EPG])
            c.trib = sb("trib", [P, P], BF16)
            c.oneb = sb("oneb", [P, P], BF16)
            with ExitStack() as middle:
                sb, ps, sem = allocators(nc, middle, "kept_middle")
                c.mixed_raw = sb("mixed_raw", [P, NT, D])
                c.ssq = sb("ssq_heads", [P, DH, NT])
                diff(nc, a, c)
                stick(nc, a, c)
                c.m_hi = sb("m_hi", [P, KD, S], F32R)
                c.m_lo = sb("m_lo", [P, KD, S], F32R)
                branch(nc, a, c)
                output(nc, a, c)
            experts(nc, a, c)


_INPUTS = ("x", "rel_bias", "ln1_g", "w_in", "qnorm_g", "knorm_g", "lambda_q1", "lambda_k1", "lambda_q2", "lambda_k2",
           "subln_g", "w_branch_diff", "w_branch_sb", "w_out", "ln2_g", "w_group", "w_router", "w_gate", "w_up", "w_down")


def kernel(**inputs):
    import concourse.bacc as bacc
    from concourse.bass_utils import run_bass_kernel_spmd

    nc = bacc.Bacc("TRN2", target_bir_lowering=False, num_devices=1)
    arrays = {name: np.ascontiguousarray(inputs[name]) for name in _INPUTS}
    arrays["onehot"] = bucket_onehot()
    aps = Arrays({n: nc.dram_tensor(n, v.shape, F32, kind="ExternalInput").ap() for n, v in arrays.items()})
    out = nc.dram_tensor("out", (1, S, D), F32, kind="ExternalOutput").ap()
    build(nc, aps, out)
    return run_bass_kernel_spmd(nc, [arrays], core_ids=[0]).results[0]["out"]
```
